# Optimizing a Trainium2 kernel written in Bass

```python
import jax, jax.numpy as jnp
from jax import lax
import numpy as np

D_MODEL = 1024
BATCH = 1
SEQ = 256
DEPTH = 1
DEC_BATCH = 8
DEC_SEQ = 1
PAST_LEN = 2048
PAGE_SIZE = 128

D_RNN = D_MODEL
RNN_HEADS = 16
RNN_BLOCK = D_RNN // RNN_HEADS
CONV_W = 4
RG_C = 8.0
SSD_EXPAND = 2
D_INNER = SSD_EXPAND * D_MODEL
SSD_HEAD_DIM = 64
SSD_HEADS = D_INNER // SSD_HEAD_DIM
SSD_GROUPS = 4
HEADS_PER_GROUP = SSD_HEADS // SSD_GROUPS
D_STATE = 128
SSD_CONV_DIM = D_INNER + 2 * SSD_GROUPS * D_STATE
CHUNK = 128
N_EXPERTS = 32
TOP_K = 4
D_EXPERT = D_MODEL
SWIGLU_LIMIT = 7.0
SWIGLU_ALPHA = 1.702
EXPERT_BLOCK = 128
EPS = 1e-6

IN_SPLITS = (D_RNN,
             2 * D_RNN,
             2 * D_RNN + D_INNER,
             2 * D_RNN + D_INNER + SSD_CONV_DIM,
             2 * D_RNN + D_INNER + SSD_CONV_DIM + SSD_HEADS,
             2 * D_RNN + D_INNER + SSD_CONV_DIM + SSD_HEADS + D_MODEL)
N_IN = IN_SPLITS[-1] + D_MODEL

kernel_name = 'hybrid_rglru_ssd_moe_step'

def rmsnorm(x, g):
    xf = x.astype(jnp.float32)
    y = xf * lax.rsqrt(jnp.mean(xf * xf, axis=-1, keepdims=True) + EPS)
    return (y * g.astype(jnp.float32)).astype(x.dtype)

def causal_conv(x, buf, w, b):
    xx = jnp.concatenate([buf.astype(x.dtype), x], axis=1)
    c = x.shape[-1]
    y = lax.conv_general_dilated(xx, w[:, None, :].astype(x.dtype), window_strides=(1,), padding='VALID',
                                 dimension_numbers=('NWC', 'WIO', 'NWC'), feature_group_count=c)
    return y + b.astype(x.dtype), xx[:, -(CONV_W - 1):].astype(buf.dtype)

def rg_lru(x, h0, w_rg, b_rg, w_ig, b_ig, lam):
    bsz, L, _ = x.shape
    xb = x.reshape(bsz, L, RNN_HEADS, RNN_BLOCK)
    r = jax.nn.sigmoid(jnp.einsum('blhi,hij->blhj', xb, w_rg) + b_rg).reshape(bsz, L, D_RNN)
    i = jax.nn.sigmoid(jnp.einsum('blhi,hij->blhj', xb, w_ig) + b_ig).reshape(bsz, L, D_RNN)
    log_a = (-RG_C * r.astype(jnp.float32)) * jax.nn.softplus(-lam.astype(jnp.float32))
    a = jnp.exp(log_a)
    mult = jnp.sqrt(-jnp.expm1(2.0 * log_a))
    bt = mult * (i * x).astype(jnp.float32)

    def combine(lhs, rhs):
        a1, b1 = lhs
        a2, b2 = rhs
        return a1 * a2, a2 * b1 + b2

    a_cum, b_cum = lax.associative_scan(combine, (a, bt), axis=1)
    h = a_cum * h0.astype(jnp.float32)[:, None] + b_cum
    return h.astype(x.dtype), h[:, -1].astype(h0.dtype)

def ssd_chunked(x, dt, A, Bm, Cm, s0):
    b, L = x.shape[:2]
    q = min(CHUNK, L)
    nc = -(-L // q)
    pad = nc * q - L
    padf = lambda t: jnp.pad(t, [(0, 0), (0, pad)] + [(0, 0)] * (t.ndim - 2))
    x, dt, Bm, Cm = padf(x), padf(dt), padf(Bm), padf(Cm)
    x = x.reshape(b, nc, q, SSD_GROUPS, HEADS_PER_GROUP, SSD_HEAD_DIM)
    dt = dt.reshape(b, nc, q, SSD_GROUPS, HEADS_PER_GROUP)
    Bm = Bm.reshape(b, nc, q, SSD_GROUPS, D_STATE)
    Cm = Cm.reshape(b, nc, q, SSD_GROUPS, D_STATE)
    a_cum = jnp.cumsum(dt * A.reshape(SSD_GROUPS, HEADS_PER_GROUP), axis=2)
    xdt = x * dt[..., None]
    ac = jnp.moveaxis(a_cum, 2, -1)
    diff = ac[..., :, None] - ac[..., None, :]
    causal = jnp.tril(jnp.ones((q, q), dtype=bool))
    decay = jnp.exp(jnp.where(causal, diff, -jnp.inf))
    cb = jnp.einsum('bcqgn,bckgn->bcgqk', Cm, Bm)
    y_diag = jnp.einsum('bcgqk,bcghqk,bckghp->bcqghp', cb, decay, xdt)
    a_last = a_cum[:, :, -1]
    decay_st = jnp.exp(a_last[:, :, None] - a_cum)
    states = jnp.einsum('bcqgn,bcqgh,bcqghp->bcghpn', Bm, decay_st, xdt)

    def step(carry, inp):
        st, dec = inp
        return carry * dec[..., None, None] + st, carry

    s_init = s0.reshape(b, SSD_GROUPS, HEADS_PER_GROUP, SSD_HEAD_DIM, D_STATE)
    s_fin, prev = lax.scan(step, s_init, (jnp.moveaxis(states, 1, 0), jnp.moveaxis(jnp.exp(a_last), 1, 0)))
    prev = jnp.moveaxis(prev, 0, 1)
    y_off = jnp.einsum('bcqgn,bcghpn,bcqgh->bcqghp', Cm, prev, jnp.exp(a_cum))
    y = (y_diag + y_off).reshape(b, nc * q, SSD_HEADS, SSD_HEAD_DIM)[:, :L]
    return y, s_fin.reshape(b, SSD_HEADS, SSD_HEAD_DIM, D_STATE)

def mixer(u, lru_conv0, lru_h0, ssd_conv0, ssd_s0, w_in, conv_lru_w, conv_lru_b, w_rg, b_rg, w_ig, b_ig,
          lam, w_proj_a, conv_ssd_w, conv_ssd_b, dt_bias, a_log, d_skip, ssd_norm, w_proj_b, w_out):
    b, L, _ = u.shape
    proj = u @ w_in
    lru_x, lru_gate, z, xbc, dt_raw, g_a, g_b = jnp.split(proj, IN_SPLITS, axis=-1)
    xc, lru_conv1 = causal_conv(lru_x, lru_conv0, conv_lru_w, conv_lru_b)
    h, lru_h1 = rg_lru(xc, lru_h0, w_rg, b_rg, w_ig, b_ig, lam)
    branch_a = (jax.nn.gelu(lru_gate) * h) @ w_proj_a
    xbc_c, ssd_conv1 = causal_conv(xbc, ssd_conv0, conv_ssd_w, conv_ssd_b)
    xbc_c = jax.nn.silu(xbc_c).astype(jnp.float32)
    xs, Bm, Cm = jnp.split(xbc_c, [D_INNER, D_INNER + SSD_GROUPS * D_STATE], axis=-1)
    dt = jax.nn.softplus(dt_raw.astype(jnp.float32) + dt_bias.astype(jnp.float32))
    A = -jnp.exp(a_log.astype(jnp.float32))
    xh = xs.reshape(b, L, SSD_HEADS, SSD_HEAD_DIM)
    y, ssd_s1 = ssd_chunked(xh, dt, A, Bm.reshape(b, L, SSD_GROUPS, D_STATE),
                            Cm.reshape(b, L, SSD_GROUPS, D_STATE), ssd_s0.astype(jnp.float32))
    y = y + d_skip.astype(jnp.float32)[:, None] * xh
    y = y.reshape(b, L, D_INNER) * jax.nn.silu(z.astype(jnp.float32))
    yg = y.reshape(b, L, SSD_GROUPS, D_INNER // SSD_GROUPS)
    yg = yg * lax.rsqrt(jnp.mean(yg * yg, axis=-1, keepdims=True) + EPS)
    y = (yg.reshape(b, L, D_INNER) * ssd_norm.astype(jnp.float32)).astype(u.dtype)
    branch_b = y @ w_proj_b
    merged = jax.nn.sigmoid(g_a) * branch_a + jax.nn.sigmoid(g_b) * branch_b
    return merged @ w_out, (lru_conv1, lru_h1, ssd_conv1, ssd_s1.astype(ssd_s0.dtype))

def moe(u, w_router, b_router, w_gate_up, b_gate_up, w_down, b_down):
    b, L, D = u.shape
    xt = u.reshape(-1, D)
    T = xt.shape[0]
    logits = (xt @ w_router + b_router).astype(jnp.float32)
    top_v, top_i = lax.top_k(logits, TOP_K)
    gates = jax.nn.softmax(top_v, axis=-1)
    n_assign = T * TOP_K
    flat_e = top_i.reshape(-1)
    flat_g = gates.reshape(-1)
    flat_tok = jnp.arange(n_assign, dtype=jnp.int32) // TOP_K
    order = jnp.argsort(flat_e)
    sorted_e = flat_e[order]
    counts = jnp.bincount(flat_e, length=N_EXPERTS)
    padded = (counts + EXPERT_BLOCK - 1) // EXPERT_BLOCK * EXPERT_BLOCK
    pend = jnp.cumsum(padded)
    pstart = pend - padded
    ustart = jnp.cumsum(counts) - counts
    dest = pstart[sorted_e] + jnp.arange(n_assign) - ustart[sorted_e]
    n_blocks = -(-n_assign // EXPERT_BLOCK) + N_EXPERTS
    n_rows = n_blocks * EXPERT_BLOCK
    row_tok = jnp.zeros((n_rows,), jnp.int32).at[dest].set(flat_tok[order])
    row_g = jnp.zeros((n_rows,), jnp.float32).at[dest].set(flat_g[order])
    block_e = jnp.minimum(jnp.searchsorted(pend, jnp.arange(n_blocks) * EXPERT_BLOCK, side='right'),
                          N_EXPERTS - 1)
    xr = xt[row_tok].reshape(n_blocks, EXPERT_BLOCK, D)

    def expert_block(args):
        xb, e = args
        gu = xb @ w_gate_up[e] + b_gate_up[e]
        gate, up = gu[:, :D_EXPERT], gu[:, D_EXPERT:]
        gate = jnp.minimum(gate, SWIGLU_LIMIT)
        up = jnp.clip(up, -SWIGLU_LIMIT, SWIGLU_LIMIT)
        act = (up + 1.0) * (gate * jax.nn.sigmoid(SWIGLU_ALPHA * gate))
        return act @ w_down[e] + b_down[e]

    yr = lax.map(expert_block, (xr, block_e)).reshape(n_rows, D)
    y = jnp.zeros((T, D), jnp.float32).at[row_tok].add(yr.astype(jnp.float32) * row_g[:, None])
    return y.astype(u.dtype).reshape(b, L, D)

def setup_inputs(seed: int = 0) -> dict:
    key = jax.random.key(seed)
    ks = iter(jax.random.split(key, 40))
    f32 = jnp.float32
    nrm = lambda shape, scale: jax.random.normal(next(ks), shape, f32) * scale
    s = jax.random.uniform(next(ks), (DEPTH, D_RNN), f32, 0.9, 0.999) ** (1.0 / RG_C)
    lam = jnp.log(s) - jnp.log1p(-s)
    dt0 = jnp.exp(jax.random.uniform(next(ks), (DEPTH, SSD_HEADS), f32, float(np.log(1e-3)), float(np.log(1e-1))))
    dt_bias = dt0 + jnp.log(-jnp.expm1(-dt0))
    a_log = jnp.log(jax.random.uniform(next(ks), (DEPTH, SSD_HEADS), f32, 1.0, 16.0))
    return {
        'x_prompt': nrm((BATCH, SEQ, D_MODEL), 1.0),
        'x_sample': nrm((DEC_BATCH, DEC_SEQ, D_MODEL), 1.0),
        'state_lru_conv': nrm((DEPTH, DEC_BATCH, CONV_W - 1, D_RNN), 1.0),
        'state_lru_h': nrm((DEPTH, DEC_BATCH, D_RNN), 0.5),
        'state_ssd_conv': nrm((DEPTH, DEC_BATCH, CONV_W - 1, SSD_CONV_DIM), 1.0),
        'state_ssd': nrm((DEPTH, DEC_BATCH, SSD_HEADS, SSD_HEAD_DIM, D_STATE), 0.1),
        'norm_mix': 1.0 + nrm((DEPTH, D_MODEL), 0.02),
        'w_in': nrm((DEPTH, D_MODEL, N_IN), D_MODEL ** -0.5),
        'conv_lru_w': nrm((DEPTH, CONV_W, D_RNN), CONV_W ** -0.5),
        'conv_lru_b': nrm((DEPTH, D_RNN), 0.01),
        'w_rg': nrm((DEPTH, RNN_HEADS, RNN_BLOCK, RNN_BLOCK), RNN_BLOCK ** -0.5),
        'b_rg': nrm((DEPTH, RNN_HEADS, RNN_BLOCK), 0.01),
        'w_ig': nrm((DEPTH, RNN_HEADS, RNN_BLOCK, RNN_BLOCK), RNN_BLOCK ** -0.5),
        'b_ig': nrm((DEPTH, RNN_HEADS, RNN_BLOCK), 0.01),
        'lam': lam,
        'w_proj_a': nrm((DEPTH, D_RNN, D_MODEL), D_RNN ** -0.5),
        'conv_ssd_w': nrm((DEPTH, CONV_W, SSD_CONV_DIM), CONV_W ** -0.5),
        'conv_ssd_b': nrm((DEPTH, SSD_CONV_DIM), 0.01),
        'dt_bias': dt_bias,
        'a_log': a_log,
        'd_skip': 1.0 + nrm((DEPTH, SSD_HEADS), 0.02),
        'ssd_norm': 1.0 + nrm((DEPTH, D_INNER), 0.02),
        'w_proj_b': nrm((DEPTH, D_INNER, D_MODEL), D_INNER ** -0.5),
        'w_out': nrm((DEPTH, D_MODEL, D_MODEL), D_MODEL ** -0.5),
        'norm_ffn': 1.0 + nrm((DEPTH, D_MODEL), 0.02),
        'w_router': nrm((DEPTH, D_MODEL, N_EXPERTS), D_MODEL ** -0.5),
        'b_router': nrm((DEPTH, N_EXPERTS), 0.01),
        'w_gate_up': nrm((DEPTH, N_EXPERTS, D_MODEL, 2 * D_EXPERT), D_MODEL ** -0.5),
        'b_gate_up': nrm((DEPTH, N_EXPERTS, 2 * D_EXPERT), 0.01),
        'w_down': nrm((DEPTH, N_EXPERTS, D_EXPERT, D_MODEL), D_EXPERT ** -0.5),
        'b_down': nrm((DEPTH, N_EXPERTS, D_MODEL), 0.01),
        'norm_final': 1.0 + nrm((D_MODEL,), 0.02),
    }

def reference(x_prompt, x_sample, state_lru_conv, state_lru_h, state_ssd_conv, state_ssd,
              norm_mix, w_in, conv_lru_w, conv_lru_b, w_rg, b_rg, w_ig, b_ig, lam, w_proj_a,
              conv_ssd_w, conv_ssd_b, dt_bias, a_log, d_skip, ssd_norm, w_proj_b, w_out,
              norm_ffn, w_router, b_router, w_gate_up, b_gate_up, w_down, b_down, norm_final):
    bp = x_prompt.shape[0]
    xp, xs = x_prompt, x_sample
    p_lc, p_lh, p_sc, p_ss = [], [], [], []
    s_lc, s_lh, s_sc, s_ss = [], [], [], []
    for l in range(DEPTH):
        mix_p = (w_in[l], conv_lru_w[l], conv_lru_b[l], w_rg[l], b_rg[l], w_ig[l], b_ig[l], lam[l],
                 w_proj_a[l], conv_ssd_w[l], conv_ssd_b[l], dt_bias[l], a_log[l], d_skip[l], ssd_norm[l],
                 w_proj_b[l], w_out[l])
        ffn_p = (w_router[l], b_router[l], w_gate_up[l], b_gate_up[l], w_down[l], b_down[l])
        zero_st = (jnp.zeros((bp, CONV_W - 1, D_RNN), state_lru_conv.dtype),
                   jnp.zeros((bp, D_RNN), state_lru_h.dtype),
                   jnp.zeros((bp, CONV_W - 1, SSD_CONV_DIM), state_ssd_conv.dtype),
                   jnp.zeros((bp, SSD_HEADS, SSD_HEAD_DIM, D_STATE), state_ssd.dtype))
        m, (lc, lh, sc, ss) = mixer(rmsnorm(xp, norm_mix[l]), *zero_st, *mix_p)
        xp = xp + m
        xp = xp + moe(rmsnorm(xp, norm_ffn[l]), *ffn_p)
        p_lc.append(lc); p_lh.append(lh); p_sc.append(sc); p_ss.append(ss)
        m, (lc, lh, sc, ss) = mixer(rmsnorm(xs, norm_mix[l]), state_lru_conv[l], state_lru_h[l],
                                    state_ssd_conv[l], state_ssd[l], *mix_p)
        xs = xs + m
        xs = xs + moe(rmsnorm(xs, norm_ffn[l]), *ffn_p)
        s_lc.append(lc); s_lh.append(lh); s_sc.append(sc); s_ss.append(ss)
    y_prompt = rmsnorm(xp, norm_final)
    y_sample = rmsnorm(xs, norm_final)
    return (y_prompt, y_sample,
            jnp.stack(p_lc), jnp.stack(p_lh), jnp.stack(p_sc), jnp.stack(p_ss),
            jnp.stack(s_lc), jnp.stack(s_lh), jnp.stack(s_sc), jnp.stack(s_ss))


_drawn_inputs = setup_inputs


def setup_inputs(seed=0):
    import zlib

    import numpy as np

    out = dict(_drawn_inputs(seed))
    spreads = {}
    factors = {'b_rg': 26.762, 'b_ig': 7.519, 'b_gate_up': 8.0, 'b_down': 8.0, 'norm_final': 8.352}
    for name, (base, spread) in spreads.items():
        noise = np.random.default_rng([zlib.crc32(name.encode()), seed]).standard_normal(out[name].shape)
        drawn = base * np.exp(spread * noise) if base else spread * noise
        out[name] = __import__('jax').numpy.asarray(drawn.astype(out[name].dtype))
    for name, factor in factors.items():
        out[name] = (out[name] * factor).astype(out[name].dtype)
    return out
```

```python
from contextlib import ExitStack

import concourse.bass as bass
from concourse import mybir
from concourse.alu_op_type import AluOpType as ALU

ACT = mybir.ActivationFunctionType
F32 = mybir.dt.float32
U32 = mybir.dt.uint32
I32 = mybir.dt.int32
AXX = mybir.AxisListType.X

P = 128
D = 1024
KT = D // P
TP = 256
TS = 8
NT = TP + TS
CHUNK = 128
CW = 4
HIST = CW - 1
CIN = HIST + TP + CW * TS
S_IN = HIST + TP
HEADS, HD, GROUPS, NS = 32, 64, 4, 128
HPG = HEADS // GROUPS
E, TOPK, SLOTS = 32, 4, 64
MAXP = -(-NT // SLOTS)
EPS = 1e-6
NEG = -1e30
XS, BT, CT, LX = 0, 16, 20, 24
NCONV = 32
GATE, Z, GA, GB, NPLAIN = 0, 8, 24, 32, 40
W_COL = [4096, 5120, 6144, 0, 1024, 2048, 3072, 7200, 8224]
DT_COL = 7168
SLOT = 2048
NSLOT = 12


def build(nc, a):
    with ExitStack() as ctx:
        def sb(name, shape, dt=F32):
            return ctx.enter_context(nc.sbuf_tensor(name, shape, dt))

        def sem(name):
            return ctx.enter_context(nc.semaphore(name))

        ring = sb("ring", [P, NSLOT * SLOT])
        plain_t = sb("plain", [P, NPLAIN * NT])
        conv_t = sb("conv", [P, NCONV * NT])
        xT = sb("xT", [P, KT, NT])
        xnT = sb("xnT", [P, KT, NT])
        ident = sb("ident", [P, P])
        ones = sb("ones", [P, P])
        before = sb("before", [P, P])
        cmask = sb("cmask", [P, P])
        slot_no = sb("slot_no", [P, MAXP * SLOTS])
        ex_t = sb("ex", [E, HEADS * HD])
        cvec = sb("cvec", [P, CW + 1, NCONV])
        vec = sb("vec", [P, 88])
        rstd = sb("rstd", [P, 4, NT])
        small = sb("small", [P, 704])
        hv = sb("hv", [HEADS, 64])
        go = sb("go", [P, 1])

        plain = plain_t[:, :].rearrange("p (t n) -> p t n", n=NT)
        conv = conv_t[:, :].rearrange("p (t n) -> p t n", n=NT)
        ex = ex_t[:, :].rearrange("p (h c) -> p h c", c=HD)
        stream = [ring[:, s * SLOT:(s + 1) * SLOT] for s in range(NSLOT)]

        A0 = 4 * SLOT

        def arena(start, size):
            return ring[:, A0 + start:A0 + start + size]

        cin = arena(0, NCONV * CIN).rearrange("p (t n) -> p t n", n=CIN)
        T0 = NCONV * CIN
        sq = arena(T0, KT * NT).rearrange("p (t n) -> p t n", n=NT)
        lru = [arena(T0 + i * KT * NT, KT * NT).rearrange("p (t n) -> p t n", n=NT) for i in range(3)]
        crow = arena(T0 + 3 * KT * NT, 736)
        x_rows = plain_t[:, 0:3 * D].rearrange("p (t d) -> p t d", d=D)
        hist_rows = plain_t[:, 3 * D:7 * D]
        rows_a = plain_t[:, 7 * D:7 * D + P]
        rows_b = plain_t[:, 7 * D + P:7 * D + 2 * P]
        h0_rows = plain_t[:, 7 * D + 2 * P:8 * D + 2 * P]
        gw = plain_t[:, GB * NT:GB * NT + 16 * P].rearrange("p (g t c) -> p g t c", g=2, t=KT)

        b_rg, b_ig, lam = vec[:, 0:8], vec[:, 8:16], vec[:, 16:24]
        ssd_norm, n_ffn, n_mix, dskip = vec[:, 24:40], vec[:, 40:48], vec[:, 48:56], vec[:, 56:72]
        sp4 = vec[:, 72:80]
        lt = [small[:, 8 * i:8 * i + 8] for i in range(5)]
        h0T = small[:, 64:128].rearrange("p (t b) -> p t b", b=TS)
        dsk = small[:, 128:130]
        dt_b, a_log, a_neg = hv[:, 0:1], hv[:, 1:2], hv[:, 2:3]

        xd = arena(0, 2 * 2048).rearrange("p (c h q) -> p c h q", c=2, h=HEADS)
        b_tok = arena(4096, 1024).rearrange("p (c g n) -> p c g n", c=2, g=GROUPS)
        s0T = arena(5120, 2048)
        fin_st = arena(7168, 1024).rearrange("p (r t n) -> p r t n", r=2, t=4)
        m_dec = [arena(o, 1024).rearrange("p (h q) -> p h q", h=HPG) for o in (8192, T0 + 5248)]
        yT = arena(T0, 16 * NT).rearrange("p (t n) -> p t n", n=NT)
        c_dec = [arena(o, 1024).rearrange("p (h q) -> p h q", h=HPG) for o in (T0 + 4224, 0)]
        xw = arena(T0 + 5248, 1536).rearrange("p (w h q) -> p w h q", w=3, h=HPG)
        cb = plain_t[:, GA * NT:GA * NT + 1024].rearrange("p (c g q) -> p c g q", c=2, g=GROUPS)
        hist_out = plain_t[:, Z * NT:Z * NT + 4096]
        h_out_t = plain_t[:, GB * NT:GB * NT + 1024]
        tok = small[:, 384:512].rearrange("p (w h) -> p w h", w=4)
        last = small[:, 512:576].rearrange("p (c h) -> p c h", c=2)
        wdec = small[:, 576:672].rearrange("p (w h) -> p w h", w=3)
        tmp_s = small[:, 192:384]
        dtw = [lru[i // 4][0:HEADS, i % 4 * 2, :] for i in range(8)]
        dtT, acT, daT = rstd[0:HEADS, 1, :], rstd[0:HEADS, 2, :], rstd[0:HEADS, 3, :]
        diag = hv[:, 0:64]
        st = [arena(i * 2048, 2048).rearrange("p (t n) -> p t n", n=NS) for i in range(2)]
        outer = arena(4096, 2048).rearrange("p (t n) -> p t n", n=NS)
        bc_rows = arena(6144, 1024)
        bc_all = arena(7168, 1024).rearrange("p (w g n) -> p w g n", w=2, g=GROUPS)
        dx = arena(8192, 256).rearrange("p (t w) -> p t w", w=2 * TS)
        xds = arena(8448, 128).rearrange("p (t b) -> p t b", b=TS)
        ys = arena(8576, 128).rearrange("p (t b) -> p t b", b=TS)
        products = arena(T0 + 4224, 2048).rearrange("p (t n) -> p t n", n=NS)
        e_bias = plain_t[0:E, 0:3 * D]
        xg, g1, u1, sg, ha, y_out = (plain_t[:, 3 * D + 512 * i:3 * D + 512 * i + 512] for i in range(6))
        xt, ht = (plain_t[:, 6 * D + 512 * i:6 * D + 512 * i + 512].rearrange("p (c s) -> p c s", c=4) for i in range(2))
        pick = plain_t[:, 7 * D:7 * D + 3 * SLOTS].rearrange("p (t s) -> p t s", t=3)
        pick_e = plain_t[0:E, 7 * D + 192:7 * D + 256]
        n_final = plain_t[:, 9 * D:10 * D]
        u_tok = conv_t[:, 0:3 * D].rearrange("p (t d) -> p t d", t=3)
        x1_tok = conv_t[:, 3 * D:6 * D].rearrange("p (t d) -> p t d", t=3)
        at = [6 * D]

        def scratch(*shape):
            size = 1
            for n in shape:
                size *= n
            v = conv_t[:, at[0]:at[0] + size]
            at[0] += size
            assert at[0] <= NCONV * NT
            if len(shape) == 1:
                return v
            names = "abc"[:len(shape)]
            return v.rearrange(f"p ({' '.join(names)}) -> p {' '.join(names)}", **dict(zip(names, shape)))

        logits, mark, rank = scratch(3, E), scratch(3, E), scratch(3, E)
        slot_of = scratch(3, E + 1)
        top, top_i, top_f, gates = scratch(3, 8), scratch(3, 8).bitcast(U32), scratch(3, 8), scratch(3, TOPK)
        hot = scratch(3, TOPK, E)
        picked, picked_i = scratch(3, TOPK), scratch(3, TOPK).bitcast(U32)
        pass_of, gates_p = scratch(3, TOPK), scratch(3, TOPK)
        b_router, total, tmp_e = scratch(E), scratch(E), scratch(3, E)
        most, passes_f, passes, ssq = scratch(1), scratch(1), scratch(1).bitcast(I32), scratch(3)
        w_router = scratch(KT * E).rearrange("p (k e) -> p k e", k=KT)
        ROWS = (P, P, TS)
        rows_y = [ring[:, 4 * D * t:4 * D * t + 4 * D].rearrange("p (k d) -> p k d", k=TOPK) for t in range(3)]
        slots_y = nc.dram_tensor("slots_y", [E * SLOTS, D], F32, kind="Internal").ap()

        ps = [ctx.enter_context(nc.psum_tensor(f"bank{i}", [P, 512], F32)) for i in range(8)]

        uses = [("vec", "v"), ("hist0", "v"), ("hist1", "v"), ("h0", "v")]
        uses += [(f"x{k}", "s") for k in range(KT)] + [("ss0", "s"), ("dt", "v"), ("tok", "v")]
        uses += [(f"ho{q}", "s") for q in range(8)]
        uses += [(f"xs{c}{g}", "v") for c in range(2) for g in range(GROUPS)]
        uses += [(f"bt{c}", "s") for c in range(2)] + [(f"cb{c}", "s") for c in range(2)]
        uses += [(f"{r}{t}", "s") for t in range(KT) for r in ("rg", "ig")] + [(f"hl{q}", "s") for q in range(2)]
        for g in range(GROUPS):
            uses += [(f"s0{g}", "s"), (f"fs{g}", "s")]
        for c in range(2):
            uses += [(f"ac{c}0{i}", "v") for i in range(2)]
            for g in range(GROUPS):
                if g + 1 < GROUPS:
                    uses += [(f"ac{c}{g + 1}{i}", "v") for i in range(2)]
                uses += [(f"y{c}{g}", "v")]
        uses += [("smp", "v"), ("bc0", "s"), ("bc1", "s")]
        for b in range(TS):
            uses += [(f"B{b}", "s"), (f"C{b}", "s")]
        uses += [(f"gn{g}", "s") for g in range(GROUPS)]
        uses += [("ss1", "s"), ("logits", "v"), ("rank", "v")]
        uses += [(f"{w}{t}{h}", "s") for w in ("u", "x1_") for t in range(3) for h in range(2)]
        index = {name: n for n, (name, _) in enumerate(uses)}
        assert len(index) == len(uses)
        nth = {name: sum(w == who for _, w in uses[:index[name]]) for name, who in uses}

        def bank(name):
            return ps[2 + index[name] % 6]

        filled, emptied = sem("psum_filled"), {"v": sem("psum_emptied_by_dve"), "s": sem("psum_emptied_by_act")}

        def open_bank(name):
            if index[name] >= 6:
                prev, who = uses[index[name] - 6]
                nc.tensor.wait_ge(emptied[who], nth[prev] + 1)
            return bank(name)

        def take_bank(eng, name):
            eng.wait_ge(filled, index[name] + 1)
            return bank(name)

        names = """acc2_emptied acc_emptied acc_ready all_stored bc_used bias_loaded cdec_exp cdec_ready consts_set conv_done
            conv_step da_exp dec_exp dec_in diag_ready dskip_loaded dskip_spread dt_exp dt_z ex_set final_loaded
            fs_stored0 fs_stored1 g1_ready ga_ready gated_ready gates_exp gates_in gates_loaded gates_zeroed gu_emptied
            h_ready ha_ready heads_loaded hist_loaded hist_stored hl_stored ht_filled ht_ready lam_abs lam_exp
            m_ready mark_ready merged_ready out_ready outer_ready passes_ready pick_e_ready picked_ready pick_ready combined rows_used rms_ready
            router_loaded sg_ready silu_done slots_stored smp_ready sqrt_done squares_ready st_done st_stored
            stream_used u2_ready u_read u_ready ug_ready vec_loaded w_used wdec_exp wdec_in x1_sq x2_sq x1rms_ready
            x2_ready x2rms_ready x_loaded xg_filled xg_ready xn_ready xt_filled xt_ready xw_ready y_emptied
            y_final y_stored yrms_ready ysq_ready yz_ready z_silu st_loaded0 st_loaded1""".split()
        S = {name: sem(name) for name in names}
        w_landed = [sem(f"w_landed{i}") for i in range(NSLOT)]
        rows_landed = [sem(f"rows_landed{t}") for t in range(3)]
        p_gu, p_xg, p_xt, p_ht, p_y = ps[0:2], ps[2], ps[3], ps[4], ps[5]
        landed = [sem(f"stream_landed{i}") for i in range(4)]
        act_step, dve_step, pool_step = sem("act_step"), sem("dve_step"), sem("pool_step")

        def linker(eng, step):
            count = [0]

            def link(ins):
                count[0] += 1
                ins.then_inc(step, 1)
                eng.wait_ge(step, count[0])
            return link

        def mm(out, w, x, start, stop):
            return nc.tensor.matmul(out, w, x, start=start, stop=stop)

        block = ctx.enter_context(nc.Block())

        @block.sync
        def _(sp):
            sp.dma_start(x_rows[:, 0:2, :], a["x_prompt"][0].rearrange("(t p) d -> p t d", p=P)).then_inc(S["x_loaded"], 16)
            sp.dma_start(x_rows[0:TS, 2, :], a["x_sample"][:, 0, :]).then_inc(S["x_loaded"], 16)
            w_in = a["w_in"][0].rearrange("(k p) c -> p k c", p=P)
            free_at, tiles = [0] * 4, 0
            for col in W_COL:
                for s in range(4):
                    if free_at[s]:
                        sp.wait_ge(S["acc_ready"], free_at[s])
                    sp.dma_start(stream[s].rearrange("p (k c) -> p k c", k=KT),
                                 w_in[:, :, col + 256 * s:col + 256 * s + 256]).then_inc(landed[s], 16)
                    tiles += 2
                    free_at[s] = tiles
            for w, k in ((a["w_proj_a"], KT), (a["w_proj_b"], 2 * KT), (a["w_out"], KT)):
                width = SLOT // k
                wv = w[0].rearrange("(k p) c -> p k c", p=P)
                for c in range(D // width):
                    s = c % 4
                    sp.wait_ge(S["acc_ready"], free_at[s])
                    sp.dma_start(stream[s].rearrange("p (k c) -> p k c", k=k),
                                 wv[:, :, c * width:(c + 1) * width]).then_inc(landed[s], 16)
                    tiles += width // P
                    free_at[s] = tiles
            w_gu, w_dn = a["w_gate_up"][0], a["w_down"][0]

            def load_expert(e, free):
                for c in range(NSLOT):
                    free(c)
                    if c < KT:
                        src = w_gu[e, P * c:P * c + P, :]
                        dst = stream[c]
                    else:
                        src = w_dn[e, 2 * P * (c - KT):2 * P * (c - KT) + 2 * P, :].rearrange("(k p) n -> p k n", p=P)
                        dst = stream[c].rearrange("p (k n) -> p k n", k=2)
                    sp.dma_start(dst, src).then_inc(w_landed[c], 16)

            def after_mixer(c):
                if c < 4:
                    sp.wait_ge(S["acc_ready"], free_at[c])
                elif c == 4:
                    sp.wait_ge(S["yz_ready"], 1)
                    sp.wait_ge(S["st_stored"], 16 * TS)
                    sp.wait_ge(S["acc_ready"], 88)

            def after_item(i):
                def free(c):
                    sp.wait_ge(S["w_used"], NSLOT * (i - 1) + c + 1)
                return free

            def after_pass(p, e):
                free_of_item = after_item(E * p + e)

                def free(c):
                    if c == 0:
                        sp.wait_ge(S["rows_used"], p)
                    free_of_item(c)
                return free

            load_expert(0, after_mixer)
            with sp.Fori(1, E) as e:
                load_expert(e, after_item(e))
            sp.wait_ge(S["passes_ready"], 1)
            n_passes = sp.value_load(passes[0:1, 0:1], min_val=1, max_val=MAXP)
            with sp.If(n_passes > 1):
                with sp.Fori(1, n_passes) as p:
                    with sp.Fori(0, E) as e:
                        load_expert(e, after_pass(p, e))
            sp.wait_ge(S["out_ready"], 3)
            sp.dma_start(a["out_0"][0].rearrange("(t p) d -> p t d", p=P), x1_tok[:, 0:2, :]).then_inc(S["y_stored"], 16)
            sp.dma_start(a["out_1"][:, 0, :], x1_tok[0:TS, 2, :]).then_inc(S["y_stored"], 16)
            sp.wait_ge(S["y_stored"], 32)
            sp.wait_ge(S["fs_stored0"], 32)
            sp.wait_ge(S["fs_stored1"], 32)

        @block.gpsimd
        def _(pool):
            link = linker(pool, pool_step)
            nc.gpsimd.memset(gw, 0.0).then_inc(S["gates_zeroed"], 1)
            nc.gpsimd.memset(ones[:, :], 1.0)
            nc.gpsimd.memset(cmask[:, :], 0.0)
            nc.gpsimd.memset(before[:, :], 1.0)
            link(nc.gpsimd.memset(ident[:, :], 0.0))
            nc.gpsimd.affine_select(out=ident[:, :], in_=ident[:, :], compare_op=ALU.not_equal, fill=1.0,
                                    base=0, pattern=[[-1, P]], channel_multiplier=1)
            nc.gpsimd.affine_select(out=cmask[:, :], in_=cmask[:, :], compare_op=ALU.is_ge, fill=NEG,
                                    base=0, pattern=[[1, P]], channel_multiplier=-1)
            nc.gpsimd.affine_select(out=before[:, :], in_=before[:, :], compare_op=ALU.is_gt, fill=0.0,
                                    base=0, pattern=[[1, P]], channel_multiplier=-1)
            nc.gpsimd.iota(slot_no[:, :], pattern=[[1, MAXP * SLOTS]], base=0, channel_multiplier=0,
                           allow_small_or_imprecise_dtypes=True).then_inc(S["consts_set"], 1)
            def states(name, i):
                return a[name][0, i].rearrange("(t h) q n -> (h q) t n", h=2)

            pool.wait_ge(filled, index["y13"] + 1)
            for i in range(2):
                nc.gpsimd.dma_start(st[i], states("state_ssd", i)).then_inc(S[f"st_loaded{i}"], 16)
            pool.wait_ge(S["smp_ready"], 1)
            for i in range(TS):
                pool.wait_ge(emptied["s"], nth[f"C{i}"] + 1)
                nc.gpsimd.tensor_tensor(
                    outer.rearrange("p (g t) n -> p g t n", g=GROUPS),
                    bc_all[:, 0].unsqueeze(2).to_broadcast([P, GROUPS, 4, NS]),
                    xds[:, :, i].rearrange("p (g t) -> p g t", g=GROUPS).unsqueeze(3).to_broadcast([P, GROUPS, 4, NS]),
                    ALU.mult).then_inc(S["outer_ready"], 1)
                pool.wait_ge(S["st_done"], i + 1)
                nc.gpsimd.dma_start(states("out_9", i), st[i % 2]).then_inc(S["st_stored"], 16)
                if i + 2 < TS:
                    pool.wait_ge(S["st_stored"], 16 * (i + 1))
                    pool.wait_ge(S["bc_used"], i + 1)
                    nc.gpsimd.dma_start(st[i % 2], states("state_ssd", i + 2)).then_inc(S[f"st_loaded{i % 2}"], 16)
            pool.wait_ge(S["st_stored"], 16 * TS)
            pool.wait_ge(S["passes_ready"], 1)
            pool.wait_ge(S["picked_ready"], 3)
            link(nc.gpsimd.memset(go[:, :], 1.0))
            n_passes = pool.value_load(passes[0:1, 0:1], min_val=1, max_val=MAXP)
            with pool.Fori(0, n_passes) as p:
                pool.wait_ge(S["all_stored"], p + 1)
                nc.gpsimd.tensor_tensor(go[:, :], go[:, :], go[:, :], ALU.mult)
                for t, n in enumerate(ROWS):
                    for k in range(TOPK):
                        nc.gpsimd.indirect_dma_start(
                            out=rows_y[t][0:n, k, :], out_offset=None, in_=slots_y[:, :],
                            in_offset=bass.IndirectOffsetOnAxis(picked_i[0:n, t, k:k + 1], 0)).then_inc(rows_landed[t], 16)

        @block.scalar
        def _(act):
            link = linker(act, act_step)
            rows = [("conv_ssd_w", 0, 96, "o j (t c) -> (o j t) c"), ("conv_ssd_b", 96, 24, "o (t c) -> (o t) c")]
            for name, r, n, pat in rows:
                act.dma_start(rows_a[r:r + n, :], a[name].rearrange(pat, c=P)).then_inc(S["vec_loaded"], 16)
            rows = [("conv_lru_w", 0, 32, "o j (t c) -> (o j t) c"), ("conv_lru_b", 32, 8, "o (t c) -> (o t) c"),
                    ("lam", 56, 8, "o (t c) -> (o t) c"), ("ssd_norm", 64, 16, "o (t c) -> (o t) c"),
                    ("norm_ffn", 80, 8, "o (t c) -> (o t) c"), ("norm_mix", 88, 8, "o (t c) -> (o t) c")]
            for name, r, n, pat in rows:
                act.dma_start(rows_b[r:r + n, :], a[name].rearrange(pat, c=P)).then_inc(S["vec_loaded"], 16)
            for name, r in (("b_rg", 40), ("b_ig", 48)):
                act.dma_start(rows_b[r:r + 8, :].rearrange("t (h j) -> t h j", h=2),
                              a[name][0].rearrange("(t h) j -> t h j", h=2)).then_inc(S["vec_loaded"], 16)
            act.dma_start(dsk[96:112, :], a["d_skip"][0].rearrange("(t h) -> t h", h=2)).then_inc(S["dskip_loaded"], 16)
            act.dma_start(dt_b, a["dt_bias"][0].rearrange("(h o) -> h o", o=1)).then_inc(S["heads_loaded"], 16)
            act.dma_start(a_log, a["a_log"][0].rearrange("(h o) -> h o", o=1)).then_inc(S["heads_loaded"], 16)
            act.dma_start(hist_rows[0:24, 0:3072], a["state_ssd_conv"][0].rearrange("b j c -> (b j) c")).then_inc(S["hist_loaded"], 16)
            act.dma_start(hist_rows[0:24, 3072:4096], a["state_lru_conv"][0].rearrange("b j c -> (b j) c")).then_inc(S["hist_loaded"], 16)
            act.dma_start(h0_rows[0:TS, :], a["state_lru_h"][0]).then_inc(S["hist_loaded"], 16)
            act.wait_ge(S["gates_zeroed"], 1)
            for w, name in enumerate(("w_rg", "w_ig")):
                for h in range(2):
                    act.dma_start(gw[64 * h:64 * h + 64, w, :, 64 * h:64 * h + 64],
                                  a[name][0].rearrange("(t h) i j -> h i t j", h=2)[h]).then_inc(S["gates_loaded"], 16)
            act.dma_start(arena(T0 + 3 * KT * NT, KT * HEADS).rearrange("p (k c) -> p k c", k=KT),
                          a["w_in"][0].rearrange("(k p) c -> p k c", p=P)[:, :, DT_COL:DT_COL + HEADS]).then_inc(S["heads_loaded"], 16)
            for k in range(KT):
                b = take_bank(act, f"x{k}")
                nc.scalar.copy(xT[:, k, :], b[:, 0:NT]).then_inc(emptied["s"], 1)
            act.wait_ge(S["lam_abs"], 1)
            nc.scalar.activation(lt[1], lt[1], ACT.Exp, scale=-1.0).then_inc(S["lam_exp"], 1)
            act.wait_ge(S["heads_loaded"], 48)
            nc.scalar.activation(a_neg, a_log, ACT.Exp).then_inc(S["lam_exp"], 1)
            b = take_bank(act, "ss0")
            nc.scalar.activation(rstd[:, 0, :], b[:, 0:NT], ACT.Copy, bias=EPS, scale=1.0 / D).then_inc(emptied["s"], 1)
            act.wait_ge(emptied["s"], nth["ss0"] + 1)
            nc.scalar.activation(rstd[:, 0, :], rstd[:, 0, :], ACT.Sqrt).then_inc(S["rms_ready"], 1)

            def take_group(g):
                for j in range(8):
                    t = 8 * g + j
                    act.wait_ge(S["acc_ready"], t + 1)
                    if t < NCONV:
                        nc.scalar.copy(cin[:, t, HIST:HIST + TP], ps[t % 2][:, 0:TP])
                        nc.scalar.copy(cin[:, t, S_IN + HIST * TS:CIN], ps[t % 2][:, TP:NT]).then_inc(S["acc_emptied"], 1)
                    else:
                        nc.scalar.copy(plain[:, t - NCONV, :], ps[t % 2][:, 0:NT]).then_inc(S["acc_emptied"], 1)

            take_group(0)
            take_group(1)
            take_group(2)
            act.wait_ge(S["dt_z"], 1)
            nc.scalar.activation(dtw[1], dtw[1], ACT.Exp, scale=-1.0).then_inc(S["dt_exp"], 1)
            take_group(3)
            act.wait_ge(S["conv_done"], 1)
            for t in range(0, LX, 8):
                ins = nc.scalar.activation(conv[:, t:t + 8, :], conv[:, t:t + 8, :], ACT.Silu)
            ins.then_inc(S["silu_done"], 1)
            act.wait_ge(S["wdec_in"], 1)
            nc.scalar.activation(wdec, wdec, ACT.Exp).then_inc(S["wdec_exp"], 1)
            for q in range(8):
                b = take_bank(act, f"ho{q}")
                nc.scalar.copy(hist_out[0:35, 512 * q:512 * q + 512], b[0:35, :]).then_inc(emptied["s"], 1)
            act.wait_ge(emptied["s"], nth["ho7"] + 1)
            act.dma_start(a["out_4"][0, 0], hist_out[0:3, 0:3072]).then_inc(S["hist_stored"], 16)
            act.dma_start(a["out_8"][0, :, 2, :], hist_out[27:35, 0:3072]).then_inc(S["hist_stored"], 16)
            act.dma_start(a["out_2"][0, 0], hist_out[0:3, 3072:4096]).then_inc(S["hist_stored"], 16)
            act.dma_start(a["out_6"][0, :, 2, :], hist_out[27:35, 3072:4096]).then_inc(S["hist_stored"], 16)
            act.dma_start(a["out_8"][0, :, 0:2, :], a["state_ssd_conv"][0, :, 1:3, :]).then_inc(S["hist_stored"], 16)
            act.dma_start(a["out_6"][0, :, 0:2, :], a["state_lru_conv"][0, :, 1:3, :]).then_inc(S["hist_stored"], 16)
            act.wait_ge(S["conv_done"], 2)
            for c in range(2):
                b = take_bank(act, f"bt{c}")
                nc.scalar.copy(b_tok[:, c].rearrange("p g n -> p (g n)"), b[:, :]).then_inc(emptied["s"], 1)
            for c in range(2):
                b = take_bank(act, f"cb{c}")
                nc.scalar.copy(cb[:, c].rearrange("p g n -> p (g n)"), b[:, :]).then_inc(emptied["s"], 1)
            take_group(4)
            for t in range(KT):
                b = take_bank(act, f"rg{t}")
                nc.scalar.activation(lru[0][:, t, :], b[:, 0:NT], ACT.Sigmoid, bias=b_rg[:, t:t + 1]).then_inc(emptied["s"], 1)
                b = take_bank(act, f"ig{t}")
                nc.scalar.activation(lru[1][:, t, :], b[:, 0:NT], ACT.Sigmoid, bias=b_ig[:, t:t + 1]).then_inc(emptied["s"], 1)
            act.wait_ge(emptied["s"], nth["ig7"] + 1)
            for t in range(KT):
                ins = nc.scalar.activation(lru[0][:, t, :], lru[0][:, t, :], ACT.Tanh, scale=sp4[:, t:t + 1])
            ins.then_inc(S["u_ready"], 1)
            act.wait_ge(S["u_read"], 1)
            nc.scalar.activation(lru[0], lru[0], ACT.Sqrt).then_inc(S["sqrt_done"], 1)
            nc.scalar.activation(plain[:, GATE:GATE + 8, :], plain[:, GATE:GATE + 8, :], ACT.Gelu_apprx_tanh).then_inc(S["sqrt_done"], 1)
            for q in range(2):
                b = take_bank(act, f"hl{q}")
                nc.scalar.copy(h_out_t[0:9, 512 * q:512 * q + 512], b[0:9, :]).then_inc(emptied["s"], 1)
            act.wait_ge(emptied["s"], nth["hl1"] + 1)
            act.dma_start(a["out_3"][0], h_out_t[0:1, :]).then_inc(S["hl_stored"], 16)
            act.dma_start(a["out_7"][0], h_out_t[1:9, :]).then_inc(S["hl_stored"], 16)
            act.wait_ge(S["hist_stored"], 96)
            take_group(5)
            for g in range(GROUPS):
                b = take_bank(act, f"s0{g}")
                nc.scalar.copy(s0T[:, 512 * g:512 * g + 512], b[:, :]).then_inc(emptied["s"], 1)
                b = take_bank(act, f"fs{g}")
                if g >= 2:
                    act.wait_ge(S[f"fs_stored{g % 2}"], 16)
                nc.scalar.copy(fin_st[:, g % 2].rearrange("p t n -> p (t n)"), b[:, :]).then_inc(emptied["s"], 1)
                act.wait_ge(emptied["s"], nth[f"fs{g}"] + 1)
                act.dma_start(a["out_5"][0, 0].rearrange("(g t h) q n -> g (h q) t n", t=4, h=2)[g], fin_st[:, g % 2]).then_inc(S[f"fs_stored{g % 2}"], 16)

            def decays(c):
                for g in range(GROUPS):
                    i = GROUPS * c + g
                    if c == 1:
                        act.wait_ge(filled, index[f"y1{g - 2}" if g > 1 else "y03"] + 1)
                        for h in range(2):
                            b = take_bank(act, f"ac{c}{g}{h}")
                            ins = nc.scalar.activation(c_dec[g % 2][:, 4 * h:4 * h + 4, :].rearrange("p h q -> p (h q)"), b[:, :], ACT.Exp)
                        ins.then_inc(S["cdec_exp"], 1)
                    act.wait_ge(emptied["v"], nth[f"ac{c}{g}1"] + 1)
                    nc.scalar.activation(m_dec[i % 2], m_dec[i % 2], ACT.Exp).then_inc(S["dec_exp"], 1)

            decays(0)
            take_group(6)
            decays(1)
            nc.scalar.activation(plain[:, Z:Z + 16, :], plain[:, Z:Z + 16, :], ACT.Silu).then_inc(S["z_silu"], 1)
            act.wait_ge(S["hl_stored"], 32)
            act.wait_ge(S["m_ready"], 8)
            take_group(7)
            take_group(8)
            act.wait_ge(S["acc_emptied"], 72)
            nc.scalar.activation(plain[:, GA:GA + 16, :], plain[:, GA:GA + 16, :], ACT.Sigmoid).then_inc(S["ga_ready"], 1)
            act.wait_ge(S["smp_ready"], 1)
            nc.scalar.activation(dx[:, :, TS:2 * TS], dx[:, :, TS:2 * TS], ACT.Exp).then_inc(S["da_exp"], 1)
            for w in range(2):
                b = take_bank(act, f"bc{w}")
                nc.scalar.copy(bc_rows[0:TS, 512 * w:512 * w + 512], b[0:TS, :]).then_inc(emptied["s"], 1)
            for n in range(2):
                act.wait_ge(S[f"fs_stored{n}"], 32)
            for i in range(TS):
                if i:
                    act.wait_ge(S["outer_ready"], i)
                    act.wait_ge(S["bc_used"], i)
                for w, n in enumerate("BC"):
                    b = take_bank(act, f"{n}{i}")
                    ins = nc.scalar.copy(bc_all[:, w].rearrange("p g n -> p (g n)"), b[:, :])
                    ins.then_inc(emptied["s"], 1)
            act.wait_ge(S["yz_ready"], 1)
            nc.scalar.activation(plain[:, Z:Z + 16, :], yT, ACT.Square).then_inc(S["ysq_ready"], 1)
            for g in range(GROUPS):
                b = take_bank(act, f"gn{g}")
                nc.scalar.activation(rstd[:, g, :], b[:, 0:NT], ACT.Copy, bias=EPS, scale=4.0 / 2048).then_inc(emptied["s"], 1)
            act.wait_ge(emptied["s"], nth["gn3"] + 1)
            nc.scalar.activation(rstd[:, :, :], rstd[:, :, :], ACT.Sqrt).then_inc(S["yrms_ready"], 1)
            b = take_bank(act, "ss1")
            nc.scalar.activation(rstd[:, 0, :], b[:, 0:NT], ACT.Copy, bias=EPS, scale=1.0 / D).then_inc(emptied["s"], 1)
            act.wait_ge(emptied["s"], nth["ss1"] + 1)
            nc.scalar.activation(rstd[:, 0, :], rstd[:, 0, :], ACT.Sqrt).then_inc(S["x1rms_ready"], 1)
            act.dma_start(w_router, a["w_router"][0].rearrange("(k p) e -> p k e", p=P)).then_inc(S["router_loaded"], 16)
            act.dma_start(b_router, a["b_router"].to_broadcast([P, E])).then_inc(S["router_loaded"], 16)
            act.dma_start(n_final, a["norm_final"].rearrange("(o d) -> o d", o=1).to_broadcast([P, D])).then_inc(S["final_loaded"], 16)
            act.dma_start(e_bias[:, 0:2 * D], a["b_gate_up"][0]).then_inc(S["bias_loaded"], 16)
            act.dma_start(e_bias[:, 2 * D:3 * D], a["b_down"][0]).then_inc(S["bias_loaded"], 16)
            act.wait_ge(S["gates_in"], 3)
            for t, n in enumerate(ROWS):
                ins = nc.scalar.activation(gates[0:n, t, :], gates[0:n, t, :], ACT.Exp)
            ins.then_inc(S["gates_exp"], 1)
            for w, dst in (("u", u_tok), ("x1_", x1_tok)):
                for t, n in enumerate(ROWS):
                    for h in range(2):
                        b = take_bank(act, f"{w}{t}{h}")
                        nc.scalar.copy(dst[0:n, t, 512 * h:512 * h + 512], b[0:n, :]).then_inc(emptied["s"], 1)

            act.wait_ge(S["passes_ready"], 1)
            n_passes = act.value_load(passes[0:1, 0:1], min_val=1, max_val=MAXP)

            def take_tokens(j):
                act.wait_ge(S["xg_filled"], j + 1)
                nc.scalar.copy(xg, p_xg[:, :]).then_inc(S["xg_ready"], 1)
                act.wait_ge(S["xt_filled"], j + 1)
                nc.scalar.copy(xt.rearrange("p c s -> p (c s)"), p_xt[:, :]).then_inc(S["xt_ready"], 1)

            with act.Fori(0, n_passes) as p:
                take_tokens((E + 1) * p)
                for t in range(3):
                    act.wait_ge(rows_landed[t], 16 * TOPK * p)
                with act.Fori(0, E) as e:
                    i = E * p + e
                    act.wait_ge(S["g1_ready"], i + 1)
                    nc.scalar.activation(sg, g1, ACT.Sigmoid, scale=1.702).then_inc(S["sg_ready"], 1)
                    take_tokens((E + 1) * p + e + 1)
                    act.wait_ge(S["ht_filled"], i + 1)
                    nc.scalar.copy(ht.rearrange("p c s -> p (c s)"), p_ht[:, :]).then_inc(S["ht_ready"], 1)
                    act.wait_ge(S["w_used"], NSLOT * i + NSLOT)
                    act.wait_ge(S["slots_stored"], 32 * i)
                    nc.scalar.copy(y_out, p_y[:, :]).then_inc(S["y_emptied"], 1)
                    act.wait_ge(S["y_emptied"], i + 1)
                    for h in range(2):
                        act.dma_start(slots_y[bass.ds(SLOTS * e, SLOTS), 512 * h:512 * h + 512],
                                      y_out[SLOTS * h:SLOTS * h + SLOTS, :]).then_inc(S["slots_stored"], 16)
                act.wait_ge(S["slots_stored"], 32 * E * (p + 1))
                nc.scalar.copy(sg[:, 0:1], ssq[:, 0:1]).then_inc(S["all_stored"], 1)
                for t, n in enumerate(ROWS):
                    act.wait_ge(S["x2_ready"], 3 * p + t + 1)
                    nc.scalar.activation(rows_y[t][0:n, 0, :], x1_tok[0:n, t, :], ACT.Square,
                                         accum_out=ssq[0:n, t:t + 1]).then_inc(S["rows_used"] if t == 2 else S["x2_sq"], 1)
            act.wait_ge(S["rows_used"], n_passes)
            for t, n in enumerate(ROWS):
                link(nc.scalar.activation(ssq[0:n, t:t + 1], ssq[0:n, t:t + 1], ACT.Copy, bias=EPS, scale=1.0 / D))
                nc.scalar.activation(ssq[0:n, t:t + 1], ssq[0:n, t:t + 1], ACT.Sqrt).then_inc(S["x2rms_ready"], 1)

        @block.tensor
        def _(pe):
            pe.wait_ge(S["consts_set"], 1)

            def turn(out, src, k):
                return nc.tensor.transpose(out, src, ident[0:k, 0:k])

            pe.wait_ge(S["vec_loaded"], 160)
            pe.wait_ge(S["dskip_spread"], 1)
            b = open_bank("vec")
            turn(b[:, 0:120], rows_a[0:120, :], 120)
            turn(b[:, 128:240], rows_b[0:112, :], 112).then_inc(filled, 1)
            pe.wait_ge(S["hist_loaded"], 48)
            for q in range(2):
                b = open_bank(f"hist{q}")
                for j in range(16):
                    t = 16 * q + j
                    ins = turn(b[:, 24 * j:24 * j + 24], hist_rows[0:24, P * t:P * t + P], 24)
                ins.then_inc(filled, 1)
            b = open_bank("h0")
            for t in range(KT):
                ins = turn(b[:, TS * t:TS * t + TS], h0_rows[0:TS, P * t:P * t + P], TS)
            ins.then_inc(filled, 1)
            pe.wait_ge(S["x_loaded"], 32)
            for k in range(KT):
                b = open_bank(f"x{k}")
                for t in range(3):
                    n = P if t < 2 else TS
                    ins = turn(b[:, P * t:P * t + n], x_rows[0:n, t, P * k:P * k + P], n)
                ins.then_inc(filled, 1)

            def sum_squares(name, sq_of, n, ready, per):
                b = open_bank(name)
                for k in range(n):
                    if per:
                        pe.wait_ge(ready, k + 1)
                    ins = mm(b[:, 0:NT], ones[:, :], sq_of(k), k == 0, k == n - 1)
                ins.then_inc(filled, 1)

            sum_squares("ss0", lambda k: sq[:, k, :], KT, S["squares_ready"], True)
            pe.wait_ge(S["xn_ready"], 1)

            def in_groups(g0, n):
                def body(g):
                    for s in range(4):
                        pe.wait_ge(landed[s], 16 * g + 16)
                        for m in range(2):
                            if not (isinstance(g, int) and g == 0 and s == 0):
                                pe.wait_ge(S["acc_emptied"], 8 * g + 2 * s + m - 1)
                            for k in range(KT):
                                w = stream[s][:, 256 * k + P * m:256 * k + P * m + P]
                                ins = mm(ps[m][:, 0:NT], w, xnT[:, k, :], k == 0, k == KT - 1)
                            ins.then_inc(S["acc_ready"], 1)
                if n == 1:
                    body(g0)
                else:
                    with pe.Fori(g0, g0 + n) as g:
                        body(g)

            in_groups(0, 1)
            in_groups(1, 2)
            b = open_bank("dt")
            wdt = arena(T0 + 3 * KT * NT, KT * HEADS).rearrange("p (k c) -> p k c", k=KT)
            pe.wait_ge(S["heads_loaded"], 48)
            for k in range(KT):
                ins = mm(b[0:HEADS, 0:NT], wdt[:, k, :], xnT[:, k, :], k == 0, k == KT - 1)
            ins.then_inc(filled, 1)
            in_groups(3, 1)
            pe.wait_ge(S["diag_ready"], 1)
            b = open_bank("tok")
            for w, src in enumerate((dtT, dtT, acT, acT)):
                turn(b[:, HEADS * w:HEADS * w + HEADS], src[:, CHUNK * (w % 2):CHUNK * (w % 2) + CHUNK], HEADS)
            mm(b[:, 128:192], ones[0:HEADS, :], diag, True, True).then_inc(filled, 1)
            pe.wait_ge(S["acc_emptied"], 32)
            for q in range(8):
                b = open_bank(f"ho{q}")
                for j in range(4):
                    ins = turn(b[0:35, P * j:P * j + P], cin[:, 4 * q + j, TP:CIN], P)
                ins.then_inc(filled, 1)
            pe.wait_ge(S["silu_done"], 1)
            for c in range(2):
                for g in range(GROUPS):
                    b = open_bank(f"xs{c}{g}")
                    for j in range(4):
                        ins = turn(b[:, P * j:P * j + P], conv[:, XS + 4 * g + j, CHUNK * c:CHUNK * c + CHUNK], P)
                    ins.then_inc(filled, 1)
            for c in range(2):
                b = open_bank(f"bt{c}")
                for g in range(GROUPS):
                    ins = turn(b[:, P * g:P * g + P], conv[:, BT + g, CHUNK * c:CHUNK * c + CHUNK], P)
                ins.then_inc(filled, 1)
            for c in range(2):
                b = open_bank(f"cb{c}")
                for g in range(GROUPS):
                    w = slice(CHUNK * c, CHUNK * c + CHUNK)
                    ins = mm(b[:, P * g:P * g + P], conv[:, BT + g, w], conv[:, CT + g, w], True, True)
                ins.then_inc(filled, 1)
            in_groups(4, 1)
            pe.wait_ge(S["gates_loaded"], 64)
            pe.wait_ge(S["conv_done"], 2)
            for t in range(KT):
                for w, n in enumerate(("rg", "ig")):
                    b = open_bank(f"{n}{t}")
                    mm(b[:, 0:NT], gw[:, w, t, :], conv[:, LX + t, :], True, True).then_inc(filled, 1)
            pe.wait_ge(S["h_ready"], 1)
            for q in range(2):
                b = open_bank(f"hl{q}")
                for j in range(4):
                    ins = turn(b[0:9, P * j:P * j + P], conv[:, LX + 4 * q + j, TP - 1:NT], P)
                ins.then_inc(filled, 1)
            in_groups(5, 1)
            for g in range(GROUPS):
                pe.wait_ge(S["xw_ready"], g + 1)
                pe.wait_ge(emptied["s"], nth["bt1"] + 1)
                b = open_bank(f"s0{g}")
                mm(b[:, :], b_tok[:, 0, g, :], xw[:, 0].rearrange("p h q -> p (h q)"), True, True).then_inc(filled, 1)
                b = open_bank(f"fs{g}")
                for j in range(4):
                    for c in range(2):
                        ins = mm(b[:, P * j:P * j + P], xw[:, 1 + c, 2 * j:2 * j + 2, :].rearrange("p h q -> p (h q)"),
                                 b_tok[:, c, g, :], c == 0, c == 1)
                ins.then_inc(filled, 1)

            def ssd(c):
                def sums(g):
                    for half in range(2):
                        b = open_bank(f"ac{c}{g}{half}")
                        for j in range(4):
                            h = HPG * g + 4 * half + j
                            for m in range(2):
                                ins = mm(b[64 * m:64 * m + 64, P * j:P * j + P], ex[:, h, :],
                                         acT[:, CHUNK * c:CHUNK * c + CHUNK], True, True)
                        ins.then_inc(filled, 1)

                sums(0)
                for g in range(GROUPS):
                    if g + 1 < GROUPS:
                        sums(g + 1)
                    i = GROUPS * c + g
                    b = open_bank(f"y{c}{g}")
                    pe.wait_ge(S["m_ready"], i + 1)
                    if c == 1:
                        pe.wait_ge(S["cdec_ready"], g + 1)
                    for h in range(HPG):
                        out = b[64 * (h % 2):64 * (h % 2) + 64, P * (h // 2):P * (h // 2) + P]
                        ins = mm(out, xd[:, c, HPG * g + h, :], m_dec[i % 2][:, h, :], True, c == 0)
                        if c == 1:
                            ins = mm(out, s0T[:, HD * (HPG * g + h):HD * (HPG * g + h) + HD], c_dec[g % 2][:, h, :], False, True)
                    ins.then_inc(filled, 1)

            pe.wait_ge(S["ex_set"], 1)
            ssd(0)
            in_groups(6, 1)
            ssd(1)
            in_groups(7, 1)
            in_groups(8, 1)
            b = open_bank("smp")
            for t in range(16):
                w = ex[:, 2 * t:2 * t + 2, :].rearrange("p h c -> p (h c)")
                mm(b[:, 16 * t:16 * t + 8], w, dtT[:, TP:NT], True, True)
                ins = mm(b[:, 16 * t + 8:16 * t + 16], w, acT[:, TP:NT], True, True)
            ins.then_inc(filled, 1)
            for w in range(2):
                b = open_bank(f"bc{w}")
                for g in range(GROUPS):
                    ins = turn(b[0:TS, P * g:P * g + P], conv[:, BT + 4 * w + g, TP:NT], P)
                ins.then_inc(filled, 1)
            pe.wait_ge(emptied["s"], nth["bc1"] + 1)
            for i in range(TS):
                for w, n in enumerate("BC"):
                    b = open_bank(f"{n}{i}")
                    for m in range(2):
                        ins = mm(b[64 * m:64 * m + 64, :], ex[0:TS, i, :], bc_rows[0:TS, 512 * w:512 * w + 512], True, True)
                    ins.then_inc(filled, 1)

            def project(g0, k_tiles, x_of, tiles0):
                per = 16 // k_tiles
                for c in range(8 // per):
                    s, g = c % 4, g0 + c // 4
                    pe.wait_ge(landed[s], 16 * g + 16)
                    for m in range(per):
                        t = per * c + m
                        n = tiles0 + t
                        if n >= 2:
                            pe.wait_ge(S["acc2_emptied"], n - 1)
                        for k in range(k_tiles):
                            width = SLOT // k_tiles
                            w = stream[s][:, width * k + P * m:width * k + P * m + P]
                            ins = mm(ps[n % 2][:, 0:NT], w, x_of(k), k == 0, k == k_tiles - 1)
                        ins.then_inc(S["acc_ready"], 1)

            pe.wait_ge(S["gated_ready"], 1)
            pe.wait_ge(S["acc_emptied"], 72)
            project(9, KT, lambda k: plain[:, GATE + k, :], 0)
            pe.wait_ge(S["ysq_ready"], 1)
            for g in range(GROUPS):
                sum_squares(f"gn{g}", lambda k: plain[:, Z + 4 * g + k, :], 4, None, False)
            pe.wait_ge(S["y_final"], 1)
            project(10, 16, lambda k: yT[:, k, :], 8)
            pe.wait_ge(S["merged_ready"], 1)
            project(12, KT, lambda k: plain[:, GA + k, :], 16)
            sum_squares("ss1", lambda k: conv[:, k, :], KT, S["x1_sq"], True)
            pe.wait_ge(S["u2_ready"], 1)
            pe.wait_ge(S["router_loaded"], 32)
            b = open_bank("logits")
            for t, n in enumerate(ROWS):
                for k in range(KT):
                    ins = mm(b[0:n, E * t:E * t + E], xnT[:, k, P * t:P * t + n], w_router[:, k, :], k == 0, k == KT - 1)
            ins.then_inc(filled, 1)
            pe.wait_ge(S["mark_ready"], 3)
            b = open_bank("rank")
            mm(b[:, 0:E], before[:, :], mark[:, 0, :], True, True)
            mm(b[:, E:2 * E], ones[:, :], mark[:, 0, :], True, False)
            mm(b[:, E:2 * E], before[:, :], mark[:, 1, :], False, True)
            mm(b[0:TS, 2 * E:3 * E], ones[:, 0:TS], mark[:, 0, :], True, False)
            mm(b[0:TS, 2 * E:3 * E], ones[:, 0:TS], mark[:, 1, :], False, False)
            mm(b[0:TS, 2 * E:3 * E], before[0:TS, 0:TS], mark[0:TS, 2, :], False, True)
            mm(b[:, 3 * E:4 * E], ones[:, :], mark[:, 0, :], True, False)
            mm(b[:, 3 * E:4 * E], ones[:, :], mark[:, 1, :], False, False)
            mm(b[:, 3 * E:4 * E], ones[0:TS, :], mark[0:TS, 2, :], False, True).then_inc(filled, 1)
            for w, src in (("u", xnT), ("x1_", xT)):
                for t, n in enumerate(ROWS):
                    for h in range(2):
                        b = open_bank(f"{w}{t}{h}")
                        for j in range(4):
                            ins = turn(b[0:n, P * j:P * j + P], src[:, 4 * h + j, P * t:P * t + n], P)
                        ins.then_inc(filled, 1)
            pe.wait_ge(S["passes_ready"], 1)
            n_passes = pe.value_load(passes[0:1, 0:1], min_val=1, max_val=MAXP)
            pe.wait_ge(emptied["s"], sum(w == "s" for _, w in uses))
            pe.wait_ge(emptied["v"], sum(w == "v" for _, w in uses))
            pe.wait_ge(S["bias_loaded"], 32)

            def gather(j):
                pe.wait_ge(S["pick_ready"], j + 1)
                for t, n in enumerate(ROWS):
                    for h in range(2):
                        ins = mm(p_xg[SLOTS * h:SLOTS * h + SLOTS, :], pick[0:n, t, :],
                                 u_tok[0:n, t, 512 * h:512 * h + 512], t == 0, t == 2)
                ins.then_inc(S["xg_filled"], 1)
                pe.wait_ge(S["xg_ready"], j + 1)
                for c in range(4):
                    ins = turn(p_xt[:, P * c:P * c + P], xg[:, P * c:P * c + P], P)
                ins.then_inc(S["xt_filled"], 1)

            with pe.Fori(0, n_passes) as p:
                gather((E + 1) * p)
                with pe.Fori(0, E) as e:
                    i = E * p + e
                    pe.wait_ge(S["xt_ready"], (E + 1) * p + e + 1)
                    pe.wait_ge(S["pick_e_ready"], i + 1)
                    pe.wait_ge(S["gu_emptied"], i)
                    for n in range(4):
                        mm(p_gu[n // 2][SLOTS * (n % 2):SLOTS * (n % 2) + SLOTS, :], pick_e, e_bias[:, 512 * n:512 * n + 512], True, False)
                    for k in range(KT):
                        pe.wait_ge(w_landed[k], 16 * i + 16)
                        for n in range(4):
                            ins = mm(p_gu[n // 2][SLOTS * (n % 2):SLOTS * (n % 2) + SLOTS, :],
                                     xt[:, k % 4, SLOTS * (k // 4):SLOTS * (k // 4) + SLOTS],
                                     stream[k][:, 512 * n:512 * n + 512], False, k == KT - 1)
                        ins.then_inc(S["w_used"], 1)
                    gather((E + 1) * p + e + 1)
                    for h in range(2):
                        mm(p_y[SLOTS * h:SLOTS * h + SLOTS, :], pick_e, e_bias[:, 2 * D + 512 * h:2 * D + 512 * h + 512], True, False)
                    pe.wait_ge(S["ha_ready"], i + 1)
                    for c in range(4):
                        ins = turn(p_ht[:, P * c:P * c + P], ha[:, P * c:P * c + P], P)
                    ins.then_inc(S["ht_filled"], 1)
                    pe.wait_ge(S["ht_ready"], i + 1)
                    for k in range(KT):
                        if k % 2 == 0:
                            pe.wait_ge(w_landed[KT + k // 2], 16 * i + 16)
                        for h in range(2):
                            ins = mm(p_y[SLOTS * h:SLOTS * h + SLOTS, :],
                                     ht[:, k % 4, SLOTS * (k // 4):SLOTS * (k // 4) + SLOTS],
                                     stream[KT + k // 2][:, D * (k % 2) + 512 * h:D * (k % 2) + 512 * h + 512], False, k == KT - 1)
                        if k % 2:
                            ins.then_inc(S["w_used"], 1)

        @block.vector
        def _(dve):
            link = linker(dve, dve_step)
            V = nc.vector

            def done(name, ins):
                ins.then_inc(S[name], 1)

            V.memset(cin[:, :, 0:HIST], 0.0)
            dve.wait_ge(S["dskip_loaded"], 16)
            done("dskip_spread", V.tensor_copy(rows_b[96:112, :].rearrange("t (h j) -> t h j", h=2),
                                               dsk[96:112, :].unsqueeze(2).to_broadcast([16, 2, HD])))
            dve.wait_ge(S["consts_set"], 1)
            done("ex_set", V.tensor_copy(ex, ident[0:E, 0:E].unsqueeze(2).to_broadcast([E, E, HD])))
            b = take_bank(dve, "vec")
            V.tensor_copy(cvec[:, :, 0:24], b[:, 0:120].rearrange("p (j t) -> p j t", j=5))
            V.tensor_copy(cvec[:, :, 24:32], b[:, 128:168].rearrange("p (j t) -> p j t", j=5))
            V.tensor_copy(vec[:, 0:72], b[:, 168:240]).then_inc(emptied["v"], 1)
            dve.wait_ge(emptied["v"], 1)
            V.tensor_scalar(lt[4], lam, -1.0, 0.0, ALU.mult, ALU.max)
            link(V.tensor_scalar(lt[1], lam, -1.0, None, ALU.mult))
            done("lam_abs", V.tensor_tensor(lt[1], lt[1], lam, ALU.max))

            def log1p(e, s, s2, p):
                link(V.tensor_scalar(p, e, 2.0, None, ALU.add))
                link(V.reciprocal(p, p))
                link(V.tensor_tensor(s, e, p, ALU.mult))
                link(V.tensor_tensor(s2, s, s, ALU.mult))
                link(V.tensor_scalar(p, s2, 1.0 / 15, None, ALU.mult))
                for n in (13, 11, 9, 7, 5, 3):
                    link(V.scalar_tensor_tensor(out=p, in0=p, scalar=1.0 / n, in1=s2, op0=ALU.add, op1=ALU.mult))
                link(V.scalar_tensor_tensor(out=p, in0=p, scalar=1.0, in1=s, op0=ALU.add, op1=ALU.mult))

            for q in range(2):
                b = take_bank(dve, f"hist{q}")
                V.tensor_copy(cin[:, 16 * q:16 * q + 16, S_IN:S_IN + HIST * TS].rearrange("p t (j b) -> p t j b", j=HIST),
                              b[:, 0:384].rearrange("p (t b j) -> p t j b", b=TS, j=HIST)).then_inc(emptied["v"], 1)
            b = take_bank(dve, "h0")
            V.tensor_copy(h0T, b[:, 0:64].rearrange("p (t b) -> p t b", b=TS)).then_inc(emptied["v"], 1)
            for k in range(KT):
                dve.wait_ge(emptied["s"], k + 1)
                done("squares_ready", V.tensor_tensor(sq[:, k, :], xT[:, k, :], xT[:, k, :], ALU.mult))
            dve.wait_ge(S["rms_ready"], 1)
            link(V.reciprocal(rstd[:, 0, :], rstd[:, 0, :]))
            for k in range(KT):
                ins = V.scalar_tensor_tensor(out=xnT[:, k, :], in0=xT[:, k, :], scalar=n_mix[:, k:k + 1],
                                             in1=rstd[:, 0, :], op0=ALU.mult, op1=ALU.mult)
            done("xn_ready", ins)
            dve.wait_ge(S["lam_exp"], 2)
            log1p(lt[1], lt[2], lt[3], lt[0])
            link(V.scalar_tensor_tensor(out=lt[0], in0=lt[0], scalar=2.0, in1=lt[4], op0=ALU.mult, op1=ALU.add))
            V.tensor_scalar(sp4, lt[0], 4.0, None, ALU.mult)
            link(V.tensor_scalar(a_neg, a_neg, -1.0, None, ALU.mult))

            steps = [0]

            def convolve(t):
                dve.wait_ge(S["acc_emptied"], t + 1)
                o = conv[:, t, 0:TP]
                V.tensor_scalar(o, cin[:, t, 0:TP], cvec[:, 0, t:t + 1], cvec[:, 4, t:t + 1], ALU.mult, ALU.add).then_inc(S["conv_step"], 1)
                steps[0] += 1
                for j in range(1, CW):
                    dve.wait_ge(S["conv_step"], steps[0])
                    V.scalar_tensor_tensor(out=o, in0=cin[:, t, j:j + TP], scalar=cvec[:, j, t:t + 1], in1=o,
                                           op0=ALU.mult, op1=ALU.add).then_inc(S["conv_step"], 1)
                    steps[0] += 1

            def convolve_samples(t0, n):
                o = conv[:, t0:t0 + n, TP:NT]
                tmp = tmp_s[:, 0:n * TS].rearrange("p (t b) -> p t b", b=TS)

                def tap(j):
                    return cvec[:, j, t0:t0 + n].unsqueeze(2).to_broadcast([P, n, TS])
                link(V.tensor_tensor(o, cin[:, t0:t0 + n, S_IN:S_IN + TS], tap(0), ALU.mult))
                for j in range(1, CW):
                    link(V.tensor_tensor(tmp, cin[:, t0:t0 + n, S_IN + TS * j:S_IN + TS * j + TS], tap(j), ALU.mult))
                    link(V.tensor_tensor(o, o, tmp, ALU.add))
                return V.tensor_tensor(o, o, tap(CW), ALU.add)

            for t in range(LX):
                convolve(t)
            done("conv_done", convolve_samples(0, LX))
            z, e, s, s2, p, mz = dtw[0:6]
            b = take_bank(dve, "dt")
            V.tensor_scalar(z, b[0:HEADS, 0:NT], dt_b, None, ALU.add).then_inc(emptied["v"], 1)
            dve.wait_ge(emptied["v"], nth["dt"] + 1)
            link(V.tensor_scalar(mz, z, 0.0, None, ALU.max))
            link(V.tensor_scalar(e, z, -1.0, None, ALU.mult))
            done("dt_z", V.tensor_tensor(e, e, z, ALU.max))
            dve.wait_ge(S["dt_exp"], 1)
            log1p(e, s, s2, p)
            link(V.scalar_tensor_tensor(out=dtT, in0=p, scalar=2.0, in1=mz, op0=ALU.mult, op1=ALU.add))
            link(V.tensor_scalar(daT, dtT, a_neg, None, ALU.mult))
            for c in range(2):
                w = slice(CHUNK * c, CHUNK * c + CHUNK)
                link(V.tensor_tensor_scan(acT[:, w], ones[0:HEADS, 0:CHUNK], daT[:, w], 0.0, ALU.mult, ALU.add))
            link(V.tensor_copy(acT[:, TP:NT], daT[:, TP:NT]))
            for c in range(2):
                last_c = CHUNK * c + CHUNK - 1
                ins = V.tensor_scalar(diag[:, HEADS * c:HEADS * c + HEADS], ident[0:HEADS, 0:HEADS], acT[:, last_c:last_c + 1], None, ALU.mult)
            done("diag_ready", ins)
            b = take_bank(dve, "tok")
            V.tensor_copy(tok.rearrange("p w h -> p (w h)"), b[:, 0:128])
            V.tensor_copy(last.rearrange("p c h -> p (c h)"), b[:, 128:192]).then_inc(emptied["v"], 1)
            dve.wait_ge(emptied["v"], nth["tok"] + 1)
            V.tensor_tensor(wdec[:, 2, :], last[:, 1, :], tok[:, 3, :], ALU.subtract)
            link(V.tensor_tensor(wdec[:, 0, :], last[:, 0, :], tok[:, 2, :], ALU.subtract))
            done("wdec_in", V.tensor_tensor(wdec[:, 1, :], wdec[:, 0, :], last[:, 1, :], ALU.add))
            for t in range(LX, NCONV):
                convolve(t)
            done("conv_done", convolve_samples(LX, KT))
            dve.wait_ge(S["conv_done"], 2)
            dve.wait_ge(filled, index["ho7"] + 1)
            for c in range(2):
                for g in range(GROUPS):
                    b = take_bank(dve, f"xs{c}{g}")
                    hs = slice(HPG * g, HPG * g + HPG)
                    V.tensor_tensor(xd[:, c, hs, :], b[:, :].rearrange("p (h q) -> p h q", q=HD),
                                    tok[:, c, hs].unsqueeze(2).to_broadcast([P, HPG, HD]), ALU.mult).then_inc(emptied["v"], 1)
            dve.wait_ge(S["u_ready"], 1)
            lx = conv[:, LX:LX + KT, :]
            link(V.tensor_tensor(lx, lx, lru[1], ALU.mult))
            link(V.tensor_scalar(lru[1], lru[0], 1.0, None, ALU.add))
            done("u_read", V.reciprocal(lru[1], lru[1]))
            dve.wait_ge(S["u_read"], 1)
            link(V.tensor_scalar(lru[2], lru[1], 2.0, -1.0, ALU.mult, ALU.add))
            dve.wait_ge(S["sqrt_done"], 1)
            link(V.scalar_tensor_tensor(out=lru[0], in0=lru[0], scalar=2.0, in1=lru[1], op0=ALU.mult, op1=ALU.mult))
            link(V.tensor_tensor(lru[0], lru[0], lx, ALU.mult))
            link(V.tensor_tensor(tmp_s[:, 0:64].rearrange("p (t b) -> p t b", b=TS), h0T, lru[2][:, :, TP:NT], ALU.mult))
            V.tensor_tensor(lx[:, :, TP:NT], tmp_s[:, 0:64].rearrange("p (t b) -> p t b", b=TS), lru[0][:, :, TP:NT], ALU.add)
            for t in range(KT):
                ins = V.tensor_tensor_scan(conv[:, LX + t, 0:TP], lru[2][:, t, 0:TP], lru[0][:, t, 0:TP], 0.0, ALU.mult, ALU.add)
            done("h_ready", ins)
            dve.wait_ge(S["h_ready"], 1)
            dve.wait_ge(S["sqrt_done"], 2)
            gate = plain[:, GATE:GATE + KT, :]
            done("gated_ready", V.tensor_tensor(gate, gate, lx, ALU.mult))
            dve.wait_ge(S["wdec_exp"], 1)
            dve.wait_ge(emptied["v"], nth["xs13"] + 1)
            for g in range(GROUPS):
                hs = slice(HPG * g, HPG * g + HPG)
                if g:
                    dve.wait_ge(filled, index[f"fs{g - 1}"] + 1)
                for w, c in ((0, 0), (1, 0), (2, 1)):
                    ins = V.tensor_tensor(xw[:, w], xd[:, c, hs, :], wdec[:, w, hs].unsqueeze(2).to_broadcast([P, HPG, HD]), ALU.mult)
                done("xw_ready", ins)

            def ssd(c):
                def differences(g):
                    i = GROUPS * c + g
                    if c == 1:
                        dve.wait_ge(S["cdec_exp"], g + 1)
                    if i:
                        j = i - 2
                        dve.wait_ge(filled, index[f"y{j // GROUPS}{j % GROUPS}" if j >= 0 else "fs3"] + 1)
                    for h in range(HPG):
                        b = take_bank(dve, f"ac{c}{g}{h // 4}")
                        ins = V.scalar_tensor_tensor(out=m_dec[i % 2][:, h, :], in0=b[:, P * (h % 4):P * (h % 4) + P],
                                                     scalar=tok[:, 2 + c, HPG * g + h:HPG * g + h + 1], in1=cmask[:, :],
                                                     op0=ALU.subtract, op1=ALU.add)
                        if h % 4 == 3:
                            ins.then_inc(emptied["v"], 1)

                differences(0)
                for g in range(GROUPS):
                    i = GROUPS * c + g
                    if g + 1 < GROUPS:
                        differences(g + 1)
                    if c == 1:
                        cw = conv[:, CT + g, CHUNK:TP].unsqueeze(1).to_broadcast([P, HPG, CHUNK])
                        done("cdec_ready", V.tensor_tensor(c_dec[g % 2], c_dec[g % 2], cw, ALU.mult))
                    dve.wait_ge(S["dec_exp"], i + 1)
                    if i == 0:
                        dve.wait_ge(emptied["s"], nth["cb1"] + 1)
                    done("m_ready", V.tensor_tensor(m_dec[i % 2], m_dec[i % 2], cb[:, c, g, :].unsqueeze(1).to_broadcast([P, HPG, CHUNK]), ALU.mult))
                    b = take_bank(dve, f"y{c}{g}")
                    for j in range(4):
                        t = 4 * g + j
                        w = slice(CHUNK * c, CHUNK * c + CHUNK)
                        ins = V.scalar_tensor_tensor(out=yT[:, t, w], in0=conv[:, XS + t, w], scalar=dskip[:, t:t + 1],
                                                     in1=b[:, P * j:P * j + P], op0=ALU.mult, op1=ALU.add)
                    ins.then_inc(emptied["v"], 1)

            ssd(0)
            ssd(1)
            b = take_bank(dve, "smp")
            V.tensor_copy(dx.rearrange("p t w -> p (t w)"), b[:, 0:256]).then_inc(emptied["v"], 1)
            dve.wait_ge(emptied["v"], nth["smp"] + 1)
            xs_s = conv[:, XS:XS + 16, TP:NT]
            done("smp_ready", V.tensor_tensor(xds, xs_s, dx[:, :, 0:TS], ALU.mult))
            dve.wait_ge(S["da_exp"], 1)
            for i in range(TS):
                dve.wait_ge(S[f"st_loaded{i % 2}"], 16 * (i // 2) + 16)
                dve.wait_ge(S["outer_ready"], i + 1)
                s_i = st[i % 2]
                for t in range(16):
                    ins = V.scalar_tensor_tensor(out=s_i[:, t, :], in0=s_i[:, t, :], scalar=dx[:, t, TS + i:TS + i + 1],
                                                 in1=outer[:, t, :], op0=ALU.mult, op1=ALU.add)
                done("st_done", ins)
                dve.wait_ge(S["st_done"], i + 1)
                for t in range(16):
                    ins = V.tensor_tensor_reduce(products[:, t, :], s_i[:, t, :], bc_all[:, 1, t // 4, :], 1.0, 0.0, ALU.mult, ALU.add,
                                                 ys[:, t, i:i + 1])
                done("bc_used", ins)
            dve.wait_ge(S["bc_used"], TS)
            link(V.tensor_tensor(xds, xs_s, dskip.unsqueeze(2).to_broadcast([P, 16, TS]), ALU.mult))
            link(V.tensor_tensor(yT[:, :, TP:NT], xds, ys, ALU.add))
            dve.wait_ge(S["z_silu"], 1)
            done("yz_ready", V.tensor_tensor(yT, yT, plain[:, Z:Z + 16, :], ALU.mult))
            dve.wait_ge(S["ga_ready"], 1)
            for t in range(KT):
                dve.wait_ge(S["acc_ready"], 72 + t + 1)
                V.tensor_tensor(plain[:, GA + t, :], plain[:, GA + t, :], ps[t % 2][:, 0:NT], ALU.mult).then_inc(S["acc2_emptied"], 1)
            dve.wait_ge(S["yrms_ready"], 1)
            link(V.reciprocal(rstd[:, :, :], rstd[:, :, :]))
            for t in range(16):
                ins = V.scalar_tensor_tensor(out=yT[:, t, :], in0=yT[:, t, :], scalar=ssd_norm[:, t:t + 1],
                                             in1=rstd[:, t // 4, :], op0=ALU.mult, op1=ALU.mult)
            done("y_final", ins)
            for t in range(KT):
                dve.wait_ge(S["acc_ready"], 80 + t + 1)
                V.tensor_tensor(plain[:, GB + t, :], plain[:, GB + t, :], ps[t % 2][:, 0:NT], ALU.mult).then_inc(S["acc2_emptied"], 1)
            dve.wait_ge(S["acc2_emptied"], 16)
            done("merged_ready", V.tensor_tensor(plain[:, GA:GA + KT, :], plain[:, GA:GA + KT, :], plain[:, GB:GB + KT, :], ALU.add))
            for t in range(KT):
                dve.wait_ge(S["acc_ready"], 88 + t + 1)
                V.tensor_tensor(xT[:, t, :], xT[:, t, :], ps[t % 2][:, 0:NT], ALU.add).then_inc(S["acc2_emptied"], 1)
                dve.wait_ge(S["acc2_emptied"], 16 + t + 1)
                done("x1_sq", V.tensor_tensor(conv[:, t, :], xT[:, t, :], xT[:, t, :], ALU.mult))
            dve.wait_ge(S["x1rms_ready"], 1)
            link(V.reciprocal(rstd[:, 0, :], rstd[:, 0, :]))
            for k in range(KT):
                ins = V.scalar_tensor_tensor(out=xnT[:, k, :], in0=xT[:, k, :], scalar=n_ffn[:, k:k + 1],
                                             in1=rstd[:, 0, :], op0=ALU.mult, op1=ALU.mult)
            done("u2_ready", ins)
            b = take_bank(dve, "logits")
            dve.wait_ge(S["router_loaded"], 32)
            for t, n in enumerate(ROWS):
                ins = V.tensor_tensor(logits[0:n, t, :], b[0:n, E * t:E * t + E], b_router[0:n, :], ALU.add)
            ins.then_inc(emptied["v"], 1)
            dve.wait_ge(emptied["v"], nth["logits"] + 1)
            for t, n in enumerate(ROWS):
                link(V.max(top[0:n, t, :], logits[0:n, t, :]))
                done("gates_in", V.tensor_scalar(gates[0:n, t, :], top[0:n, t, 0:TOPK], top[0:n, t, 0:1], None, ALU.subtract))
                link(V.max_index(top_i[0:n, t, :], top[0:n, t, :], logits[0:n, t, :]))
                link(V.tensor_copy(top_f[0:n, t, :], top_i[0:n, t, :]))
                for k in range(TOPK):
                    ins = V.tensor_scalar(hot[0:n, t, k, :], slot_no[0:n, 0:E], top_f[0:n, t, k:k + 1], None, ALU.is_equal)
                link(ins)
                V.tensor_tensor(mark[0:n, t, :], hot[0:n, t, 0, :], hot[0:n, t, 1, :], ALU.add)
                link(V.tensor_tensor(tmp_e[0:n, t, :], hot[0:n, t, 2, :], hot[0:n, t, 3, :], ALU.add))
                done("mark_ready", V.tensor_tensor(mark[0:n, t, :], mark[0:n, t, :], tmp_e[0:n, t, :], ALU.add))
            dve.wait_ge(S["mark_ready"], 3)
            b = take_bank(dve, "rank")
            for t, n in enumerate(ROWS):
                V.tensor_copy(rank[0:n, t, :], b[0:n, E * t:E * t + E])
            V.tensor_copy(total, b[:, 3 * E:4 * E]).then_inc(emptied["v"], 1)
            dve.wait_ge(emptied["v"], nth["rank"] + 1)
            link(V.tensor_reduce(most, total, AXX, ALU.max))
            link(V.tensor_scalar(passes_f, most, float(SLOTS), 1.0, ALU.is_gt, ALU.add))
            for j in range(2, MAXP):
                link(V.scalar_tensor_tensor(out=passes_f, in0=most, scalar=float(SLOTS * j), in1=passes_f, op0=ALU.is_gt, op1=ALU.add))
            done("passes_ready", V.tensor_copy(passes, passes_f))
            link(V.memset(slot_of[:, :, E:E + 1], -1.0))
            for t, n in enumerate(ROWS):
                r, m = rank[0:n, t, :], mark[0:n, t, :]
                link(V.scalar_tensor_tensor(out=slot_of[0:n, t, 0:E], in0=r, scalar=1.0, in1=m, op0=ALU.add, op1=ALU.mult))
                link(V.tensor_scalar(slot_of[0:n, t, 0:E], slot_of[0:n, t, 0:E], -1.0, None, ALU.add))
                for k in range(TOPK):
                    ins = V.tensor_tensor_reduce(hot[0:n, t, k, :], hot[0:n, t, k, :], r, 1.0, 0.0, ALU.mult, ALU.add,
                                                 picked[0:n, t, k:k + 1])
                link(ins)
                q, s = pass_of[0:n, t, :], picked[0:n, t, :]
                link(V.tensor_scalar(q, s, float(SLOTS), None, ALU.is_ge))
                for j in range(2, MAXP):
                    link(V.scalar_tensor_tensor(out=q, in0=s, scalar=float(SLOTS * j), in1=q, op0=ALU.is_ge, op1=ALU.add))
                link(V.scalar_tensor_tensor(out=s, in0=q, scalar=-float(SLOTS), in1=s, op0=ALU.mult, op1=ALU.add))
                link(V.scalar_tensor_tensor(out=s, in0=top_f[0:n, t, 0:TOPK], scalar=float(SLOTS), in1=s, op0=ALU.mult, op1=ALU.add))
                done("picked_ready", V.tensor_copy(picked_i[0:n, t, :], s))
            dve.wait_ge(S["gates_exp"], 1)
            for t, n in enumerate(ROWS):
                link(V.tensor_reduce(ssq[0:n, t:t + 1], gates[0:n, t, :], AXX, ALU.add))
                link(V.reciprocal(ssq[0:n, t:t + 1], ssq[0:n, t:t + 1]))
                link(V.tensor_scalar(gates[0:n, t, :], gates[0:n, t, :], ssq[0:n, t:t + 1], None, ALU.mult))
            n_passes = dve.value_load(passes[0:1, 0:1], min_val=1, max_val=MAXP)
            dve.wait_ge(filled, len(uses))

            def pick_tokens(p, e):
                for t, n in enumerate(ROWS):
                    ins = V.tensor_scalar(pick[0:n, t, :], slot_no[0:n, bass.ds(SLOTS * p, SLOTS)],
                                          slot_of[0:n, t, bass.ds(e, 1)], None, ALU.is_equal)
                done("pick_ready", ins)

            def pick_expert(e):
                done("pick_e_ready", V.tensor_copy(pick_e, ident[0:E, bass.ds(e, 1)].to_broadcast([E, SLOTS])))

            with dve.Fori(0, n_passes) as p:
                pick_tokens(p, 0)
                pick_expert(0)
                with dve.Fori(0, E) as e:
                    i = E * p + e
                    dve.wait_ge(S["xg_filled"], (E + 1) * p + e + 1)
                    pick_tokens(p, e + 1)
                    dve.wait_ge(S["w_used"], NSLOT * i + KT)
                    V.tensor_scalar(g1, p_gu[0][:, :], 7.0, None, ALU.min).then_inc(S["g1_ready"], 1)
                    V.tensor_scalar(u1, p_gu[1][:, :], 7.0, -7.0, ALU.min, ALU.max).then_inc(S["gu_emptied"], 1)
                    dve.wait_ge(S["gu_emptied"], i + 1)
                    V.scalar_tensor_tensor(out=u1, in0=u1, scalar=1.0, in1=g1, op0=ALU.add, op1=ALU.mult).then_inc(S["ug_ready"], 1)
                    dve.wait_ge(S["ug_ready"], i + 1)
                    dve.wait_ge(S["sg_ready"], i + 1)
                    V.tensor_tensor(ha, u1, sg, ALU.mult).then_inc(S["ha_ready"], 1)
                    dve.wait_ge(S["ht_filled"], i + 1)
                    pick_expert(e + 1)
                for t, n in enumerate(ROWS):
                    ins = V.scalar_tensor_tensor(out=gates_p[0:n, t, :], in0=pass_of[0:n, t, :], scalar=slot_no[0:n, bass.ds(p, 1)],
                                                 in1=gates[0:n, t, :], op0=ALU.is_equal, op1=ALU.mult)
                done("combined", ins)
                for t, n in enumerate(ROWS):
                    dve.wait_ge(rows_landed[t], 16 * TOPK * (p + 1))
                    for k in range(TOPK):
                        dve.wait_ge(S["combined"], (1 + 3 * (TOPK - 1)) * p + 1 + (TOPK - 1) * t + k)
                        ins = V.scalar_tensor_tensor(out=x1_tok[0:n, t, :], in0=rows_y[t][0:n, k, :], scalar=gates_p[0:n, t, k:k + 1],
                                                     in1=x1_tok[0:n, t, :], op0=ALU.mult, op1=ALU.add)
                        if k < TOPK - 1:
                            done("combined", ins)
                    done("x2_ready", ins)
            dve.wait_ge(S["final_loaded"], 16)
            for t, n in enumerate(ROWS):
                dve.wait_ge(S["x2rms_ready"], t + 1)
                link(V.reciprocal(ssq[0:n, t:t + 1], ssq[0:n, t:t + 1]))
                done("out_ready", V.scalar_tensor_tensor(out=x1_tok[0:n, t, :], in0=x1_tok[0:n, t, :], scalar=ssq[0:n, t:t + 1],
                                                         in1=n_final[0:n, :], op0=ALU.mult, op1=ALU.mult))


_INS = ['x_prompt', 'x_sample', 'state_lru_conv', 'state_lru_h', 'state_ssd_conv', 'state_ssd', 'norm_mix', 'w_in',
        'conv_lru_w', 'conv_lru_b', 'w_rg', 'b_rg', 'w_ig', 'b_ig', 'lam', 'w_proj_a', 'conv_ssd_w', 'conv_ssd_b',
        'dt_bias', 'a_log', 'd_skip', 'ssd_norm', 'w_proj_b', 'w_out', 'norm_ffn', 'w_router', 'b_router',
        'w_gate_up', 'b_gate_up', 'w_down', 'b_down', 'norm_final']
_CONV = 3072
_OUTS = [(1, TP, D), (TS, 1, D), (1, 1, HIST, D), (1, 1, D), (1, 1, HIST, _CONV), (1, 1, HEADS, HD, NS),
         (1, TS, HIST, D), (1, TS, D), (1, TS, HIST, _CONV), (1, TS, HEADS, HD, NS)]


def kernel(**inputs):
    import numpy as _np
    import concourse.bacc as _bacc
    from concourse import mybir as _mybir
    from concourse.bass_utils import run_bass_kernel_spmd as _run

    nc = _bacc.Bacc("TRN2", target_bir_lowering=False, num_devices=1)
    arrays, args = {}, {}
    for name in _INS:
        x = _np.ascontiguousarray(inputs[name])
        arrays[f"in_{name}"] = x
        args[name] = nc.dram_tensor(f"in_{name}", x.shape, _mybir.dt.from_np(x.dtype), kind="ExternalInput").ap()
    for i, shape in enumerate(_OUTS):
        args[f"out_{i}"] = nc.dram_tensor(f"out_{i}", shape, _mybir.dt.float32, kind="ExternalOutput").ap()
    build(nc, args)
    r = _run(nc, [arrays], core_ids=[0])
    return tuple(r.results[0][f"out_{i}"] for i in range(len(_OUTS)))
```

```python
from contextlib import ExitStack

import concourse.bass as bass
from concourse import mybir
from concourse.alu_op_type import AluOpType as ALU

ACT = mybir.ActivationFunctionType
F32 = mybir.dt.float32
U32 = mybir.dt.uint32
I32 = mybir.dt.int32
AXX = mybir.AxisListType.X

P = 128
D = 1024
KT = D // P
TP = 256
TS = 8
NT = TP + TS
CHUNK = 128
CW = 4
HIST = CW - 1
CIN = HIST + TP + CW * TS
S_IN = HIST + TP
HEADS, HD, GROUPS, NS = 32, 64, 4, 128
HPG = HEADS // GROUPS
E, TOPK, SLOTS = 32, 4, 64
MAXP = -(-NT // SLOTS)
EPS = 1e-6
NEG = -1e30
XS, BT, CT, LX = 0, 16, 20, 24
NCONV = 32
GATE, Z, GA, GB, NPLAIN = 0, 8, 24, 32, 40
W_COL = [4096, 5120, 6144, 0, 1024, 2048, 3072, 7200, 8224]
DT_COL = 7168
SLOT = 2048
NSLOT = 12


def build(nc, a):
    with ExitStack() as ctx:
        def sb(name, shape, dt=F32):
            return ctx.enter_context(nc.sbuf_tensor(name, shape, dt))

        def sem(name):
            return ctx.enter_context(nc.semaphore(name))

        ring = sb("ring", [P, NSLOT * SLOT])
        plain_t = sb("plain", [P, NPLAIN * NT])
        conv_t = sb("conv", [P, NCONV * NT])
        xT = sb("xT", [P, KT, NT])
        xnT = sb("xnT", [P, KT, NT])
        ident = sb("ident", [P, P])
        ones = sb("ones", [P, P])
        before = sb("before", [P, P])
        cmask = sb("cmask", [P, P])
        slot_no = sb("slot_no", [P, MAXP * SLOTS])
        ex_t = sb("ex", [E, HEADS * HD])
        cvec = sb("cvec", [P, CW + 1, NCONV])
        vec = sb("vec", [P, 88])
        rstd = sb("rstd", [P, 4, NT])
        small = sb("small", [P, 704])
        hv = sb("hv", [HEADS, 64])
        go = sb("go", [P, 1 + MAXP])

        plain = plain_t[:, :].rearrange("p (t n) -> p t n", n=NT)
        conv = conv_t[:, :].rearrange("p (t n) -> p t n", n=NT)
        ex = ex_t[:, :].rearrange("p (h c) -> p h c", c=HD)
        stream = [ring[:, s * SLOT:(s + 1) * SLOT] for s in range(NSLOT)]

        A0 = 4 * SLOT

        def arena(start, size):
            return ring[:, A0 + start:A0 + start + size]

        cin = arena(0, NCONV * CIN).rearrange("p (t n) -> p t n", n=CIN)
        T0 = NCONV * CIN
        sq = arena(T0, KT * NT).rearrange("p (t n) -> p t n", n=NT)
        lru = [arena(T0 + i * KT * NT, KT * NT).rearrange("p (t n) -> p t n", n=NT) for i in range(3)]
        x_rows = plain_t[:, 0:3 * D].rearrange("p (t d) -> p t d", d=D)
        hist_rows = plain_t[:, 3 * D:7 * D]
        rows_a = plain_t[:, 7 * D:7 * D + P]
        rows_b = plain_t[:, 7 * D + P:7 * D + 2 * P]
        h0_rows = plain_t[:, 7 * D + 2 * P:8 * D + 2 * P]
        gw = plain_t[:, GB * NT:GB * NT + 16 * P].rearrange("p (g t c) -> p g t c", g=2, t=KT)

        b_rg, b_ig, lam = vec[:, 0:8], vec[:, 8:16], vec[:, 16:24]
        ssd_norm, n_ffn, n_mix, dskip = vec[:, 24:40], vec[:, 40:48], vec[:, 48:56], vec[:, 56:72]
        sp4, sp8n = vec[:, 72:80], vec[:, 80:88]
        lt = [small[:, 8 * i:8 * i + 8] for i in range(5)]
        h0T = small[:, 64:128].rearrange("p (t b) -> p t b", b=TS)
        dsk = small[:, 128:130]
        dt_b, a_log, a_neg = hv[:, 0:1], hv[:, 1:2], hv[:, 2:3]

        xd = arena(0, 2 * 2048).rearrange("p (c h q) -> p c h q", c=2, h=HEADS)
        b_tok = arena(4096, 1024).rearrange("p (c g n) -> p c g n", c=2, g=GROUPS)
        s0T = arena(5120, 2048)
        fin_st = arena(7168, 1024).rearrange("p (r t n) -> p r t n", r=2, t=4)
        m_dec = [arena(o, 1024).rearrange("p (h q) -> p h q", h=HPG) for o in (8192, T0 + 5248)]
        yT = arena(T0, 16 * NT).rearrange("p (t n) -> p t n", n=NT)
        c_dec = [arena(o, 1024).rearrange("p (h q) -> p h q", h=HPG) for o in (T0 + 4224, 0)]
        xw = arena(T0 + 5248, 1536).rearrange("p (w h q) -> p w h q", w=3, h=HPG)
        cb = plain_t[:, GA * NT:GA * NT + 1024].rearrange("p (c g q) -> p c g q", c=2, g=GROUPS)
        hist_out = plain_t[:, Z * NT:Z * NT + 4096]
        h_out_t = plain_t[:, GB * NT:GB * NT + 1024]
        tok = small[:, 384:512].rearrange("p (w h) -> p w h", w=4)
        last = small[:, 512:576].rearrange("p (c h) -> p c h", c=2)
        wdec = small[:, 576:672].rearrange("p (w h) -> p w h", w=3)
        tmp_s = small[:, 192:384]
        dtw = [lru[i // 4][0:HEADS, i % 4 * 2, :] for i in range(8)]
        dtT, acT, daT = rstd[0:HEADS, 1, :], rstd[0:HEADS, 2, :], rstd[0:HEADS, 3, :]
        diag = hv[:, 0:64]
        st = [v.rearrange("p (t n) -> p t n", n=NS)
              for v in (conv_t[:, LX * NT:LX * NT + 2048], arena(0, 2048), arena(2048, 2048))]
        outer = [arena(o, 2048).rearrange("p (t n) -> p t n", n=NS) for o in (4096, 6144)]
        bc_rows = plain_t[:, GA * NT + 1024:GA * NT + 2048]
        bc_all = [v.rearrange("p (w g n) -> p w g n", w=2, g=GROUPS) for v in
                  (conv_t[:, BT * NT:BT * NT + 1024], conv_t[:, BT * NT + 1024:BT * NT + 2048], arena(T0 + 4224, 1024))]
        dx = rstd[:, 0, 0:32 * TS].rearrange("p (t w) -> p t w", w=2 * TS)
        xds = small[:, 256:384].rearrange("p (t b) -> p t b", b=TS)
        ys = small[:, 0:128].rearrange("p (t b) -> p t b", b=TS)
        e_bias = plain_t[0:E, 0:3 * D]
        xg, g1, u1, sg, ha, y_out = (plain_t[:, 3 * D + 512 * i:3 * D + 512 * i + 512] for i in range(6))
        xt, ht = (plain_t[:, 6 * D + 512 * i:6 * D + 512 * i + 512].rearrange("p (c s) -> p c s", c=4) for i in range(2))
        pick = plain_t[:, 7 * D:7 * D + 3 * SLOTS].rearrange("p (t s) -> p t s", t=3)
        pick_e = plain_t[0:E, 7 * D + 192:7 * D + 256]
        n_final = plain_t[:, 9 * D:10 * D]
        u_tok = conv_t[:, 0:3 * D].rearrange("p (t d) -> p t d", t=3)
        x1_tok = conv_t[:, 3 * D:6 * D].rearrange("p (t d) -> p t d", t=3)
        at = [6 * D]

        def scratch(*shape):
            size = 1
            for n in shape:
                size *= n
            v = conv_t[:, at[0]:at[0] + size]
            at[0] += size
            assert at[0] <= NCONV * NT
            if len(shape) == 1:
                return v
            names = "abc"[:len(shape)]
            return v.rearrange(f"p ({' '.join(names)}) -> p {' '.join(names)}", **dict(zip(names, shape)))

        logits, mark, rank = scratch(3, E), scratch(3, E), scratch(3, E)
        slot_of = scratch(3, E + 1)
        top, top_i, top_f, gates = scratch(3, 8), scratch(3, 8).bitcast(U32), scratch(3, 8), scratch(3, TOPK)
        hot = scratch(3, TOPK, E)
        picked, picked_i = scratch(3, TOPK), scratch(3, TOPK).bitcast(U32)
        pass_of, gates_p = scratch(3, TOPK), scratch(3, TOPK)
        total, tmp_e = scratch(E), scratch(3, E)
        most, passes_f, passes, ssq = scratch(1), scratch(1), scratch(1).bitcast(I32), scratch(3)
        w_router = plain_t[:, 3 * D:3 * D + KT * E].rearrange("p (k e) -> p k e", k=KT)
        b_router = small[:, 672:704]
        ROWS = (P, P, TS)
        rows_y = [ring[:, 4 * D * t:4 * D * t + 4 * D].rearrange("p (k d) -> p k d", k=TOPK) for t in range(3)]
        bc_dram = nc.dram_tensor("bc_dram", [TS, 2 * GROUPS * NS], F32, kind="Internal").ap()
        slots_y = nc.dram_tensor("slots_y", [E * SLOTS, D], F32, kind="Internal").ap()

        ps = [ctx.enter_context(nc.psum_tensor(f"bank{i}", [P, 512], F32)) for i in range(8)]

        uses = [("vec", "v"), ("hist0", "v"), ("hist1", "v"), ("h0", "v")]
        uses += [(f"x{k}", "s") for k in range(KT)] + [("ss0", "s"), ("dt", "v"), ("tok", "v")]
        uses += [(f"ho{q}", "s") for q in range(8)]
        uses += [(f"xs{c}{g}", "v") for c in range(2) for g in range(GROUPS)]
        uses += [(f"bt{c}", "s") for c in range(2)] + [(f"cb{c}", "s") for c in range(2)]
        uses += [("smp", "v"), ("bc0", "s"), ("bc1", "s")]
        uses += [(f"{r}{t}", "s") for t in range(KT) for r in ("rg", "ig")] + [(f"hl{q}", "s") for q in range(2)]
        for g in range(GROUPS):
            uses += [(f"s0{g}", "s"), (f"fs{g}", "s")]
        for c in range(2):
            uses += [(f"ac{c}0{i}", "v") for i in range(2)]
            for g in range(GROUPS):
                if g + 1 < GROUPS:
                    uses += [(f"ac{c}{g + 1}{i}", "v") for i in range(2)]
                uses += [(f"y{c}{g}", "v")]
        uses += [(f"gn{g}", "s") for g in range(GROUPS)] + [("ss1", "s")]
        uses += [(f"x1_{t}{h}", "s") for t in range(3) for h in range(2)] + [("logits", "v")]
        uses += [(f"u{t}{h}", "s") for t in range(3) for h in range(2)] + [("rank", "v")]
        index = {name: n for n, (name, _) in enumerate(uses)}
        assert len(index) == len(uses)
        nth = {name: sum(w == who for _, w in uses[:index[name]]) for name, who in uses}

        def bank(name):
            return ps[2 + index[name] % 6]

        filled, emptied = sem("psum_filled"), {"v": sem("psum_emptied_by_dve"), "s": sem("psum_emptied_by_act")}

        def open_bank(name):
            if index[name] >= 6:
                prev, who = uses[index[name] - 6]
                nc.tensor.wait_ge(emptied[who], nth[prev] + 1)
            return bank(name)

        def take_bank(eng, name):
            eng.wait_ge(filled, index[name] + 1)
            return bank(name)

        names = """acc2_emptied acc_emptied acc_ready all_stored bc_used bias_loaded cdec_exp cdec_ready consts_set conv_done
            conv_step da_exp dec_exp dec_in diag_ready dskip_loaded dskip_spread dt_exp dt_z ex_set final_loaded
            fs_stored0 fs_stored1 g1_ready ga_ready gated_ready gates_exp gates_in gates_loaded gates_zeroed gu_emptied
            h_ready ha_ready heads_loaded hist_loaded hist_stored hl_stored ht_filled ht_ready lam_abs lam_exp
            m_ready mark_ready merged_ready out_ready outer_ready passes_ready pick_e_ready picked_ready pick_ready combined rows_used rms_ready
            router_loaded sg_ready silu_done slots_stored smp_ready sqrt_done squares_ready st_done st_stored
            stream_used u2_ready a_ready u_ready ug_ready vec_loaded w_used wdec_exp wdec_in x1_sq x2_sq x1rms_ready
            x2_ready x2rms_ready x_loaded xg_filled xg_ready xn_ready xt_filled xt_ready xw_ready y_emptied
            y_final y_stored yrms_ready ysq_ready yz_ready z_silu bc_stored""".split()
        S = {name: sem(name) for name in names}
        st_loaded = [sem(f"st_loaded{i}") for i in range(3)]
        bc_landed = [sem(f"bc_landed{i}") for i in range(3)]
        w_landed = [sem(f"w_landed{i}") for i in range(NSLOT)]
        rows_landed = [sem(f"rows_landed{t}") for t in range(3)]
        p_gu, p_xg, p_xt, p_ht, p_y = ps[0:2], ps[2], ps[3], ps[4], ps[5]
        landed = [sem(f"stream_landed{i}") for i in range(4)]
        act_step, dve_step, pool_step = sem("act_step"), sem("dve_step"), sem("pool_step")

        def linker(eng, step):
            count = [0]

            def link(ins):
                count[0] += 1
                ins.then_inc(step, 1)
                eng.wait_ge(step, count[0])
            return link

        def mm(out, w, x, start, stop):
            return nc.tensor.matmul(out, w, x, start=start, stop=stop)

        block = ctx.enter_context(nc.Block())

        @block.sync
        def _(sp):
            sp.dma_start(x_rows[:, 0:2, :], a["x_prompt"][0].rearrange("(t p) d -> p t d", p=P)).then_inc(S["x_loaded"], 16)
            sp.dma_start(x_rows[0:TS, 2, :], a["x_sample"][:, 0, :]).then_inc(S["x_loaded"], 16)
            w_in = a["w_in"][0].rearrange("(k p) c -> p k c", p=P)
            free_at, tiles = [0] * 4, 0
            for col in W_COL:
                for s in range(4):
                    if free_at[s]:
                        sp.wait_ge(S["acc_ready"], free_at[s])
                    sp.dma_start(stream[s].rearrange("p (k c) -> p k c", k=KT),
                                 w_in[:, :, col + 256 * s:col + 256 * s + 256]).then_inc(landed[s], 16)
                    tiles += 2
                    free_at[s] = tiles
            w_gu, w_dn = a["w_gate_up"][0], a["w_down"][0]

            def load_expert(e, free, slots=range(NSLOT)):
                for c in slots:
                    free(c)
                    if c < KT:
                        src = w_gu[e, P * c:P * c + P, :]
                        dst = stream[c]
                    else:
                        src = w_dn[e, 2 * P * (c - KT):2 * P * (c - KT) + 2 * P, :].rearrange("(k p) n -> p k n", p=P)
                        dst = stream[c].rearrange("p (k n) -> p k n", k=2)
                    sp.dma_start(dst, src).then_inc(w_landed[c], 16)

            def after_samples(c):
                sp.wait_ge(S["yz_ready"], 1)
                sp.wait_ge(S["st_stored"], 16 * TS)

            for w, k in ((a["w_proj_a"], KT), (a["w_proj_b"], 2 * KT), (a["w_out"], KT)):
                width = SLOT // k
                wv = w[0].rearrange("(k p) c -> p k c", p=P)
                for c in range(D // width):
                    s = c % 4
                    sp.wait_ge(S["acc_ready"], free_at[s])
                    sp.dma_start(stream[s].rearrange("p (k c) -> p k c", k=k),
                                 wv[:, :, c * width:(c + 1) * width]).then_inc(landed[s], 16)
                    tiles += width // P
                    free_at[s] = tiles
                    if k == 2 * KT and c == 4:
                        load_expert(0, after_samples, (4, 5, 6, 7, 11))
            def after_mixer(c):
                if c < 4:
                    sp.wait_ge(S["acc_ready"], free_at[c])
                else:
                    sp.wait_ge(S["acc_ready"], 88)

            def after_item(i):
                def free(c):
                    sp.wait_ge(S["w_used"], NSLOT * (i - 1) + c + 1)
                return free

            def after_pass(p, e):
                free_of_item = after_item(E * p + e)

                def free(c):
                    if c == 0:
                        sp.wait_ge(S["rows_used"], p)
                    free_of_item(c)
                return free

            load_expert(0, after_mixer, (8, 9, 10, 0, 1, 2, 3))
            with sp.Fori(1, E) as e:
                load_expert(e, after_item(e))
            sp.wait_ge(S["passes_ready"], 1)
            n_passes = sp.value_load(passes[0:1, 0:1], min_val=1, max_val=MAXP)
            with sp.If(n_passes > 1):
                with sp.Fori(1, n_passes) as p:
                    with sp.Fori(0, E) as e:
                        load_expert(e, after_pass(p, e))
            sp.wait_ge(S["out_ready"], 3)
            sp.dma_start(a["out_0"][0].rearrange("(t p) d -> p t d", p=P), x1_tok[:, 0:2, :]).then_inc(S["y_stored"], 16)
            sp.dma_start(a["out_1"][:, 0, :], x1_tok[0:TS, 2, :]).then_inc(S["y_stored"], 16)
            sp.wait_ge(S["y_stored"], 32)
            sp.wait_ge(S["fs_stored0"], 32)
            sp.wait_ge(S["fs_stored1"], 32)

        @block.gpsimd
        def _(pool):
            link = linker(pool, pool_step)
            nc.gpsimd.memset(gw, 0.0).then_inc(S["gates_zeroed"], 1)
            nc.gpsimd.memset(ones[:, :], 1.0)
            nc.gpsimd.memset(cmask[:, :], 0.0)
            nc.gpsimd.memset(before[:, :], 1.0)
            link(nc.gpsimd.memset(ident[:, :], 0.0))
            nc.gpsimd.affine_select(out=ident[:, :], in_=ident[:, :], compare_op=ALU.not_equal, fill=1.0,
                                    base=0, pattern=[[-1, P]], channel_multiplier=1)
            nc.gpsimd.affine_select(out=cmask[:, :], in_=cmask[:, :], compare_op=ALU.is_ge, fill=NEG,
                                    base=0, pattern=[[1, P]], channel_multiplier=-1)
            nc.gpsimd.affine_select(out=before[:, :], in_=before[:, :], compare_op=ALU.is_gt, fill=0.0,
                                    base=0, pattern=[[1, P]], channel_multiplier=-1)
            nc.gpsimd.iota(slot_no[:, :], pattern=[[1, MAXP * SLOTS]], base=0, channel_multiplier=0,
                           allow_small_or_imprecise_dtypes=True).then_inc(S["consts_set"], 1)
            def states(name, i):
                return a[name][0, i].rearrange("(t h) q n -> (h q) t n", h=2)

            def load_state(i):
                nc.gpsimd.dma_start(st[i % 3], states("state_ssd", i)).then_inc(st_loaded[i % 3], 16)

            def outer_product(i):
                pool.wait_ge(bc_landed[i % 3], 16 * (i // 3) + 16)
                if i > 1:
                    pool.wait_ge(S["bc_used"], i - 1)
                nc.gpsimd.tensor_tensor(
                    outer[i % 2].rearrange("p (g t) n -> p g t n", g=GROUPS),
                    bc_all[i % 3][:, 0].unsqueeze(2).to_broadcast([P, GROUPS, 4, NS]),
                    xds[:, :, i].rearrange("p (g t) -> p g t", g=GROUPS).unsqueeze(3).to_broadcast([P, GROUPS, 4, NS]),
                    ALU.mult).then_inc(S["outer_ready"], 1)

            pool.wait_ge(filled, index["hl1"] + 1)
            pool.wait_ge(S["gated_ready"], 1)
            load_state(0)
            pool.wait_ge(filled, index["y13"] + 1)
            load_state(1)
            load_state(2)
            for n in range(2):
                pool.wait_ge(S[f"fs_stored{n}"], 32)
            pool.wait_ge(S["smp_ready"], 1)
            outer_product(0)
            for i in range(TS):
                if i + 1 < TS:
                    outer_product(i + 1)
                if 1 <= i < TS - 2:
                    pool.wait_ge(S["st_stored"], 16 * i)
                    pool.wait_ge(S["bc_used"], i)
                    load_state(i + 2)
                pool.wait_ge(S["st_done"], i + 1)
                nc.gpsimd.dma_start(states("out_9", i), st[i % 3]).then_inc(S["st_stored"], 16)
            pool.wait_ge(S["st_stored"], 16 * TS)
            pool.wait_ge(S["passes_ready"], 1)
            pool.wait_ge(S["picked_ready"], 3)
            link(nc.gpsimd.memset(go[:, :], 1.0))
            n_passes = pool.value_load(passes[0:1, 0:1], min_val=1, max_val=MAXP)
            with pool.Fori(0, n_passes) as p:
                pool.wait_ge(S["all_stored"], p + 1)
                nc.gpsimd.tensor_tensor(go[:, bass.ds(p + 1, 1)], go[:, 0:1], go[:, 0:1], ALU.mult)
                for t, n in enumerate(ROWS):
                    for k in range(TOPK):
                        nc.gpsimd.indirect_dma_start(
                            out=rows_y[t][0:n, k, :], out_offset=None, in_=slots_y[:, :],
                            in_offset=bass.IndirectOffsetOnAxis(picked_i[0:n, t, k:k + 1], 0)).then_inc(rows_landed[t], 16)

        @block.scalar
        def _(act):
            link = linker(act, act_step)
            rows = [("conv_ssd_w", 0, 96, "o j (t c) -> (o j t) c"), ("conv_ssd_b", 96, 24, "o (t c) -> (o t) c")]
            for name, r, n, pat in rows:
                act.dma_start(rows_a[r:r + n, :], a[name].rearrange(pat, c=P)).then_inc(S["vec_loaded"], 16)
            rows = [("conv_lru_w", 0, 32, "o j (t c) -> (o j t) c"), ("conv_lru_b", 32, 8, "o (t c) -> (o t) c"),
                    ("lam", 56, 8, "o (t c) -> (o t) c"), ("ssd_norm", 64, 16, "o (t c) -> (o t) c"),
                    ("norm_ffn", 80, 8, "o (t c) -> (o t) c"), ("norm_mix", 88, 8, "o (t c) -> (o t) c")]
            for name, r, n, pat in rows:
                act.dma_start(rows_b[r:r + n, :], a[name].rearrange(pat, c=P)).then_inc(S["vec_loaded"], 16)
            for name, r in (("b_rg", 40), ("b_ig", 48)):
                act.dma_start(rows_b[r:r + 8, :].rearrange("t (h j) -> t h j", h=2),
                              a[name][0].rearrange("(t h) j -> t h j", h=2)).then_inc(S["vec_loaded"], 16)
            act.dma_start(dsk[96:112, :], a["d_skip"][0].rearrange("(t h) -> t h", h=2)).then_inc(S["dskip_loaded"], 16)
            act.dma_start(dt_b, a["dt_bias"][0].rearrange("(h o) -> h o", o=1)).then_inc(S["heads_loaded"], 16)
            act.dma_start(a_log, a["a_log"][0].rearrange("(h o) -> h o", o=1)).then_inc(S["heads_loaded"], 16)
            act.dma_start(hist_rows[0:24, 0:3072], a["state_ssd_conv"][0].rearrange("b j c -> (b j) c")).then_inc(S["hist_loaded"], 16)
            act.dma_start(hist_rows[0:24, 3072:4096], a["state_lru_conv"][0].rearrange("b j c -> (b j) c")).then_inc(S["hist_loaded"], 16)
            act.dma_start(h0_rows[0:TS, :], a["state_lru_h"][0]).then_inc(S["hist_loaded"], 16)
            act.wait_ge(S["gates_zeroed"], 1)
            for w, name in enumerate(("w_rg", "w_ig")):
                for h in range(2):
                    act.dma_start(gw[64 * h:64 * h + 64, w, :, 64 * h:64 * h + 64],
                                  a[name][0].rearrange("(t h) i j -> h i t j", h=2)[h]).then_inc(S["gates_loaded"], 16)
            act.dma_start(arena(T0 + 3 * KT * NT, KT * HEADS).rearrange("p (k c) -> p k c", k=KT),
                          a["w_in"][0].rearrange("(k p) c -> p k c", p=P)[:, :, DT_COL:DT_COL + HEADS]).then_inc(S["heads_loaded"], 16)
            for k in range(KT):
                b = take_bank(act, f"x{k}")
                nc.scalar.copy(xT[:, k, :], b[:, 0:NT]).then_inc(emptied["s"], 1)
            act.wait_ge(S["lam_abs"], 1)
            nc.scalar.activation(lt[1], lt[1], ACT.Exp, scale=-1.0).then_inc(S["lam_exp"], 1)
            act.wait_ge(S["heads_loaded"], 48)
            nc.scalar.activation(a_neg, a_log, ACT.Exp).then_inc(S["lam_exp"], 1)
            b = take_bank(act, "ss0")
            nc.scalar.activation(rstd[:, 0, :], b[:, 0:NT], ACT.Copy, bias=EPS, scale=1.0 / D).then_inc(emptied["s"], 1)
            act.wait_ge(emptied["s"], nth["ss0"] + 1)
            nc.scalar.activation(rstd[:, 0, :], rstd[:, 0, :], ACT.Sqrt).then_inc(S["rms_ready"], 1)

            def take_tiles(first, end):
                for t in range(first, end):
                    act.wait_ge(S["acc_ready"], t + 1)
                    if t < NCONV:
                        nc.scalar.copy(cin[:, t, HIST:HIST + TP], ps[t % 2][:, 0:TP])
                        nc.scalar.copy(cin[:, t, S_IN + HIST * TS:CIN], ps[t % 2][:, TP:NT]).then_inc(S["acc_emptied"], 1)
                    elif t < NCONV + NPLAIN:
                        nc.scalar.copy(plain[:, t - NCONV, :], ps[t % 2][:, 0:NT]).then_inc(S["acc_emptied"], 1)

                    else:
                        nc.scalar.copy(xnT[:, t - NCONV - NPLAIN, :], ps[t % 2][:, 0:NT]).then_inc(S["acc_emptied"], 1)

            take_tiles(0, LX)
            act.wait_ge(S["dt_z"], 1)
            nc.scalar.activation(dtw[1], dtw[1], ACT.Exp, scale=-1.0).then_inc(S["dt_exp"], 1)
            take_tiles(LX, LX + 4)
            act.wait_ge(S["conv_done"], 1)
            for t in range(0, LX, 8):
                nc.scalar.activation(conv[:, t:t + 8, :], conv[:, t:t + 8, :], ACT.Silu).then_inc(S["silu_done"], 1)
                take_tiles(LX + 4 + t // 4, LX + 6 + t // 4)
            act.wait_ge(S["wdec_in"], 1)
            nc.scalar.activation(wdec, wdec, ACT.Exp).then_inc(S["wdec_exp"], 1)
            take_tiles(34, 40)
            for q in range(8):
                b = take_bank(act, f"ho{q}")
                nc.scalar.copy(hist_out[0:35, 512 * q:512 * q + 512], b[0:35, :]).then_inc(emptied["s"], 1)
            act.wait_ge(emptied["s"], nth["ho7"] + 1)
            act.dma_start(a["out_4"][0, 0], hist_out[0:3, 0:3072]).then_inc(S["hist_stored"], 16)
            act.dma_start(a["out_8"][0, :, 2, :], hist_out[27:35, 0:3072]).then_inc(S["hist_stored"], 16)
            act.dma_start(a["out_2"][0, 0], hist_out[0:3, 3072:4096]).then_inc(S["hist_stored"], 16)
            act.dma_start(a["out_6"][0, :, 2, :], hist_out[27:35, 3072:4096]).then_inc(S["hist_stored"], 16)
            act.dma_start(a["out_8"][0, :, 0:2, :], a["state_ssd_conv"][0, :, 1:3, :]).then_inc(S["hist_stored"], 16)
            act.dma_start(a["out_6"][0, :, 0:2, :], a["state_lru_conv"][0, :, 1:3, :]).then_inc(S["hist_stored"], 16)
            act.wait_ge(S["conv_done"], 2)
            for c in range(2):
                b = take_bank(act, f"bt{c}")
                nc.scalar.copy(b_tok[:, c].rearrange("p g n -> p (g n)"), b[:, :]).then_inc(emptied["s"], 1)
            for c in range(2):
                b = take_bank(act, f"cb{c}")
                nc.scalar.copy(cb[:, c].rearrange("p g n -> p (g n)"), b[:, :]).then_inc(emptied["s"], 1)
            for w in range(2):
                b = take_bank(act, f"bc{w}")
                nc.scalar.copy(bc_rows[0:TS, 512 * w:512 * w + 512], b[0:TS, :]).then_inc(emptied["s"], 1)
            act.wait_ge(emptied["s"], nth["bc1"] + 1)
            act.dma_start(bc_dram[:, :], bc_rows[0:TS, :]).then_inc(S["bc_stored"], 16)
            for t in range(KT):
                b = take_bank(act, f"rg{t}")
                nc.scalar.activation(lru[0][:, t, :], b[:, 0:NT], ACT.Sigmoid, bias=b_rg[:, t:t + 1]).then_inc(emptied["s"], 1)
                b = take_bank(act, f"ig{t}")
                nc.scalar.activation(lru[1][:, t, :], b[:, 0:NT], ACT.Sigmoid, bias=b_ig[:, t:t + 1]).then_inc(emptied["s"], 1)
            act.wait_ge(emptied["s"], nth["ig7"] + 1)
            for t in range(KT):
                ins = nc.scalar.activation(lru[2][:, t, :], lru[0][:, t, :], ACT.Exp, scale=sp8n[:, t:t + 1])
            ins.then_inc(S["a_ready"], 1)
            act.wait_ge(S["a_ready"], 1)
            for t in range(KT):
                ins = nc.scalar.activation(lru[0][:, t, :], lru[0][:, t, :], ACT.Tanh, scale=sp4[:, t:t + 1])
            ins.then_inc(S["u_ready"], 1)
            act.wait_ge(S["u_ready"], 1)
            nc.scalar.activation(lru[0], lru[0], ACT.Sqrt).then_inc(S["sqrt_done"], 1)
            act.wait_ge(S["hist_stored"], 96)
            take_tiles(40, 42)
            nc.scalar.activation(plain[:, GATE:GATE + 8, :], plain[:, GATE:GATE + 8, :], ACT.Gelu_apprx_tanh).then_inc(S["sqrt_done"], 1)
            act.wait_ge(S["smp_ready"], 1)
            nc.scalar.activation(dx[:, :, TS:2 * TS], dx[:, :, TS:2 * TS], ACT.Exp).then_inc(S["da_exp"], 1)
            take_tiles(42, 48)
            for q in range(2):
                b = take_bank(act, f"hl{q}")
                nc.scalar.copy(h_out_t[0:9, 512 * q:512 * q + 512], b[0:9, :]).then_inc(emptied["s"], 1)
            act.wait_ge(emptied["s"], nth["hl1"] + 1)
            act.dma_start(a["out_3"][0], h_out_t[0:1, :]).then_inc(S["hl_stored"], 16)
            act.dma_start(a["out_7"][0], h_out_t[1:9, :]).then_inc(S["hl_stored"], 16)
            for g in range(GROUPS):
                b = take_bank(act, f"s0{g}")
                nc.scalar.copy(s0T[:, 512 * g:512 * g + 512], b[:, :]).then_inc(emptied["s"], 1)
                b = take_bank(act, f"fs{g}")
                if g >= 2:
                    act.wait_ge(S[f"fs_stored{g % 2}"], 16)
                nc.scalar.copy(fin_st[:, g % 2].rearrange("p t n -> p (t n)"), b[:, :]).then_inc(emptied["s"], 1)
                act.wait_ge(emptied["s"], nth[f"fs{g}"] + 1)
                act.dma_start(a["out_5"][0, 0].rearrange("(g t h) q n -> g (h q) t n", t=4, h=2)[g], fin_st[:, g % 2]).then_inc(S[f"fs_stored{g % 2}"], 16)

            def decay_since_start(g):
                act.wait_ge(filled, index[f"y1{g - 2}" if g > 1 else "y03"] + 1)
                for h in range(2):
                    b = take_bank(act, f"ac1{g}{h}")
                    ins = nc.scalar.activation(c_dec[g % 2][:, 4 * h:4 * h + 4, :].rearrange("p h q -> p (h q)"), b[:, :], ACT.Exp)
                ins.then_inc(S["cdec_exp"], 1)

            def decay_between(c, g):
                act.wait_ge(emptied["v"], nth[f"ac{c}{g}1"] + 1)
                m = m_dec[(GROUPS * c + g) % 2]
                nc.scalar.activation(m, m, ACT.Exp).then_inc(S["dec_exp"], 1)

            for g in range(GROUPS):
                decay_between(0, g)
            decay_since_start(0)
            decay_between(1, 0)
            for g in range(GROUPS):
                if g + 1 < GROUPS:
                    decay_since_start(g + 1)
                take_tiles(48 + 2 * g, 49 + 2 * g)
                if g + 1 < GROUPS:
                    decay_between(1, g + 1)
                take_tiles(49 + 2 * g, 50 + 2 * g)
            act.wait_ge(S["m_ready"], 8)
            act.wait_ge(filled, index["y13"] + 1)
            act.wait_ge(S["bc_stored"], 16)

            def load_bc(i):
                act.dma_start(bc_all[i % 3].rearrange("p w g n -> p (w g n)"), bc_dram[i:i + 1, :].to_broadcast([P, 1024])).then_inc(bc_landed[i % 3], 16)

            for i in range(3):
                load_bc(i)
            act.wait_ge(S["acc_emptied"], 56)
            nc.scalar.activation(plain[:, Z:Z + 16, :], plain[:, Z:Z + 16, :], ACT.Silu).then_inc(S["z_silu"], 1)
            act.wait_ge(S["hl_stored"], 32)
            take_tiles(56, 60)
            for i in range(3, TS):
                act.wait_ge(S["bc_used"], i - 2)
                load_bc(i)
                take_tiles(54 + 2 * i, 56 + 2 * i)
            take_tiles(70, 72)
            act.wait_ge(S["acc_emptied"], 72)
            nc.scalar.activation(plain[:, GA:GA + 16, :], plain[:, GA:GA + 16, :], ACT.Sigmoid).then_inc(S["ga_ready"], 1)
            take_tiles(72, 76)
            act.wait_ge(S["yz_ready"], 1)
            nc.scalar.activation(plain[:, Z:Z + 16, :], yT, ACT.Square).then_inc(S["ysq_ready"], 1)
            take_tiles(76, 77)
            for g in range(GROUPS):
                b = take_bank(act, f"gn{g}")
                nc.scalar.activation(rstd[:, g, :], b[:, 0:NT], ACT.Copy, bias=EPS, scale=4.0 / 2048).then_inc(emptied["s"], 1)
            act.wait_ge(emptied["s"], nth["gn3"] + 1)
            nc.scalar.activation(rstd[:, :, :], rstd[:, :, :], ACT.Sqrt).then_inc(S["yrms_ready"], 1)
            take_tiles(77, 80)
            act.dma_start(w_router, a["w_router"][0].rearrange("(k p) e -> p k e", p=P)).then_inc(S["router_loaded"], 16)
            act.dma_start(b_router, a["b_router"].to_broadcast([P, E])).then_inc(S["router_loaded"], 16)
            act.wait_ge(S["acc_ready"], 80)
            act.dma_start(e_bias[:, 0:2 * D], a["b_gate_up"][0]).then_inc(S["bias_loaded"], 16)
            act.dma_start(e_bias[:, 2 * D:3 * D], a["b_down"][0]).then_inc(S["bias_loaded"], 16)
            b = take_bank(act, "ss1")
            nc.scalar.activation(rstd[:, 0, :], b[:, 0:NT], ACT.Copy, bias=EPS, scale=1.0 / D).then_inc(emptied["s"], 1)
            act.wait_ge(emptied["s"], nth["ss1"] + 1)
            nc.scalar.activation(rstd[:, 0, :], rstd[:, 0, :], ACT.Sqrt).then_inc(S["x1rms_ready"], 1)
            act.dma_start(n_final, a["norm_final"].rearrange("(o d) -> o d", o=1).to_broadcast([P, D])).then_inc(S["final_loaded"], 16)

            def take_rows(w, dst):
                for t, n in enumerate(ROWS):
                    for h in range(2):
                        b = take_bank(act, f"{w}{t}{h}")
                        nc.scalar.copy(dst[0:n, t, 512 * h:512 * h + 512], b[0:n, :]).then_inc(emptied["s"], 1)

            take_rows("x1_", x1_tok)
            take_rows("u", u_tok)
            act.wait_ge(S["gates_in"], 3)
            for t, n in enumerate(ROWS):
                ins = nc.scalar.activation(gates[0:n, t, :], gates[0:n, t, :], ACT.Exp)
            ins.then_inc(S["gates_exp"], 1)
            act.wait_ge(S["passes_ready"], 1)
            n_passes = act.value_load(passes[0:1, 0:1], min_val=1, max_val=MAXP)

            def take_tokens(j):
                act.wait_ge(S["xg_filled"], j + 1)
                nc.scalar.copy(xg, p_xg[:, :]).then_inc(S["xg_ready"], 1)
                act.wait_ge(S["xt_filled"], j + 1)
                nc.scalar.copy(xt.rearrange("p c s -> p (c s)"), p_xt[:, :]).then_inc(S["xt_ready"], 1)

            with act.Fori(0, n_passes) as p:
                take_tokens((E + 1) * p)
                for t in range(3):
                    act.wait_ge(rows_landed[t], 16 * TOPK * p)
                with act.Fori(0, E) as e:
                    i = E * p + e
                    act.wait_ge(S["g1_ready"], i + 1)
                    nc.scalar.activation(sg, g1, ACT.Sigmoid, scale=1.702).then_inc(S["sg_ready"], 1)
                    take_tokens((E + 1) * p + e + 1)
                    act.wait_ge(S["ht_filled"], i + 1)
                    nc.scalar.copy(ht.rearrange("p c s -> p (c s)"), p_ht[:, :]).then_inc(S["ht_ready"], 1)
                    act.wait_ge(S["w_used"], NSLOT * i + NSLOT)
                    act.wait_ge(S["slots_stored"], 32 * i)
                    nc.scalar.copy(y_out, p_y[:, :]).then_inc(S["y_emptied"], 1)
                    act.wait_ge(S["y_emptied"], i + 1)
                    for h in range(2):
                        act.dma_start(slots_y[bass.ds(SLOTS * e, SLOTS), 512 * h:512 * h + 512],
                                      y_out[SLOTS * h:SLOTS * h + SLOTS, :]).then_inc(S["slots_stored"], 16)
                act.wait_ge(S["slots_stored"], 32 * E * (p + 1))
                nc.scalar.copy(sg[:, 0:1], ssq[:, 0:1]).then_inc(S["all_stored"], 1)
                for t, n in enumerate(ROWS):
                    act.wait_ge(S["x2_ready"], 3 * p + t + 1)
                    nc.scalar.activation(rows_y[t][0:n, 0, :], x1_tok[0:n, t, :], ACT.Square,
                                         accum_out=ssq[0:n, t:t + 1]).then_inc(S["rows_used"] if t == 2 else S["x2_sq"], 1)
            act.wait_ge(S["rows_used"], n_passes)
            for t, n in enumerate(ROWS):
                link(nc.scalar.activation(ssq[0:n, t:t + 1], ssq[0:n, t:t + 1], ACT.Copy, bias=EPS, scale=1.0 / D))
                nc.scalar.activation(ssq[0:n, t:t + 1], ssq[0:n, t:t + 1], ACT.Sqrt).then_inc(S["x2rms_ready"], 1)

        @block.tensor
        def _(pe):
            pe.wait_ge(S["consts_set"], 1)

            def turn(out, src, k):
                return nc.tensor.transpose(out, src, ident[0:k, 0:k])

            pe.wait_ge(S["vec_loaded"], 160)
            pe.wait_ge(S["dskip_spread"], 1)
            b = open_bank("vec")
            turn(b[:, 0:120], rows_a[0:120, :], 120)
            turn(b[:, 128:240], rows_b[0:112, :], 112).then_inc(filled, 1)
            pe.wait_ge(S["hist_loaded"], 48)
            for q in range(2):
                b = open_bank(f"hist{q}")
                for j in range(16):
                    t = 16 * q + j
                    ins = turn(b[:, 24 * j:24 * j + 24], hist_rows[0:24, P * t:P * t + P], 24)
                ins.then_inc(filled, 1)
            b = open_bank("h0")
            for t in range(KT):
                ins = turn(b[:, TS * t:TS * t + TS], h0_rows[0:TS, P * t:P * t + P], TS)
            ins.then_inc(filled, 1)
            pe.wait_ge(S["x_loaded"], 32)
            for k in range(KT):
                b = open_bank(f"x{k}")
                for t in range(3):
                    n = P if t < 2 else TS
                    ins = turn(b[:, P * t:P * t + n], x_rows[0:n, t, P * k:P * k + P], n)
                ins.then_inc(filled, 1)

            def sum_squares(name, sq_of, n, ready, per):
                b = open_bank(name)
                for k in range(n):
                    if per:
                        pe.wait_ge(ready, k + 1)
                    ins = mm(b[:, 0:NT], ones[:, :], sq_of(k), k == 0, k == n - 1)
                ins.then_inc(filled, 1)

            sum_squares("ss0", lambda k: sq[:, k, :], KT, S["squares_ready"], True)
            pe.wait_ge(S["xn_ready"], 1)

            def in_slot(g, s):
                pe.wait_ge(landed[s], 16 * g + 16)
                for m in range(2):
                    if not (isinstance(g, int) and g == 0 and s == 0):
                        pe.wait_ge(S["acc_emptied"], 8 * g + 2 * s + m - 1)
                    for k in range(KT):
                        w = stream[s][:, 256 * k + P * m:256 * k + P * m + P]
                        ins = mm(ps[m][:, 0:NT], w, xnT[:, k, :], k == 0, k == KT - 1)
                    ins.then_inc(S["acc_ready"], 1)

            def in_groups(g0, n):
                if n == 1:
                    for s in range(4):
                        in_slot(g0, s)
                else:
                    with pe.Fori(g0, g0 + n) as g:
                        for s in range(4):
                            in_slot(g, s)

            in_groups(0, 1)
            in_groups(1, 2)
            b = open_bank("dt")
            wdt = arena(T0 + 3 * KT * NT, KT * HEADS).rearrange("p (k c) -> p k c", k=KT)
            pe.wait_ge(S["heads_loaded"], 48)
            for k in range(KT):
                ins = mm(b[0:HEADS, 0:NT], wdt[:, k, :], xnT[:, k, :], k == 0, k == KT - 1)
            ins.then_inc(filled, 1)
            in_groups(3, 1)
            pe.wait_ge(S["diag_ready"], 1)
            b = open_bank("tok")
            for w, src in enumerate((dtT, dtT, acT, acT)):
                turn(b[:, HEADS * w:HEADS * w + HEADS], src[:, CHUNK * (w % 2):CHUNK * (w % 2) + CHUNK], HEADS)
            mm(b[:, 128:192], ones[0:HEADS, :], diag, True, True).then_inc(filled, 1)
            in_groups(4, 1)
            for q in range(8):
                b = open_bank(f"ho{q}")
                for j in range(4):
                    ins = turn(b[0:35, P * j:P * j + P], cin[:, 4 * q + j, TP:CIN], P)
                ins.then_inc(filled, 1)
            pe.wait_ge(S["silu_done"], 3)
            for c in range(2):
                for g in range(GROUPS):
                    b = open_bank(f"xs{c}{g}")
                    for j in range(4):
                        ins = turn(b[:, P * j:P * j + P], conv[:, XS + 4 * g + j, CHUNK * c:CHUNK * c + CHUNK], P)
                    ins.then_inc(filled, 1)
            for c in range(2):
                b = open_bank(f"bt{c}")
                for g in range(GROUPS):
                    ins = turn(b[:, P * g:P * g + P], conv[:, BT + g, CHUNK * c:CHUNK * c + CHUNK], P)
                ins.then_inc(filled, 1)
            for c in range(2):
                b = open_bank(f"cb{c}")
                for g in range(GROUPS):
                    w = slice(CHUNK * c, CHUNK * c + CHUNK)
                    ins = mm(b[:, P * g:P * g + P], conv[:, BT + g, w], conv[:, CT + g, w], True, True)
                ins.then_inc(filled, 1)
            b = open_bank("smp")
            for t in range(16):
                w = ex[:, 2 * t:2 * t + 2, :].rearrange("p h c -> p (h c)")
                mm(b[:, 16 * t:16 * t + 8], w, dtT[:, TP:NT], True, True)
                ins = mm(b[:, 16 * t + 8:16 * t + 16], w, acT[:, TP:NT], True, True)
            ins.then_inc(filled, 1)
            for w in range(2):
                b = open_bank(f"bc{w}")
                for g in range(GROUPS):
                    ins = turn(b[0:TS, P * g:P * g + P], conv[:, BT + 4 * w + g, TP:NT], P)
                ins.then_inc(filled, 1)
            pe.wait_ge(S["gates_loaded"], 64)
            pe.wait_ge(S["conv_done"], 2)
            for t in range(KT):
                for w, n in enumerate(("rg", "ig")):
                    b = open_bank(f"{n}{t}")
                    mm(b[:, 0:NT], gw[:, w, t, :], conv[:, LX + t, :], True, True).then_inc(filled, 1)
            in_groups(5, 1)
            pe.wait_ge(S["h_ready"], 1)
            for q in range(2):
                b = open_bank(f"hl{q}")
                for j in range(4):
                    ins = turn(b[0:9, P * j:P * j + P], conv[:, LX + 4 * q + j, TP - 1:NT], P)
                ins.then_inc(filled, 1)
            for g in range(GROUPS):
                pe.wait_ge(S["xw_ready"], g + 1)
                pe.wait_ge(emptied["s"], nth["bt1"] + 1)
                b = open_bank(f"s0{g}")
                mm(b[:, :], b_tok[:, 0, g, :], xw[:, 0].rearrange("p h q -> p (h q)"), True, True).then_inc(filled, 1)
                b = open_bank(f"fs{g}")
                for j in range(4):
                    for c in range(2):
                        ins = mm(b[:, P * j:P * j + P], xw[:, 1 + c, 2 * j:2 * j + 2, :].rearrange("p h q -> p (h q)"),
                                 b_tok[:, c, g, :], c == 0, c == 1)
                ins.then_inc(filled, 1)

            def ssd(c):
                def sums(g):
                    for half in range(2):
                        b = open_bank(f"ac{c}{g}{half}")
                        for j in range(4):
                            h = HPG * g + 4 * half + j
                            for m in range(2):
                                ins = mm(b[64 * m:64 * m + 64, P * j:P * j + P], ex[:, h, :],
                                         acT[:, CHUNK * c:CHUNK * c + CHUNK], True, True)
                        ins.then_inc(filled, 1)

                sums(0)
                for g in range(GROUPS):
                    if g + 1 < GROUPS:
                        sums(g + 1)
                    i = GROUPS * c + g
                    if c == 1:
                        in_slot(6, g)
                    b = open_bank(f"y{c}{g}")
                    pe.wait_ge(S["m_ready"], i + 1)
                    if c == 1:
                        pe.wait_ge(S["cdec_ready"], g + 1)
                    for h in range(HPG):
                        out = b[64 * (h % 2):64 * (h % 2) + 64, P * (h // 2):P * (h // 2) + P]
                        ins = mm(out, xd[:, c, HPG * g + h, :], m_dec[i % 2][:, h, :], True, c == 0)
                        if c == 1:
                            ins = mm(out, s0T[:, HD * (HPG * g + h):HD * (HPG * g + h) + HD], c_dec[g % 2][:, h, :], False, True)
                    ins.then_inc(filled, 1)

            pe.wait_ge(S["ex_set"], 1)
            ssd(0)
            ssd(1)
            in_groups(7, 1)
            in_groups(8, 1)
            def project(g0, k_tiles, x_of, tiles0, first=0, end=8, ready=None):
                per = 16 // k_tiles
                for t in range(first, end):
                    c, m = t // per, t % per
                    s, n = c % 4, tiles0 + t
                    if m == 0:
                        pe.wait_ge(landed[s], 16 * (g0 + c // 4) + 16)
                    if n < 10:
                        pe.wait_ge(S["acc_emptied"], 72 + n - 1)
                    else:
                        pe.wait_ge(S["acc2_emptied"], n - 9)
                    for k in range(k_tiles):
                        if t == 0 and ready:
                            pe.wait_ge(ready, k + 1)
                        width = SLOT // k_tiles
                        w = stream[s][:, width * k + P * m:width * k + P * m + P]
                        ins = mm(ps[n % 2][:, 0:NT], w, x_of(k), k == 0, k == k_tiles - 1)
                    ins.then_inc(S["acc_ready"], 1)

            pe.wait_ge(S["gated_ready"], 1)
            project(9, KT, lambda k: plain[:, GATE + k, :], 0, 0, 5)
            pe.wait_ge(S["ysq_ready"], 1)
            for g in range(GROUPS):
                sum_squares(f"gn{g}", lambda k: plain[:, Z + 4 * g + k, :], 4, None, False)
            project(9, KT, lambda k: plain[:, GATE + k, :], 0, 5, 8)
            project(10, 16, lambda k: yT[:, k, :], 8, ready=S["y_final"])
            project(12, KT, lambda k: plain[:, GA + k, :], 16, ready=S["merged_ready"])
            sum_squares("ss1", lambda k: conv[:, k, :], KT, S["x1_sq"], True)

            def turn_rows(w, src):
                for t, n in enumerate(ROWS):
                    for h in range(2):
                        b = open_bank(f"{w}{t}{h}")
                        for j in range(4):
                            ins = turn(b[0:n, P * j:P * j + P], src[:, 4 * h + j, P * t:P * t + n], P)
                        ins.then_inc(filled, 1)

            turn_rows("x1_", xT)
            pe.wait_ge(S["u2_ready"], 1)
            pe.wait_ge(S["router_loaded"], 32)
            b = open_bank("logits")
            for t, n in enumerate(ROWS):
                for k in range(KT):
                    ins = mm(b[0:n, E * t:E * t + E], xnT[:, k, P * t:P * t + n], w_router[:, k, :], k == 0, k == KT - 1)
            ins.then_inc(filled, 1)
            turn_rows("u", xnT)
            pe.wait_ge(S["mark_ready"], 3)
            b = open_bank("rank")
            mm(b[:, 0:E], before[:, :], mark[:, 0, :], True, True)
            mm(b[:, E:2 * E], ones[:, :], mark[:, 0, :], True, False)
            mm(b[:, E:2 * E], before[:, :], mark[:, 1, :], False, True)
            mm(b[0:TS, 2 * E:3 * E], ones[:, 0:TS], mark[:, 0, :], True, False)
            mm(b[0:TS, 2 * E:3 * E], ones[:, 0:TS], mark[:, 1, :], False, False)
            mm(b[0:TS, 2 * E:3 * E], before[0:TS, 0:TS], mark[0:TS, 2, :], False, True)
            mm(b[:, 3 * E:4 * E], ones[:, :], mark[:, 0, :], True, False)
            mm(b[:, 3 * E:4 * E], ones[:, :], mark[:, 1, :], False, False)
            mm(b[:, 3 * E:4 * E], ones[0:TS, :], mark[0:TS, 2, :], False, True).then_inc(filled, 1)
            pe.wait_ge(S["passes_ready"], 1)
            n_passes = pe.value_load(passes[0:1, 0:1], min_val=1, max_val=MAXP)
            pe.wait_ge(emptied["s"], sum(w == "s" for _, w in uses))
            pe.wait_ge(emptied["v"], sum(w == "v" for _, w in uses))
            pe.wait_ge(S["bias_loaded"], 32)

            def gather(j):
                pe.wait_ge(S["pick_ready"], j + 1)
                for t, n in enumerate(ROWS):
                    for h in range(2):
                        ins = mm(p_xg[SLOTS * h:SLOTS * h + SLOTS, :], pick[0:n, t, :],
                                 u_tok[0:n, t, 512 * h:512 * h + 512], t == 0, t == 2)
                ins.then_inc(S["xg_filled"], 1)
                pe.wait_ge(S["xg_ready"], j + 1)
                for c in range(4):
                    ins = turn(p_xt[:, P * c:P * c + P], xg[:, P * c:P * c + P], P)
                ins.then_inc(S["xt_filled"], 1)

            with pe.Fori(0, n_passes) as p:
                gather((E + 1) * p)
                with pe.Fori(0, E) as e:
                    i = E * p + e
                    pe.wait_ge(S["xt_ready"], (E + 1) * p + e + 1)
                    pe.wait_ge(S["pick_e_ready"], (E + 1) * p + e + 1)
                    pe.wait_ge(S["gu_emptied"], i)
                    for n in range(4):
                        mm(p_gu[n // 2][SLOTS * (n % 2):SLOTS * (n % 2) + SLOTS, :], pick_e, e_bias[:, 512 * n:512 * n + 512], True, False)
                    for k in range(KT):
                        pe.wait_ge(w_landed[k], 16 * i + 16)
                        for n in range(4):
                            ins = mm(p_gu[n // 2][SLOTS * (n % 2):SLOTS * (n % 2) + SLOTS, :],
                                     xt[:, k % 4, SLOTS * (k // 4):SLOTS * (k // 4) + SLOTS],
                                     stream[k][:, 512 * n:512 * n + 512], False, k == KT - 1)
                        ins.then_inc(S["w_used"], 1)
                    gather((E + 1) * p + e + 1)
                    for h in range(2):
                        mm(p_y[SLOTS * h:SLOTS * h + SLOTS, :], pick_e, e_bias[:, 2 * D + 512 * h:2 * D + 512 * h + 512], True, False)
                    pe.wait_ge(S["ha_ready"], i + 1)
                    for c in range(4):
                        ins = turn(p_ht[:, P * c:P * c + P], ha[:, P * c:P * c + P], P)
                    ins.then_inc(S["ht_filled"], 1)
                    pe.wait_ge(S["ht_ready"], i + 1)
                    for k in range(KT):
                        if k % 2 == 0:
                            pe.wait_ge(w_landed[KT + k // 2], 16 * i + 16)
                        for h in range(2):
                            ins = mm(p_y[SLOTS * h:SLOTS * h + SLOTS, :],
                                     ht[:, k % 4, SLOTS * (k // 4):SLOTS * (k // 4) + SLOTS],
                                     stream[KT + k // 2][:, D * (k % 2) + 512 * h:D * (k % 2) + 512 * h + 512], False, k == KT - 1)
                        if k % 2:
                            ins.then_inc(S["w_used"], 1)

        @block.vector
        def _(dve):
            link = linker(dve, dve_step)
            V = nc.vector

            def done(name, ins):
                ins.then_inc(S[name], 1)

            V.memset(cin[:, :, 0:HIST], 0.0)
            dve.wait_ge(S["dskip_loaded"], 16)
            done("dskip_spread", V.tensor_copy(rows_b[96:112, :].rearrange("t (h j) -> t h j", h=2),
                                               dsk[96:112, :].unsqueeze(2).to_broadcast([16, 2, HD])))
            dve.wait_ge(S["consts_set"], 1)
            done("ex_set", V.tensor_copy(ex, ident[0:E, 0:E].unsqueeze(2).to_broadcast([E, E, HD])))
            b = take_bank(dve, "vec")
            V.tensor_copy(cvec[:, :, 0:24], b[:, 0:120].rearrange("p (j t) -> p j t", j=5))
            V.tensor_copy(cvec[:, :, 24:32], b[:, 128:168].rearrange("p (j t) -> p j t", j=5))
            V.tensor_copy(vec[:, 0:72], b[:, 168:240]).then_inc(emptied["v"], 1)
            dve.wait_ge(emptied["v"], 1)
            V.tensor_scalar(lt[4], lam, -1.0, 0.0, ALU.mult, ALU.max)
            link(V.tensor_scalar(lt[1], lam, -1.0, None, ALU.mult))
            done("lam_abs", V.tensor_tensor(lt[1], lt[1], lam, ALU.max))

            def log1p(e, s, s2, p):
                link(V.tensor_scalar(p, e, 2.0, None, ALU.add))
                link(V.reciprocal(p, p))
                link(V.tensor_tensor(s, e, p, ALU.mult))
                link(V.tensor_tensor(s2, s, s, ALU.mult))
                link(V.tensor_scalar(p, s2, 1.0 / 15, None, ALU.mult))
                for n in (13, 11, 9, 7, 5, 3):
                    link(V.scalar_tensor_tensor(out=p, in0=p, scalar=1.0 / n, in1=s2, op0=ALU.add, op1=ALU.mult))
                link(V.scalar_tensor_tensor(out=p, in0=p, scalar=1.0, in1=s, op0=ALU.add, op1=ALU.mult))

            for q in range(2):
                b = take_bank(dve, f"hist{q}")
                V.tensor_copy(cin[:, 16 * q:16 * q + 16, S_IN:S_IN + HIST * TS].rearrange("p t (j b) -> p t j b", j=HIST),
                              b[:, 0:384].rearrange("p (t b j) -> p t j b", b=TS, j=HIST)).then_inc(emptied["v"], 1)
            b = take_bank(dve, "h0")
            V.tensor_copy(h0T, b[:, 0:64].rearrange("p (t b) -> p t b", b=TS)).then_inc(emptied["v"], 1)
            for k in range(KT):
                dve.wait_ge(emptied["s"], k + 1)
                done("squares_ready", V.tensor_tensor(sq[:, k, :], xT[:, k, :], xT[:, k, :], ALU.mult))
            dve.wait_ge(S["rms_ready"], 1)
            link(V.reciprocal(rstd[:, 0, :], rstd[:, 0, :]))
            for k in range(KT):
                ins = V.scalar_tensor_tensor(out=xnT[:, k, :], in0=xT[:, k, :], scalar=n_mix[:, k:k + 1],
                                             in1=rstd[:, 0, :], op0=ALU.mult, op1=ALU.mult)
            done("xn_ready", ins)
            dve.wait_ge(S["lam_exp"], 2)
            log1p(lt[1], lt[2], lt[3], lt[0])
            link(V.scalar_tensor_tensor(out=lt[0], in0=lt[0], scalar=2.0, in1=lt[4], op0=ALU.mult, op1=ALU.add))
            V.tensor_scalar(sp4, lt[0], 4.0, None, ALU.mult)
            V.tensor_scalar(sp8n, lt[0], -8.0, None, ALU.mult)
            link(V.tensor_scalar(a_neg, a_neg, -1.0, None, ALU.mult))

            steps = [0]

            def convolve(t):
                dve.wait_ge(S["acc_emptied"], t + 1)
                o = conv[:, t, 0:TP]
                V.tensor_scalar(o, cin[:, t, 0:TP], cvec[:, 0, t:t + 1], cvec[:, 4, t:t + 1], ALU.mult, ALU.add).then_inc(S["conv_step"], 1)
                steps[0] += 1
                for j in range(1, CW):
                    dve.wait_ge(S["conv_step"], steps[0])
                    V.scalar_tensor_tensor(out=o, in0=cin[:, t, j:j + TP], scalar=cvec[:, j, t:t + 1], in1=o,
                                           op0=ALU.mult, op1=ALU.add).then_inc(S["conv_step"], 1)
                    steps[0] += 1

            def convolve_samples(t0, n):
                o = conv[:, t0:t0 + n, TP:NT]
                tmp = tmp_s[:, 0:n * TS].rearrange("p (t b) -> p t b", b=TS)

                def tap(j):
                    return cvec[:, j, t0:t0 + n].unsqueeze(2).to_broadcast([P, n, TS])
                link(V.tensor_tensor(o, cin[:, t0:t0 + n, S_IN:S_IN + TS], tap(0), ALU.mult))
                for j in range(1, CW):
                    link(V.tensor_tensor(tmp, cin[:, t0:t0 + n, S_IN + TS * j:S_IN + TS * j + TS], tap(j), ALU.mult))
                    link(V.tensor_tensor(o, o, tmp, ALU.add))
                return V.tensor_tensor(o, o, tap(CW), ALU.add)

            for t in range(LX):
                convolve(t)
            done("conv_done", convolve_samples(0, LX))
            z, e, s, s2, p, mz = dtw[0:6]
            b = take_bank(dve, "dt")
            V.tensor_scalar(z, b[0:HEADS, 0:NT], dt_b, None, ALU.add).then_inc(emptied["v"], 1)
            dve.wait_ge(emptied["v"], nth["dt"] + 1)
            link(V.tensor_scalar(mz, z, 0.0, None, ALU.max))
            link(V.tensor_scalar(e, z, -1.0, None, ALU.mult))
            done("dt_z", V.tensor_tensor(e, e, z, ALU.max))
            dve.wait_ge(S["dt_exp"], 1)
            log1p(e, s, s2, p)
            link(V.scalar_tensor_tensor(out=dtT, in0=p, scalar=2.0, in1=mz, op0=ALU.mult, op1=ALU.add))
            link(V.tensor_scalar(daT, dtT, a_neg, None, ALU.mult))
            for c in range(2):
                w = slice(CHUNK * c, CHUNK * c + CHUNK)
                link(V.tensor_tensor_scan(acT[:, w], ones[0:HEADS, 0:CHUNK], daT[:, w], 0.0, ALU.mult, ALU.add))
            link(V.tensor_copy(acT[:, TP:NT], daT[:, TP:NT]))
            for c in range(2):
                last_c = CHUNK * c + CHUNK - 1
                ins = V.tensor_scalar(diag[:, HEADS * c:HEADS * c + HEADS], ident[0:HEADS, 0:HEADS], acT[:, last_c:last_c + 1], None, ALU.mult)
            done("diag_ready", ins)
            b = take_bank(dve, "tok")
            V.tensor_copy(tok.rearrange("p w h -> p (w h)"), b[:, 0:128])
            V.tensor_copy(last.rearrange("p c h -> p (c h)"), b[:, 128:192]).then_inc(emptied["v"], 1)
            dve.wait_ge(emptied["v"], nth["tok"] + 1)
            V.tensor_tensor(wdec[:, 2, :], last[:, 1, :], tok[:, 3, :], ALU.subtract)
            link(V.tensor_tensor(wdec[:, 0, :], last[:, 0, :], tok[:, 2, :], ALU.subtract))
            done("wdec_in", V.tensor_tensor(wdec[:, 1, :], wdec[:, 0, :], last[:, 1, :], ALU.add))
            for t in range(LX, NCONV):
                convolve(t)
            done("conv_done", convolve_samples(LX, KT))
            dve.wait_ge(S["conv_done"], 2)
            dve.wait_ge(filled, index["ho7"] + 1)
            for c in range(2):
                for g in range(GROUPS):
                    b = take_bank(dve, f"xs{c}{g}")
                    hs = slice(HPG * g, HPG * g + HPG)
                    V.tensor_tensor(xd[:, c, hs, :], b[:, :].rearrange("p (h q) -> p h q", q=HD),
                                    tok[:, c, hs].unsqueeze(2).to_broadcast([P, HPG, HD]), ALU.mult).then_inc(emptied["v"], 1)
            b = take_bank(dve, "smp")
            V.tensor_copy(dx.rearrange("p t w -> p (t w)"), b[:, 0:256]).then_inc(emptied["v"], 1)
            dve.wait_ge(emptied["v"], nth["smp"] + 1)
            xs_s = conv[:, XS:XS + 16, TP:NT]
            done("smp_ready", V.tensor_tensor(xds, xs_s, dx[:, :, 0:TS], ALU.mult))
            dve.wait_ge(S["u_ready"], 1)
            lx = conv[:, LX:LX + KT, :]
            link(V.tensor_tensor(lx, lx, lru[1], ALU.mult))
            dve.wait_ge(S["sqrt_done"], 1)
            link(V.scalar_tensor_tensor(out=lru[0], in0=lru[2], scalar=1.0, in1=lru[0], op0=ALU.add, op1=ALU.mult))
            link(V.tensor_tensor(lru[0], lru[0], lx, ALU.mult))
            link(V.tensor_tensor(tmp_s[:, 0:64].rearrange("p (t b) -> p t b", b=TS), h0T, lru[2][:, :, TP:NT], ALU.mult))
            V.tensor_tensor(lx[:, :, TP:NT], tmp_s[:, 0:64].rearrange("p (t b) -> p t b", b=TS), lru[0][:, :, TP:NT], ALU.add)
            for t in range(KT):
                ins = V.tensor_tensor_scan(conv[:, LX + t, 0:TP], lru[2][:, t, 0:TP], lru[0][:, t, 0:TP], 0.0, ALU.mult, ALU.add)
            done("h_ready", ins)
            dve.wait_ge(S["h_ready"], 1)
            dve.wait_ge(S["sqrt_done"], 2)
            gate = plain[:, GATE:GATE + KT, :]
            done("gated_ready", V.tensor_tensor(gate, gate, lx, ALU.mult))
            dve.wait_ge(S["wdec_exp"], 1)
            dve.wait_ge(emptied["v"], nth["xs13"] + 1)
            for g in range(GROUPS):
                hs = slice(HPG * g, HPG * g + HPG)
                if g:
                    dve.wait_ge(filled, index[f"fs{g - 1}"] + 1)
                for w, c in ((0, 0), (1, 0), (2, 1)):
                    ins = V.tensor_tensor(xw[:, w], xd[:, c, hs, :], wdec[:, w, hs].unsqueeze(2).to_broadcast([P, HPG, HD]), ALU.mult)
                done("xw_ready", ins)

            def ssd(c):
                def differences(g):
                    i = GROUPS * c + g
                    if c == 1:
                        dve.wait_ge(S["cdec_exp"], g + 1)
                    if i:
                        j = i - 2
                        dve.wait_ge(filled, index[f"y{j // GROUPS}{j % GROUPS}" if j >= 0 else "fs3"] + 1)
                    for h in range(HPG):
                        b = take_bank(dve, f"ac{c}{g}{h // 4}")
                        ins = V.scalar_tensor_tensor(out=m_dec[i % 2][:, h, :], in0=b[:, P * (h % 4):P * (h % 4) + P],
                                                     scalar=tok[:, 2 + c, HPG * g + h:HPG * g + h + 1], in1=cmask[:, :],
                                                     op0=ALU.subtract, op1=ALU.add)
                        if h % 4 == 3:
                            ins.then_inc(emptied["v"], 1)

                differences(0)
                for g in range(GROUPS):
                    i = GROUPS * c + g
                    if g + 1 < GROUPS:
                        differences(g + 1)
                    if c == 1:
                        cw = conv[:, CT + g, CHUNK:TP].unsqueeze(1).to_broadcast([P, HPG, CHUNK])
                        done("cdec_ready", V.tensor_tensor(c_dec[g % 2], c_dec[g % 2], cw, ALU.mult))
                    dve.wait_ge(S["dec_exp"], i + 1)
                    if i == 0:
                        dve.wait_ge(emptied["s"], nth["cb1"] + 1)
                    done("m_ready", V.tensor_tensor(m_dec[i % 2], m_dec[i % 2], cb[:, c, g, :].unsqueeze(1).to_broadcast([P, HPG, CHUNK]), ALU.mult))
                    b = take_bank(dve, f"y{c}{g}")
                    for j in range(4):
                        t = 4 * g + j
                        w = slice(CHUNK * c, CHUNK * c + CHUNK)
                        ins = V.scalar_tensor_tensor(out=yT[:, t, w], in0=conv[:, XS + t, w], scalar=dskip[:, t:t + 1],
                                                     in1=b[:, P * j:P * j + P], op0=ALU.mult, op1=ALU.add)
                    ins.then_inc(emptied["v"], 1)

            ssd(0)
            ssd(1)
            dve.wait_ge(S["da_exp"], 1)
            for i in range(TS):
                dve.wait_ge(st_loaded[i % 3], 16 * (i // 3) + 16)
                dve.wait_ge(S["outer_ready"], i + 1)
                s_i, o_i = st[i % 3], outer[i % 2]
                for t in range(16):
                    ins = V.scalar_tensor_tensor(out=s_i[:, t, :], in0=s_i[:, t, :], scalar=dx[:, t, TS + i:TS + i + 1],
                                                 in1=o_i[:, t, :], op0=ALU.mult, op1=ALU.add)
                done("st_done", ins)
                dve.wait_ge(S["st_done"], i + 1)
                for t in range(16):
                    ins = V.tensor_tensor_reduce(o_i[:, t, :], s_i[:, t, :], bc_all[i % 3][:, 1, t // 4, :], 1.0, 0.0, ALU.mult, ALU.add,
                                                 ys[:, t, i:i + 1])
                done("bc_used", ins)
            dve.wait_ge(S["bc_used"], TS)
            link(V.tensor_tensor(xds, xs_s, dskip.unsqueeze(2).to_broadcast([P, 16, TS]), ALU.mult))
            link(V.tensor_tensor(yT[:, :, TP:NT], xds, ys, ALU.add))
            dve.wait_ge(S["z_silu"], 1)
            done("yz_ready", V.tensor_tensor(yT, yT, plain[:, Z:Z + 16, :], ALU.mult))
            dve.wait_ge(S["yrms_ready"], 1)
            for g in range(GROUPS):
                link(V.reciprocal(rstd[:, g, :], rstd[:, g, :]))
                for t in range(4 * g, 4 * g + 4):
                    done("y_final", V.scalar_tensor_tensor(out=yT[:, t, :], in0=yT[:, t, :], scalar=ssd_norm[:, t:t + 1],
                                                           in1=rstd[:, g, :], op0=ALU.mult, op1=ALU.mult))
            dve.wait_ge(S["ga_ready"], 1)
            dve.wait_ge(S["acc_emptied"], 80)
            link(V.tensor_tensor(plain[:, GA:GA + KT, :], plain[:, GA:GA + KT, :], xnT[:, :, :], ALU.mult))
            for t in range(KT):
                dve.wait_ge(S["acc_ready"], 80 + t + 1)
                V.tensor_tensor(plain[:, GB + t, :], plain[:, GB + t, :], ps[t % 2][:, 0:NT], ALU.mult).then_inc(S["acc2_emptied"], 1)
                dve.wait_ge(S["acc2_emptied"], t + 1)
                done("merged_ready", V.tensor_tensor(plain[:, GA + t, :], plain[:, GA + t, :], plain[:, GB + t, :], ALU.add))
            for t in range(KT):
                dve.wait_ge(S["acc_ready"], 88 + t + 1)
                V.tensor_tensor(xT[:, t, :], xT[:, t, :], ps[t % 2][:, 0:NT], ALU.add).then_inc(S["acc2_emptied"], 1)
                dve.wait_ge(S["acc2_emptied"], 8 + t + 1)
                done("x1_sq", V.tensor_tensor(conv[:, t, :], xT[:, t, :], xT[:, t, :], ALU.mult))
            dve.wait_ge(S["x1rms_ready"], 1)
            link(V.reciprocal(rstd[:, 0, :], rstd[:, 0, :]))
            for k in range(KT):
                ins = V.scalar_tensor_tensor(out=xnT[:, k, :], in0=xT[:, k, :], scalar=n_ffn[:, k:k + 1],
                                             in1=rstd[:, 0, :], op0=ALU.mult, op1=ALU.mult)
            done("u2_ready", ins)
            b = take_bank(dve, "logits")
            dve.wait_ge(S["st_stored"], 16 * TS)
            dve.wait_ge(S["router_loaded"], 32)
            for t, n in enumerate(ROWS):
                ins = V.tensor_tensor(logits[0:n, t, :], b[0:n, E * t:E * t + E], b_router[0:n, :], ALU.add)
            ins.then_inc(emptied["v"], 1)
            dve.wait_ge(emptied["v"], nth["logits"] + 1)
            for t, n in enumerate(ROWS):
                link(V.max(top[0:n, t, :], logits[0:n, t, :]))
                done("gates_in", V.tensor_scalar(gates[0:n, t, :], top[0:n, t, 0:TOPK], top[0:n, t, 0:1], None, ALU.subtract))
                link(V.max_index(top_i[0:n, t, :], top[0:n, t, :], logits[0:n, t, :]))
                link(V.tensor_copy(top_f[0:n, t, :], top_i[0:n, t, :]))
                for k in range(TOPK):
                    ins = V.tensor_scalar(hot[0:n, t, k, :], slot_no[0:n, 0:E], top_f[0:n, t, k:k + 1], None, ALU.is_equal)
                link(ins)
                V.tensor_tensor(mark[0:n, t, :], hot[0:n, t, 0, :], hot[0:n, t, 1, :], ALU.add)
                link(V.tensor_tensor(tmp_e[0:n, t, :], hot[0:n, t, 2, :], hot[0:n, t, 3, :], ALU.add))
                done("mark_ready", V.tensor_tensor(mark[0:n, t, :], mark[0:n, t, :], tmp_e[0:n, t, :], ALU.add))
            dve.wait_ge(S["mark_ready"], 3)
            b = take_bank(dve, "rank")
            for t, n in enumerate(ROWS):
                V.tensor_copy(rank[0:n, t, :], b[0:n, E * t:E * t + E])
            V.tensor_copy(total, b[:, 3 * E:4 * E]).then_inc(emptied["v"], 1)
            dve.wait_ge(emptied["v"], nth["rank"] + 1)
            link(V.tensor_reduce(most, total, AXX, ALU.max))
            link(V.tensor_scalar(passes_f, most, float(SLOTS), 1.0, ALU.is_gt, ALU.add))
            for j in range(2, MAXP):
                link(V.scalar_tensor_tensor(out=passes_f, in0=most, scalar=float(SLOTS * j), in1=passes_f, op0=ALU.is_gt, op1=ALU.add))
            done("passes_ready", V.tensor_copy(passes, passes_f))
            link(V.memset(slot_of[:, :, E:E + 1], -1.0))
            for t, n in enumerate(ROWS):
                r, m = rank[0:n, t, :], mark[0:n, t, :]
                link(V.scalar_tensor_tensor(out=slot_of[0:n, t, 0:E], in0=r, scalar=1.0, in1=m, op0=ALU.add, op1=ALU.mult))
                link(V.tensor_scalar(slot_of[0:n, t, 0:E], slot_of[0:n, t, 0:E], -1.0, None, ALU.add))
                for k in range(TOPK):
                    ins = V.tensor_tensor_reduce(hot[0:n, t, k, :], hot[0:n, t, k, :], r, 1.0, 0.0, ALU.mult, ALU.add,
                                                 picked[0:n, t, k:k + 1])
                link(ins)
                q, s = pass_of[0:n, t, :], picked[0:n, t, :]
                link(V.tensor_scalar(q, s, float(SLOTS), None, ALU.is_ge))
                for j in range(2, MAXP):
                    link(V.scalar_tensor_tensor(out=q, in0=s, scalar=float(SLOTS * j), in1=q, op0=ALU.is_ge, op1=ALU.add))
                link(V.scalar_tensor_tensor(out=s, in0=q, scalar=-float(SLOTS), in1=s, op0=ALU.mult, op1=ALU.add))
                link(V.scalar_tensor_tensor(out=s, in0=top_f[0:n, t, 0:TOPK], scalar=float(SLOTS), in1=s, op0=ALU.mult, op1=ALU.add))
                done("picked_ready", V.tensor_copy(picked_i[0:n, t, :], s))
            dve.wait_ge(S["gates_exp"], 1)
            for t, n in enumerate(ROWS):
                link(V.tensor_reduce(ssq[0:n, t:t + 1], gates[0:n, t, :], AXX, ALU.add))
                link(V.reciprocal(ssq[0:n, t:t + 1], ssq[0:n, t:t + 1]))
                link(V.tensor_scalar(gates[0:n, t, :], gates[0:n, t, :], ssq[0:n, t:t + 1], None, ALU.mult))
            n_passes = dve.value_load(passes[0:1, 0:1], min_val=1, max_val=MAXP)
            dve.wait_ge(filled, len(uses))

            def pick_tokens(p, e):
                for t, n in enumerate(ROWS):
                    ins = V.tensor_scalar(pick[0:n, t, :], slot_no[0:n, bass.ds(SLOTS * p, SLOTS)],
                                          slot_of[0:n, t, bass.ds(e, 1)], None, ALU.is_equal)
                done("pick_ready", ins)

            def pick_expert(e):
                done("pick_e_ready", V.tensor_copy(pick_e, ident[0:E, bass.ds(e, 1)].to_broadcast([E, SLOTS])))

            with dve.Fori(0, n_passes) as p:
                pick_tokens(p, 0)
                pick_expert(0)
                with dve.Fori(0, E) as e:
                    i = E * p + e
                    dve.wait_ge(S["xg_filled"], (E + 1) * p + e + 1)
                    pick_tokens(p, e + 1)
                    dve.wait_ge(S["w_used"], NSLOT * i + KT)
                    V.tensor_scalar(g1, p_gu[0][:, :], 7.0, None, ALU.min).then_inc(S["g1_ready"], 1)
                    V.tensor_scalar(u1, p_gu[1][:, :], 7.0, -7.0, ALU.min, ALU.max).then_inc(S["gu_emptied"], 1)
                    dve.wait_ge(S["gu_emptied"], i + 1)
                    V.scalar_tensor_tensor(out=u1, in0=u1, scalar=1.0, in1=g1, op0=ALU.add, op1=ALU.mult).then_inc(S["ug_ready"], 1)
                    dve.wait_ge(S["ug_ready"], i + 1)
                    dve.wait_ge(S["sg_ready"], i + 1)
                    V.tensor_tensor(ha, u1, sg, ALU.mult).then_inc(S["ha_ready"], 1)
                    dve.wait_ge(S["ht_filled"], i + 1)
                    pick_expert(e + 1)
                for t, n in enumerate(ROWS):
                    ins = V.scalar_tensor_tensor(out=gates_p[0:n, t, :], in0=pass_of[0:n, t, :], scalar=slot_no[0:n, bass.ds(p, 1)],
                                                 in1=gates[0:n, t, :], op0=ALU.is_equal, op1=ALU.mult)
                done("combined", ins)
                for t, n in enumerate(ROWS):
                    dve.wait_ge(rows_landed[t], 16 * TOPK * (p + 1))
                    for k in range(TOPK):
                        dve.wait_ge(S["combined"], (1 + 3 * (TOPK - 1)) * p + 1 + (TOPK - 1) * t + k)
                        ins = V.scalar_tensor_tensor(out=x1_tok[0:n, t, :], in0=rows_y[t][0:n, k, :], scalar=gates_p[0:n, t, k:k + 1],
                                                     in1=x1_tok[0:n, t, :], op0=ALU.mult, op1=ALU.add)
                        if k < TOPK - 1:
                            done("combined", ins)
                    done("x2_ready", ins)
            dve.wait_ge(S["final_loaded"], 16)
            for t, n in enumerate(ROWS):
                dve.wait_ge(S["x2rms_ready"], t + 1)
                link(V.reciprocal(ssq[0:n, t:t + 1], ssq[0:n, t:t + 1]))
                done("out_ready", V.scalar_tensor_tensor(out=x1_tok[0:n, t, :], in0=x1_tok[0:n, t, :], scalar=ssq[0:n, t:t + 1],
                                                         in1=n_final[0:n, :], op0=ALU.mult, op1=ALU.mult))


_INS = ['x_prompt', 'x_sample', 'state_lru_conv', 'state_lru_h', 'state_ssd_conv', 'state_ssd', 'norm_mix', 'w_in',
        'conv_lru_w', 'conv_lru_b', 'w_rg', 'b_rg', 'w_ig', 'b_ig', 'lam', 'w_proj_a', 'conv_ssd_w', 'conv_ssd_b',
        'dt_bias', 'a_log', 'd_skip', 'ssd_norm', 'w_proj_b', 'w_out', 'norm_ffn', 'w_router', 'b_router',
        'w_gate_up', 'b_gate_up', 'w_down', 'b_down', 'norm_final']
_CONV = 3072
_OUTS = [(1, TP, D), (TS, 1, D), (1, 1, HIST, D), (1, 1, D), (1, 1, HIST, _CONV), (1, 1, HEADS, HD, NS),
         (1, TS, HIST, D), (1, TS, D), (1, TS, HIST, _CONV), (1, TS, HEADS, HD, NS)]


def kernel(**inputs):
    import numpy as _np
    import concourse.bacc as _bacc
    from concourse import mybir as _mybir
    from concourse.bass_utils import run_bass_kernel_spmd as _run

    nc = _bacc.Bacc("TRN2", target_bir_lowering=False, num_devices=1)
    arrays, args = {}, {}
    for name in _INS:
        x = _np.ascontiguousarray(inputs[name])
        arrays[f"in_{name}"] = x
        args[name] = nc.dram_tensor(f"in_{name}", x.shape, _mybir.dt.from_np(x.dtype), kind="ExternalInput").ap()
    for i, shape in enumerate(_OUTS):
        args[f"out_{i}"] = nc.dram_tensor(f"out_{i}", shape, _mybir.dt.float32, kind="ExternalOutput").ap()
    build(nc, args)
    r = _run(nc, [arrays], core_ids=[0])
    return tuple(r.results[0][f"out_{i}"] for i in range(len(_OUTS)))
```

```python
from contextlib import ExitStack

import concourse.bass as bass
from concourse import mybir
from concourse.alu_op_type import AluOpType as ALU

ACT = mybir.ActivationFunctionType
F32 = mybir.dt.float32
U32 = mybir.dt.uint32
I32 = mybir.dt.int32
AXX = mybir.AxisListType.X

P = 128
D = 1024
KT = D // P
TP = 256
TS = 8
NT = TP + TS
CHUNK = 128
CW = 4
HIST = CW - 1
CIN = HIST + TP + CW * TS
S_IN = HIST + TP
HEADS, HD, GROUPS, NS = 32, 64, 4, 128
HPG = HEADS // GROUPS
E, TOPK, SLOTS = 32, 4, 64
MAXP = -(-NT // SLOTS)
EPS = 1e-6
NEG = -1e30
XS, BT, CT, LX = 0, 16, 20, 24
NCONV = 32
GATE, Z, GA, GB, NPLAIN = 0, 8, 24, 32, 40
W_COL = [4096, 5120, 6144, 0, 1024, 2048, 3072, 7200, 8224]
DT_COL = 7168
FILL = (0,), (1,), (2,), (3,), (4,), (5,), (6,), (7,)
SLOT = 2048
NSLOT = 12
MSLOT = 16
ROUND = 4


def build(nc, a):
    with ExitStack() as ctx:
        def sb(name, shape, dt=F32):
            return ctx.enter_context(nc.sbuf_tensor(name, shape, dt))

        def sem(name):
            return ctx.enter_context(nc.semaphore(name))

        ring = sb("ring", [P, NSLOT * SLOT])
        plain_t = sb("plain", [P, NPLAIN * NT])
        conv_t = sb("conv", [P, NCONV * NT])
        xT_t = sb("xT", [P, KT * NT])
        xnT_t = sb("xnT", [P, KT * NT])
        ident = sb("ident", [P, P])
        ones = sb("ones", [P, P])
        before = sb("before", [P, P])
        cmask = sb("cmask", [P, P])
        slot_no = sb("slot_no", [P, (MAXP + 1) * SLOTS])
        ex_t = sb("ex", [P, HEADS * HD])
        cvec = sb("cvec", [P, CW + 1, NCONV])
        vec = sb("vec", [P, 88])
        rstd_t = sb("rstd", [P, 4 * NT])
        small = sb("small", [P, 704])
        hv = sb("hv", [HEADS, 64])

        plain = plain_t[:, :].rearrange("p (t n) -> p t n", n=NT)
        conv = conv_t[:, :].rearrange("p (t n) -> p t n", n=NT)
        xT, xnT = (v[:, :].rearrange("p (k n) -> p k n", n=NT) for v in (xT_t, xnT_t))
        ex = ex_t[0:E, :].rearrange("p (h c) -> p h c", c=HD)
        stream = [ring[:, s * SLOT:(s + 1) * SLOT] for s in range(NSLOT)]

        stream += [ex_t[:, :], plain_t[:, GB * NT:GB * NT + SLOT], conv_t[:, 3 * D:3 * D + SLOT], xnT_t[:, 0:SLOT]]

        A0 = 4 * SLOT

        def arena(start, size):
            return ring[:, A0 + start:A0 + start + size]

        cin = arena(0, NCONV * CIN).rearrange("p (t n) -> p t n", n=CIN)
        T0 = NCONV * CIN
        sq = arena(T0, KT * NT).rearrange("p (t n) -> p t n", n=NT)
        lru = [arena(T0 + i * KT * NT, KT * NT).rearrange("p (t n) -> p t n", n=NT) for i in range(3)]
        x_rows = plain_t[:, 0:3 * D].rearrange("p (t d) -> p t d", d=D)
        hist_rows = plain_t[:, 3 * D:7 * D]
        rows_a = plain_t[:, 7 * D:7 * D + P]
        rows_b = plain_t[:, 7 * D + P:7 * D + 2 * P]
        h0_rows = plain_t[:, 7 * D + 2 * P:8 * D + 2 * P]
        gw = plain_t[:, GB * NT:GB * NT + 16 * P].rearrange("p (g t c) -> p g t c", g=2, t=KT)

        b_rg, b_ig, lam = vec[:, 0:8], vec[:, 8:16], vec[:, 16:24]
        ssd_norm, n_ffn, n_mix, dskip = vec[:, 24:40], vec[:, 40:48], vec[:, 48:56], vec[:, 56:72]
        sp4, sp8n = vec[:, 72:80], vec[:, 80:88]
        lt = [small[:, 8 * i:8 * i + 8] for i in range(5)]
        h0T = small[:, 64:128].rearrange("p (t b) -> p t b", b=TS)
        dsk = small[:, 128:130]
        dt_b, a_log, a_neg = hv[:, 0:1], hv[:, 1:2], hv[:, 2:3]

        xd = arena(0, 2 * 2048).rearrange("p (c h q) -> p c h q", c=2, h=HEADS)
        b_tok = arena(4096, 1024).rearrange("p (c g n) -> p c g n", c=2, g=GROUPS)
        s0T = arena(5120, 2048)
        fin_st = arena(7168, 1024).rearrange("p (r t n) -> p r t n", r=2, t=4)
        m_dec = [arena(o, 1024).rearrange("p (h q) -> p h q", h=HPG) for o in (8192, T0 + 5248)]
        yT = arena(T0, 16 * NT).rearrange("p (t n) -> p t n", n=NT)
        c_dec = [arena(o, 1024).rearrange("p (h q) -> p h q", h=HPG) for o in (T0 + 4224, 4096)]
        xw = [arena(o, 1536).rearrange("p (w h q) -> p w h q", w=3, h=HPG) for o in (T0 + 5248, T0)]
        cb = plain_t[:, GA * NT:GA * NT + 1024].rearrange("p (c g q) -> p c g q", c=2, g=GROUPS)
        hist_out = plain_t[:, Z * NT:Z * NT + 4096]
        h_out_t = plain_t[:, GB * NT:GB * NT + 1024]
        tok = small[:, 384:512].rearrange("p (w h) -> p w h", w=4)
        last = small[:, 512:576].rearrange("p (c h) -> p c h", c=2)
        wdec = small[:, 576:672].rearrange("p (w h) -> p w h", w=3)
        tmp_s = small[:, 192:384]
        dtw = [lru[i // 4][0:HEADS, i % 4 * 2, :] for i in range(8)]
        rstd = rstd_t[:, :].rearrange("p (w n) -> p w n", n=NT)
        dtT, acT, daT = rstd[0:HEADS, 1, :], rstd[0:HEADS, 2, :], rstd[0:HEADS, 3, :]
        diag = hv[:, 0:64]
        st = [v.rearrange("p (t n) -> p t n", n=NS)
              for v in (conv_t[:, LX * NT:LX * NT + 2048], arena(0, 2048), arena(2048, 2048), arena(T0 + 4224, 2048))]
        outer = [arena(o, 2048).rearrange("p (t n) -> p t n", n=NS) for o in (4096, 6144)]
        bc_rows = plain_t[:, GA * NT + 1024:GA * NT + 2048]
        bc_all = [v.rearrange("p (w g n) -> p w g n", w=2, g=GROUPS) for v in
                  (conv_t[:, BT * NT:BT * NT + 1024], conv_t[:, BT * NT + 1024:BT * NT + 2048], arena(8192, 1024))]
        dx = rstd[:, 0, 0:32 * TS].rearrange("p (t w) -> p t w", w=2 * TS)
        xds = small[:, 256:384].rearrange("p (t b) -> p t b", b=TS)
        ys = small[:, 0:128].rearrange("p (t b) -> p t b", b=TS)
        e_bias = plain_t[0:E, 0:3 * D]
        xg, g1, u1, sg, ha, y_out = (plain_t[:, 3 * D + 512 * i:3 * D + 512 * i + 512] for i in range(6))
        xt, ht = (plain_t[:, 6 * D + 512 * i:6 * D + 512 * i + 512].rearrange("p (c s) -> p c s", c=4) for i in range(2))
        pick = plain_t[:, 7 * D:7 * D + 3 * SLOTS].rearrange("p (t s) -> p t s", t=3)
        pick_e = plain_t[0:E, 7 * D + 192:7 * D + 256]
        n_final = plain_t[:, 7 * D + 256:8 * D + 256]
        u_tok = conv_t[:, 0:3 * D].rearrange("p (t d) -> p t d", t=3)
        rows_out = u_tok
        squares = ring[:, 0:3 * D].rearrange("p (t d) -> p t d", t=3)
        at = [6 * D]

        def scratch(*shape):
            size = 1
            for n in shape:
                size *= n
            v = conv_t[:, at[0]:at[0] + size]
            at[0] += size
            assert at[0] <= NCONV * NT
            if len(shape) == 1:
                return v
            names = "abc"[:len(shape)]
            return v.rearrange(f"p ({' '.join(names)}) -> p {' '.join(names)}", **dict(zip(names, shape)))

        logits, mark, rank = scratch(3, E), scratch(3, E), scratch(3, E)
        slot_of = scratch(3, E + 1)
        top, top_i, top_f, gates = scratch(3, 8), scratch(3, 8).bitcast(U32), scratch(3, 8), scratch(3, TOPK)
        hot = scratch(3, TOPK, E)
        total, tmp_e = scratch(E), scratch(3, E)
        gates_e = scratch(3, E)
        pg = rstd_t[:, 0:3 * P].rearrange("p (t s) -> p t s", t=3)
        pgt = rstd_t[:, 3 * P:3 * P + NT]
        most, passes_f, passes = scratch(1), scratch(1), scratch(1).bitcast(I32)
        ssq, ssq_h = scratch(3), scratch(3, 2)
        w_router = plain_t[:, 3 * D:3 * D + KT * E].rearrange("p (k e) -> p k e", k=KT)
        b_router = small[:, 672:704]
        ROWS = (P, P, TS)
        ac_dram = nc.dram_tensor("ac_dram", [HEADS, TP], F32, kind="Internal").ap()
        bc_dram = nc.dram_tensor("bc_dram", [TS, 2 * GROUPS * NS], F32, kind="Internal").ap()

        ps = [ctx.enter_context(nc.psum_tensor(f"bank{i}", [P, 512], F32)) for i in range(8)]

        uses = [(f"x{k}", "s") for k in range(KT)] + [("ss0", "s"), ("vec", "v")]
        uses += [("hist0", "v"), ("hist1", "v"), ("h0", "v"), ("dt", "v"), ("tok", "v")]
        uses += [(f"ho{q}", "s") for q in range(8)]
        uses += [(f"xs{c}{g}", "v") for c in range(2) for g in range(GROUPS)]
        uses += [(f"bt{c}", "s") for c in range(2)] + [(f"cb{c}", "s") for c in range(2)]
        uses += [("smp", "v"), ("bc0", "s"), ("bc1", "s")]
        uses += [(f"{r}{t}", "s") for t in range(KT) for r in ("rg", "ig")] + [(f"hl{q}", "s") for q in range(2)]
        for g in range(GROUPS):
            uses += [(f"s0{g}", "s"), (f"fs{g}", "s")]
        uses += [(f"y{c}{g}", "v") for c in range(2) for g in range(GROUPS)]
        uses += [(f"gn{g}", "s") for g in range(GROUPS)] + [("ss1", "s")]
        uses += [("logits", "v")]
        uses += [(f"u{t}{h}", "s") for t in range(3) for h in range(2)] + [("rank", "v")]
        index = {name: n for n, (name, _) in enumerate(uses)}
        assert len(index) == len(uses)
        nth = {name: sum(w == who for _, w in uses[:index[name]]) for name, who in uses}

        def bank(name):
            return ps[2 + index[name] % 6]

        filled, emptied = sem("psum_filled"), {"v": sem("psum_emptied_by_dve"), "s": sem("psum_emptied_by_act")}

        def open_bank(name):
            if index[name] >= 6:
                prev, who = uses[index[name] - 6]
                nc.tensor.wait_ge(emptied[who], nth[prev] + 1)
            return bank(name)

        def take_bank(eng, name):
            eng.wait_ge(filled, index[name] + 1)
            return bank(name)

        names = """a_ready ac_stored acc2_emptied acc_emptied acc_ready bc_stored bc_used bias_loaded cdec_exp
            cdec_ready comb_emptied comb_filled consts_set conv_done conv_step da_exp dec_exp dec_in diag_ready
            dskip_loaded dskip_spread dt_exp dt_z ex_set fin_filled fin_rms final_loaded fs_stored0 fs_stored1
            g1_ready ga_ready gated_ready gates_exp gates_in gates_loaded gates_zeroed gu_emptied h_ready
            ha_ready heads_loaded hist_loaded hist_stored hl_stored ht_filled ht_ready ident_set lam_abs lam_exp
            m_ready mark_ready merged_ready out_ready outer_ready passes_ready pg_filled pg_ready pgt_ready
            pick_e_ready pick_ready rms_in rms_ready router_loaded sg_ready silu_done smp_ready sq_sum sqrt_done
            squares_ready st_done u2_ready u_ready ug_ready vec_loaded w_used wdec_exp wdec_in x1_sq x1rms_ready
            x_loaded xg_filled xg_ready xn_ready xt_filled xt_ready xw_ready y_copied y_final y_stored
            yrms_ready ysq_ready yz_ready z_silu""".split()
        S = {name: sem(name) for name in names}
        st_loaded, st_stored = [sem(f"st_loaded{i}") for i in range(4)], [sem(f"st_stored{i}") for i in range(4)]
        m_spread, c_spread = [sem(f"m_spread{i}") for i in range(2)], [sem(f"c_spread{i}") for i in range(2)]
        bc_landed = [sem(f"bc_landed{i}") for i in range(3)]
        w_landed = [sem(f"w_landed{i}") for i in range(MSLOT)]
        p_comb = ps[6:8]
        p_rows = [ps[2 * t:2 * t + 2] for t in range(3)]
        p_gu, p_xg, p_xt, p_ht, p_y = ps[0:2], ps[2], ps[3], ps[4], ps[5]
        landed = [sem(f"stream_landed{i}") for i in range(4)]
        dve_step, pool_step = sem("dve_step"), sem("pool_step")

        def linker(eng, step):
            count = [0]

            def link(ins):
                count[0] += 1
                ins.then_inc(step, 1)
                eng.wait_ge(step, count[0])
            return link

        def mm(out, w, x, start, stop):
            return nc.tensor.matmul(out, w, x, start=start, stop=stop)

        block = ctx.enter_context(nc.Block())

        @block.sync
        def _(sp):
            sp.dma_start(x_rows[:, 0:2, :], a["x_prompt"][0].rearrange("(t p) d -> p t d", p=P)).then_inc(S["x_loaded"], 16)
            sp.dma_start(x_rows[0:TS, 2, :], a["x_sample"][:, 0, :]).then_inc(S["x_loaded"], 16)
            for name, r, n in (("lam", 56, 8), ("ssd_norm", 64, 16)):
                sp.dma_start(rows_b[r:r + n, :], a[name].rearrange("o (t c) -> (o t) c", c=P)).then_inc(S["vec_loaded"], 16)
            for name, r in (("b_rg", 40), ("b_ig", 48)):
                sp.dma_start(rows_b[r:r + 8, :].rearrange("t (h j) -> t h j", h=2),
                              a[name][0].rearrange("(t h) j -> t h j", h=2)).then_inc(S["vec_loaded"], 16)
            sp.dma_start(dsk[96:112, :], a["d_skip"][0].rearrange("(t h) -> t h", h=2)).then_inc(S["dskip_loaded"], 16)
            w_in = a["w_in"][0].rearrange("(k p) c -> p k c", p=P)

            def load_small():
                sp.dma_start(dt_b, a["dt_bias"][0].rearrange("(h o) -> h o", o=1)).then_inc(S["heads_loaded"], 16)
                sp.dma_start(a_log, a["a_log"][0].rearrange("(h o) -> h o", o=1)).then_inc(S["heads_loaded"], 16)
                sp.dma_start(hist_rows[0:24, 0:3072], a["state_ssd_conv"][0].rearrange("b j c -> (b j) c")).then_inc(S["hist_loaded"], 16)
                sp.dma_start(hist_rows[0:24, 3072:4096], a["state_lru_conv"][0].rearrange("b j c -> (b j) c")).then_inc(S["hist_loaded"], 16)
                sp.dma_start(h0_rows[0:TS, :], a["state_lru_h"][0]).then_inc(S["hist_loaded"], 16)
                sp.wait_ge(S["gates_zeroed"], 1)
                for w, name in enumerate(("w_rg", "w_ig")):
                    for h in range(2):
                        sp.dma_start(gw[64 * h:64 * h + 64, w, :, 64 * h:64 * h + 64],
                                      a[name][0].rearrange("(t h) i j -> h i t j", h=2)[h]).then_inc(S["gates_loaded"], 16)
                sp.dma_start(arena(T0 + 3 * KT * NT, KT * HEADS).rearrange("p (k c) -> p k c", k=KT),
                              a["w_in"][0].rearrange("(k p) c -> p k c", p=P)[:, :, DT_COL:DT_COL + HEADS]).then_inc(S["heads_loaded"], 16)

            free_at, tiles = [0] * 4, 0
            for col in W_COL:
                if col == W_COL[1]:
                    load_small()
                for s in range(4):
                    if free_at[s]:
                        sp.wait_ge(S["acc_ready"], free_at[s])
                    sp.dma_start(stream[s].rearrange("p (k c) -> p k c", k=KT),
                                 w_in[:, :, col + 256 * s:col + 256 * s + 256]).then_inc(landed[s], 16)
                    tiles += 2
                    free_at[s] = tiles
            w_gu, w_dn = a["w_gate_up"][0], a["w_down"][0]

            def load_chunk(e, c, slot):
                if c < KT:
                    src = w_gu[e, P * c:P * c + P, :]
                    dst = stream[slot]
                else:
                    src = w_dn[e, 2 * P * (c - KT):2 * P * (c - KT) + 2 * P, :].rearrange("(k p) n -> p k n", p=P)
                    dst = stream[slot].rearrange("p (k n) -> p k n", k=2)
                sp.dma_start(dst, src).then_inc(w_landed[slot], 16)

            for w, k in ((a["w_proj_a"], KT), (a["w_proj_b"], 2 * KT), (a["w_out"], KT)):
                width = SLOT // k
                wv = w[0].rearrange("(k p) c -> p k c", p=P)
                for c in range(D // width):
                    s = c % 4
                    sp.wait_ge(S["acc_ready"], free_at[s])
                    sp.dma_start(stream[s].rearrange("p (k c) -> p k c", k=k),
                                 wv[:, :, c * width:(c + 1) * width]).then_inc(landed[s], 16)
                    tiles += width // P
                    free_at[s] = tiles
                    if k == 2 * KT and c == 4:
                        sp.wait_ge(S["yz_ready"], GROUPS)
                        for n in range(4):
                            sp.wait_ge(st_stored[n], 32)
                        for chunk in (4, 5, 6, 7, 11):
                            load_chunk(0, chunk, chunk)
            sp.wait_ge(S["acc_ready"], 88)
            for c in (8, 9, 10):
                load_chunk(0, c, c)
            for c in range(4):
                sp.wait_ge(S["acc_ready"], free_at[c])
                load_chunk(0, c, c)
            load_chunk(1, 0, 12)
            sp.wait_ge(S["merged_ready"], KT)
            load_chunk(1, 1, 13)
            load_chunk(1, 2, 14)
            sp.wait_ge(filled, index["u21"] + 1)
            load_chunk(1, 3, 15)

            def load_expert(i, r, e, first=0):
                for c in range(first, NSLOT):
                    sp.wait_ge(S["w_used"], NSLOT * i + (c + 1 - MSLOT))
                    load_chunk(e, c, (NSLOT * r + c) % MSLOT)

            load_expert(1, 1, 1, first=4)
            load_expert(2, 2, 2)
            load_expert(3, 3, 3)
            with sp.Fori(1, E // ROUND) as q:
                for r in range(ROUND):
                    load_expert(ROUND * q + r, r, ROUND * q + r)
            sp.wait_ge(S["passes_ready"], 1)
            n_passes = sp.value_load(passes[0:1, 0:1], min_val=1, max_val=MAXP)
            with sp.If(n_passes > 1):
                with sp.Fori(1, n_passes) as p:
                    with sp.Fori(0, E // ROUND) as q:
                        for r in range(ROUND):
                            load_expert(E * p + ROUND * q + r, r, ROUND * q + r)
            for t in range(2):
                sp.wait_ge(S["out_ready"], 2 * t + 2)
                sp.dma_start(a["out_0"][0, P * t:P * t + P, :], rows_out[:, t, :]).then_inc(S["y_stored"], 16)
            sp.wait_ge(S["out_ready"], 6)
            sp.dma_start(a["out_1"][:, 0, :], rows_out[0:TS, 2, :]).then_inc(S["y_stored"], 16)
            sp.wait_ge(S["y_stored"], 48)

        @block.gpsimd
        def _(pool):
            link = linker(pool, pool_step)
            nc.gpsimd.memset(ones[:, :], 1.0)
            link(nc.gpsimd.memset(ident[:, :], 0.0))
            nc.gpsimd.affine_select(out=ident[:, :], in_=ident[:, :], compare_op=ALU.not_equal, fill=1.0,
                                    base=0, pattern=[[-1, P]], channel_multiplier=1).then_inc(S["ident_set"], 1)
            nc.gpsimd.memset(gw, 0.0).then_inc(S["gates_zeroed"], 1)
            nc.gpsimd.memset(cmask[:, :], 0.0)
            link(nc.gpsimd.memset(before[:, :], 1.0))
            nc.gpsimd.affine_select(out=cmask[:, :], in_=cmask[:, :], compare_op=ALU.is_ge, fill=NEG,
                                    base=0, pattern=[[1, P]], channel_multiplier=-1)
            nc.gpsimd.affine_select(out=before[:, :], in_=before[:, :], compare_op=ALU.is_gt, fill=0.0,
                                    base=0, pattern=[[1, P]], channel_multiplier=-1)
            nc.gpsimd.iota(slot_no[:, :], pattern=[[1, (MAXP + 1) * SLOTS]], base=0, channel_multiplier=0,
                           allow_small_or_imprecise_dtypes=True).then_inc(S["consts_set"], 1)
            def states(name, i):
                return a[name][0, i].rearrange("(t h) q n -> (h q) t n", h=2)

            def load_state(i):
                nc.gpsimd.dma_start(st[i % 4], states("state_ssd", i)).then_inc(st_loaded[i % 4], 16)

            def outer_product(i):
                pool.wait_ge(bc_landed[i % 3], 16 * (i // 3) + 16)
                if i > 1:
                    pool.wait_ge(S["bc_used"], i - 1)
                nc.gpsimd.tensor_tensor(
                    outer[i % 2].rearrange("p (g t) n -> p g t n", g=GROUPS),
                    bc_all[i % 3][:, 0].unsqueeze(2).to_broadcast([P, GROUPS, 4, NS]),
                    xds[:, :, i].rearrange("p (g t) -> p g t", g=GROUPS).unsqueeze(3).to_broadcast([P, GROUPS, 4, NS]),
                    ALU.mult).then_inc(S["outer_ready"], 1)

            pool.wait_ge(S["diag_ready"], 1)
            nc.gpsimd.dma_start(ac_dram[:, :], acT[:, 0:TP]).then_inc(S["ac_stored"], 16)

            def spread(dst, c, g, landed):
                nc.gpsimd.dma_start(dst, ac_dram[HPG * g:HPG * g + HPG, CHUNK * c:CHUNK * c + CHUNK].unsqueeze(0)
                                    .to_broadcast([P, HPG, CHUNK])).then_inc(landed, 16)

            def spread_m(i):
                spread(m_dec[i % 2], i // GROUPS, i % GROUPS, m_spread[i % 2])

            def spread_c(g):
                spread(c_dec[g % 2], 1, g, c_spread[g % 2])

            pool.wait_ge(S["ac_stored"], 16)
            pool.wait_ge(filled, index["ho7"] + 1)
            pool.wait_ge(S["conv_done"], 2)
            spread_m(0)
            pool.wait_ge(filled, index["hl1"] + 1)
            pool.wait_ge(S["gated_ready"], 1)
            load_state(0)
            spread_c(0)
            pool.wait_ge(filled, index["fs2"] + 1)
            spread_m(1)
            pool.wait_ge(filled, index["fs3"] + 1)
            spread_c(1)
            for i in range(2, 2 * GROUPS):
                pool.wait_ge(filled, index[f"y{(i - 2) // GROUPS}{(i - 2) % GROUPS}"] + 1)
                spread_m(i)
                if i == 5:
                    load_state(1)
                if i >= 6:
                    spread_c(i - GROUPS)
            pool.wait_ge(S["smp_ready"], 1)
            for n in range(2):
                pool.wait_ge(S[f"fs_stored{n}"], 32)
            pool.wait_ge(filled, index["y13"] + 1)
            outer_product(0)
            load_state(2)
            for i in range(TS):
                if i + 1 < TS:
                    outer_product(i + 1)
                if i == 0:
                    load_state(3)
                pool.wait_ge(S["st_done"], i + 1)
                nc.gpsimd.dma_start(states("out_9", i), st[i % 4]).then_inc(st_stored[i % 4], 16)
                if 1 <= i < TS - 3:
                    pool.wait_ge(st_stored[(i - 1) % 4], 16 * ((i - 1) // 4) + 16)
                    load_state(i + 3)
            for n in range(4):
                pool.wait_ge(st_stored[n], 32)

        @block.scalar
        def _(act):
            rows = [("conv_ssd_w", 0, 96, "o j (t c) -> (o j t) c"), ("conv_ssd_b", 96, 24, "o (t c) -> (o t) c")]
            for name, r, n, pat in rows:
                act.dma_start(rows_a[r:r + n, :], a[name].rearrange(pat, c=P)).then_inc(S["vec_loaded"], 16)
            rows = [("conv_lru_w", 0, 32, "o j (t c) -> (o j t) c"), ("conv_lru_b", 32, 8, "o (t c) -> (o t) c"),
                    ("norm_ffn", 80, 8, "o (t c) -> (o t) c"), ("norm_mix", 88, 8, "o (t c) -> (o t) c")]
            for name, r, n, pat in rows:
                act.dma_start(rows_b[r:r + n, :], a[name].rearrange(pat, c=P)).then_inc(S["vec_loaded"], 16)
            for k in range(KT):
                b = take_bank(act, f"x{k}")
                nc.scalar.copy(xT[:, k, :], b[:, 0:NT]).then_inc(emptied["s"], 1)
            b = take_bank(act, "ss0")
            nc.scalar.activation(rstd[:, 0, :], b[:, 0:NT], ACT.Copy, bias=EPS, scale=1.0 / D).then_inc(emptied["s"], 1)
            act.wait_ge(emptied["s"], nth["ss0"] + 1)
            nc.scalar.activation(rstd[:, 0, :], rstd[:, 0, :], ACT.Sqrt).then_inc(S["rms_ready"], 1)

            act.wait_ge(S["lam_abs"], 1)
            nc.scalar.activation(lt[1], lt[1], ACT.Exp, scale=-1.0).then_inc(S["lam_exp"], 1)
            act.wait_ge(S["heads_loaded"], 48)
            nc.scalar.activation(a_neg, a_log, ACT.Exp).then_inc(S["lam_exp"], 1)

            def take_tiles(first, end):
                for t in range(first, end):
                    act.wait_ge(S["acc_ready"], t + 1)
                    if t < NCONV:
                        nc.scalar.copy(cin[:, t, HIST:HIST + TP], ps[t % 2][:, 0:TP])
                        nc.scalar.copy(cin[:, t, S_IN + HIST * TS:CIN], ps[t % 2][:, TP:NT]).then_inc(S["acc_emptied"], 1)
                    elif t < NCONV + NPLAIN:
                        nc.scalar.copy(plain[:, t - NCONV, :], ps[t % 2][:, 0:NT]).then_inc(S["acc_emptied"], 1)

                    else:
                        nc.scalar.copy(xnT[:, t - NCONV - NPLAIN, :], ps[t % 2][:, 0:NT]).then_inc(S["acc_emptied"], 1)

            take_tiles(0, LX)
            act.wait_ge(S["dt_z"], 1)
            nc.scalar.activation(dtw[1], dtw[1], ACT.Exp, scale=-1.0).then_inc(S["dt_exp"], 1)
            take_tiles(LX, LX + 4)
            act.wait_ge(S["conv_done"], 1)
            for t in range(0, LX, 8):
                nc.scalar.activation(conv[:, t:t + 8, :], conv[:, t:t + 8, :], ACT.Silu).then_inc(S["silu_done"], 1)
                take_tiles(LX + 4 + t // 4, LX + 6 + t // 4)
            act.wait_ge(S["wdec_in"], 1)
            nc.scalar.activation(wdec, wdec, ACT.Exp).then_inc(S["wdec_exp"], 1)
            take_tiles(34, 40)
            for q in range(8):
                b = take_bank(act, f"ho{q}")
                nc.scalar.copy(hist_out[0:35, 512 * q:512 * q + 512], b[0:35, :]).then_inc(emptied["s"], 1)
            act.wait_ge(emptied["s"], nth["ho7"] + 1)
            act.dma_start(a["out_4"][0, 0], hist_out[0:3, 0:3072]).then_inc(S["hist_stored"], 16)
            act.dma_start(a["out_8"][0, :, 2, :], hist_out[27:35, 0:3072]).then_inc(S["hist_stored"], 16)
            act.dma_start(a["out_2"][0, 0], hist_out[0:3, 3072:4096]).then_inc(S["hist_stored"], 16)
            act.dma_start(a["out_6"][0, :, 2, :], hist_out[27:35, 3072:4096]).then_inc(S["hist_stored"], 16)
            act.dma_start(a["out_8"][0, :, 0:2, :], a["state_ssd_conv"][0, :, 1:3, :]).then_inc(S["hist_stored"], 16)
            act.dma_start(a["out_6"][0, :, 0:2, :], a["state_lru_conv"][0, :, 1:3, :]).then_inc(S["hist_stored"], 16)
            act.wait_ge(S["conv_done"], 2)
            for c in range(2):
                b = take_bank(act, f"bt{c}")
                nc.scalar.copy(b_tok[:, c].rearrange("p g n -> p (g n)"), b[:, :]).then_inc(emptied["s"], 1)
            for c in range(2):
                b = take_bank(act, f"cb{c}")
                nc.scalar.copy(cb[:, c].rearrange("p g n -> p (g n)"), b[:, :]).then_inc(emptied["s"], 1)
            for w in range(2):
                b = take_bank(act, f"bc{w}")
                nc.scalar.copy(bc_rows[0:TS, 512 * w:512 * w + 512], b[0:TS, :]).then_inc(emptied["s"], 1)
            act.wait_ge(emptied["s"], nth["bc1"] + 1)
            act.dma_start(bc_dram[:, :], bc_rows[0:TS, :]).then_inc(S["bc_stored"], 16)
            for t in range(KT):
                b = take_bank(act, f"rg{t}")
                nc.scalar.activation(lru[0][:, t, :], b[:, 0:NT], ACT.Sigmoid, bias=b_rg[:, t:t + 1]).then_inc(emptied["s"], 1)
                b = take_bank(act, f"ig{t}")
                nc.scalar.activation(lru[1][:, t, :], b[:, 0:NT], ACT.Sigmoid, bias=b_ig[:, t:t + 1]).then_inc(emptied["s"], 1)
            act.wait_ge(emptied["s"], nth["ig7"] + 1)
            for t in range(KT):
                ins = nc.scalar.activation(lru[2][:, t, :], lru[0][:, t, :], ACT.Exp, scale=sp8n[:, t:t + 1])
            ins.then_inc(S["a_ready"], 1)
            act.wait_ge(S["a_ready"], 1)
            for t in range(KT):
                ins = nc.scalar.activation(lru[0][:, t, :], lru[0][:, t, :], ACT.Tanh, scale=sp4[:, t:t + 1])
            ins.then_inc(S["u_ready"], 1)
            act.wait_ge(S["hist_stored"], 96)
            take_tiles(40, 41)
            act.wait_ge(S["u_ready"], 1)
            nc.scalar.activation(lru[0], lru[0], ACT.Sqrt).then_inc(S["sqrt_done"], 1)
            take_tiles(41, 42)
            nc.scalar.activation(plain[:, GATE:GATE + 8, :], plain[:, GATE:GATE + 8, :], ACT.Gelu_apprx_tanh).then_inc(S["sqrt_done"], 1)
            act.wait_ge(S["smp_ready"], 1)
            nc.scalar.activation(dx[:, :, TS:2 * TS], dx[:, :, TS:2 * TS], ACT.Exp).then_inc(S["da_exp"], 1)
            take_tiles(42, 48)
            for q in range(2):
                b = take_bank(act, f"hl{q}")
                nc.scalar.copy(h_out_t[0:9, 512 * q:512 * q + 512], b[0:9, :]).then_inc(emptied["s"], 1)
            act.wait_ge(emptied["s"], nth["hl1"] + 1)
            act.dma_start(a["out_3"][0], h_out_t[0:1, :]).then_inc(S["hl_stored"], 16)
            act.dma_start(a["out_7"][0], h_out_t[1:9, :]).then_inc(S["hl_stored"], 16)
            for g in range(GROUPS):
                b = take_bank(act, f"s0{g}")
                nc.scalar.copy(s0T[:, 512 * g:512 * g + 512], b[:, :]).then_inc(emptied["s"], 1)
                b = take_bank(act, f"fs{g}")
                if g >= 2:
                    act.wait_ge(S[f"fs_stored{g % 2}"], 16)
                nc.scalar.copy(fin_st[:, g % 2].rearrange("p t n -> p (t n)"), b[:, :]).then_inc(emptied["s"], 1)
                act.wait_ge(emptied["s"], nth[f"fs{g}"] + 1)
                act.dma_start(a["out_5"][0, 0].rearrange("(g t h) q n -> g (h q) t n", t=4, h=2)[g], fin_st[:, g % 2]).then_inc(S[f"fs_stored{g % 2}"], 16)

            def decay_since_start(g):
                act.wait_ge(c_spread[g % 2], 16 * (g // 2) + 16)
                nc.scalar.activation(c_dec[g % 2], c_dec[g % 2], ACT.Exp).then_inc(S["cdec_exp"], 1)

            def decay_between(i):
                act.wait_ge(S["dec_in"], i + 1)
                nc.scalar.activation(m_dec[i % 2], m_dec[i % 2], ACT.Exp).then_inc(S["dec_exp"], 1)

            def load_bc(i):
                act.dma_start(bc_all[i % 3].rearrange("p w g n -> p (w g n)"),
                              bc_dram[i:i + 1, :].to_broadcast([P, 1024])).then_inc(bc_landed[i % 3], 16)

            act.wait_ge(S["bc_stored"], 16)
            load_bc(0)
            decay_between(0)
            for i in range(2 * GROUPS):
                for t in FILL[i]:
                    take_tiles(48 + t, 49 + t)
                if i + 1 >= GROUPS and i + 1 < 2 * GROUPS:
                    decay_since_start(i + 1 - GROUPS)
                if i + 1 < 2 * GROUPS:
                    decay_between(i + 1)
            act.wait_ge(S["m_ready"], 8)
            load_bc(1)
            act.wait_ge(filled, index["y13"] + 1)
            load_bc(2)
            take_tiles(48 + sum(map(len, FILL)), 56)
            act.wait_ge(S["acc_emptied"], 56)
            nc.scalar.activation(plain[:, Z:Z + 16, :], plain[:, Z:Z + 16, :], ACT.Silu).then_inc(S["z_silu"], 1)
            act.wait_ge(S["hl_stored"], 32)
            take_tiles(56, 60)
            for i in range(3, TS):
                act.wait_ge(S["bc_used"], i - 2)
                load_bc(i)
                take_tiles(54 + 2 * i, 56 + 2 * i)
            take_tiles(70, 72)
            act.wait_ge(S["acc_emptied"], 72)
            nc.scalar.activation(plain[:, GA:GA + 16, :], plain[:, GA:GA + 16, :], ACT.Sigmoid).then_inc(S["ga_ready"], 1)
            take_tiles(72, 76)
            for g in range(GROUPS):
                act.wait_ge(S["yz_ready"], g + 1)
                nc.scalar.activation(plain[:, Z + 4 * g:Z + 4 * g + 4, :], yT[:, 4 * g:4 * g + 4, :], ACT.Square).then_inc(S["ysq_ready"], 1)
            take_tiles(76, 77)
            for g in range(GROUPS):
                b = take_bank(act, f"gn{g}")
                nc.scalar.activation(rstd[:, g, :], b[:, 0:NT], ACT.Copy, bias=EPS, scale=4.0 / 2048).then_inc(emptied["s"], 1)
            act.wait_ge(emptied["s"], nth["gn3"] + 1)
            nc.scalar.activation(rstd[:, :, :], rstd[:, :, :], ACT.Sqrt).then_inc(S["yrms_ready"], 1)
            take_tiles(77, 80)
            act.dma_start(w_router, a["w_router"][0].rearrange("(k p) e -> p k e", p=P)).then_inc(S["router_loaded"], 16)
            act.dma_start(b_router, a["b_router"].to_broadcast([P, E])).then_inc(S["router_loaded"], 16)
            act.wait_ge(S["acc_ready"], 80)
            act.dma_start(e_bias[:, 0:2 * D], a["b_gate_up"][0]).then_inc(S["bias_loaded"], 16)
            act.dma_start(e_bias[:, 2 * D:3 * D], a["b_down"][0]).then_inc(S["bias_loaded"], 16)
            b = take_bank(act, "ss1")
            nc.scalar.activation(rstd[:, 0, :], b[:, 0:NT], ACT.Copy, bias=EPS, scale=1.0 / D).then_inc(emptied["s"], 1)
            act.wait_ge(emptied["s"], nth["ss1"] + 1)
            nc.scalar.activation(rstd[:, 0, :], rstd[:, 0, :], ACT.Sqrt).then_inc(S["x1rms_ready"], 1)
            act.dma_start(n_final, a["norm_final"].rearrange("(o d) -> o d", o=1).to_broadcast([P, D])).then_inc(S["final_loaded"], 16)

            def take_rows(w, dst):
                for t, n in enumerate(ROWS):
                    for h in range(2):
                        b = take_bank(act, f"{w}{t}{h}")
                        nc.scalar.copy(dst[0:n, t, 512 * h:512 * h + 512], b[0:n, :]).then_inc(emptied["s"], 1)

            take_rows("u", u_tok)
            act.wait_ge(S["gates_in"], 3)
            for t, n in enumerate(ROWS):
                ins = nc.scalar.activation(gates[0:n, t, :], gates[0:n, t, :], ACT.Exp)
            ins.then_inc(S["gates_exp"], 1)
            act.wait_ge(S["passes_ready"], 1)
            n_passes = act.value_load(passes[0:1, 0:1], min_val=1, max_val=MAXP)

            def take_tokens(j):
                act.wait_ge(S["xg_filled"], j + 1)
                nc.scalar.copy(xg, p_xg[:, :]).then_inc(S["xg_ready"], 1)
                act.wait_ge(S["xt_filled"], j + 1)
                nc.scalar.copy(xt.rearrange("p c s -> p (c s)"), p_xt[:, :]).then_inc(S["xt_ready"], 1)

            act.wait_ge(S["comb_emptied"], 2)
            nc.scalar.copy(y_out[:, 0:1], y_out[:, 0:1]).then_inc(S["y_copied"], 1)
            nc.scalar.copy(pgt[:, 0:1], pgt[:, 0:1]).then_inc(S["pgt_ready"], 1)
            with act.Fori(0, n_passes) as p:
                take_tokens((E + 1) * p)
                with act.Fori(0, E) as e:
                    i = E * p + e
                    act.wait_ge(S["g1_ready"], i + 1)
                    nc.scalar.activation(sg, g1, ACT.Sigmoid, scale=1.702).then_inc(S["sg_ready"], 1)
                    take_tokens((E + 1) * p + e + 1)
                    act.wait_ge(S["pg_filled"], i + 1)
                    nc.scalar.copy(pgt, p_xg[:, 0:NT]).then_inc(S["pgt_ready"], 1)
                    act.wait_ge(S["ht_filled"], i + 1)
                    nc.scalar.copy(ht.rearrange("p c s -> p (c s)"), p_ht[:, :]).then_inc(S["ht_ready"], 1)
                    act.wait_ge(S["w_used"], NSLOT * i + NSLOT)
                    nc.scalar.copy(y_out, p_y[:, :]).then_inc(S["y_copied"], 1)
            act.wait_ge(S["fin_filled"], KT)
            for t, n in enumerate(ROWS):
                for h in range(2):
                    nc.scalar.activation(squares[0:n, t, 512 * h:512 * h + 512],
                                         p_rows[t][h][0:n, :], ACT.Square, accum_out=ssq_h[0:n, t, h:h + 1]).then_inc(S["sq_sum"], 1)
            for t, n in enumerate(ROWS):
                act.wait_ge(S["rms_in"], t + 1)
                nc.scalar.activation(ssq[0:n, t:t + 1], ssq[0:n, t:t + 1], ACT.Sqrt).then_inc(S["fin_rms"], 1)

        @block.tensor
        def _(pe):
            pe.wait_ge(S["ident_set"], 1)

            def turn(out, src, k):
                return nc.tensor.transpose(out, src, ident[0:k, 0:k])

            pe.wait_ge(S["x_loaded"], 32)
            for k in range(KT):
                b = open_bank(f"x{k}")
                for t in range(3):
                    n = P if t < 2 else TS
                    ins = turn(b[:, P * t:P * t + n], x_rows[0:n, t, P * k:P * k + P], n)
                ins.then_inc(filled, 1)
            def sum_squares(name, sq_of, n, ready, per):
                b = open_bank(name)
                for k in range(n):
                    if per:
                        pe.wait_ge(ready, k + 1)
                    ins = mm(b[:, 0:NT], ones[:, :], sq_of(k), k == 0, k == n - 1)
                ins.then_inc(filled, 1)

            sum_squares("ss0", lambda k: sq[:, k, :], KT, S["squares_ready"], True)
            pe.wait_ge(S["vec_loaded"], 160)
            pe.wait_ge(S["dskip_spread"], 1)
            b = open_bank("vec")
            turn(b[:, 0:120], rows_a[0:120, :], 120)
            turn(b[:, 128:240], rows_b[0:112, :], 112).then_inc(filled, 1)

            pe.wait_ge(S["consts_set"], 1)

            def in_tile(g, t):
                slot, m = t // 2, t % 2
                if m == 0:
                    pe.wait_ge(landed[slot], 16 * g + 16)
                first = isinstance(g, int) and g == t == 0
                if not first:
                    pe.wait_ge(S["acc_emptied"], 8 * g + t - 1)
                for k in range(KT):
                    w = stream[slot][:, 256 * k + P * m:256 * k + P * m + P]
                    if first:
                        pe.wait_ge(S["xn_ready"], k + 1)
                    ins = mm(ps[m][:, 0:NT], w, xnT[:, k, :], k == 0, k == KT - 1)
                ins.then_inc(S["acc_ready"], 1)

            def in_groups(g0, n):
                if n == 1:
                    for t in range(8):
                        in_tile(g0, t)
                else:
                    with pe.Fori(g0, g0 + n) as g:
                        for t in range(8):
                            in_tile(g, t)

            in_groups(0, 1)
            pe.wait_ge(S["hist_loaded"], 48)
            for q in range(2):
                b = open_bank(f"hist{q}")
                for j in range(16):
                    t = 16 * q + j
                    ins = turn(b[:, 24 * j:24 * j + 24], hist_rows[0:24, P * t:P * t + P], 24)
                ins.then_inc(filled, 1)
            b = open_bank("h0")
            for t in range(KT):
                ins = turn(b[:, TS * t:TS * t + TS], h0_rows[0:TS, P * t:P * t + P], TS)
            ins.then_inc(filled, 1)
            in_groups(1, 2)
            b = open_bank("dt")
            wdt = arena(T0 + 3 * KT * NT, KT * HEADS).rearrange("p (k c) -> p k c", k=KT)
            pe.wait_ge(S["heads_loaded"], 48)
            for k in range(KT):
                ins = mm(b[0:HEADS, 0:NT], wdt[:, k, :], xnT[:, k, :], k == 0, k == KT - 1)
            ins.then_inc(filled, 1)
            in_groups(3, 1)
            pe.wait_ge(S["diag_ready"], 1)
            b = open_bank("tok")
            for w, src in enumerate((dtT, dtT, acT, acT)):
                turn(b[:, HEADS * w:HEADS * w + HEADS], src[:, CHUNK * (w % 2):CHUNK * (w % 2) + CHUNK], HEADS)
            mm(b[:, 128:192], ones[0:HEADS, :], diag, True, True).then_inc(filled, 1)
            in_groups(4, 1)
            for q in range(8):
                b = open_bank(f"ho{q}")
                for j in range(4):
                    ins = turn(b[0:35, P * j:P * j + P], cin[:, 4 * q + j, TP:CIN], P)
                ins.then_inc(filled, 1)
            pe.wait_ge(S["silu_done"], 3)
            for c in range(2):
                for g in range(GROUPS):
                    b = open_bank(f"xs{c}{g}")
                    for j in range(4):
                        ins = turn(b[:, P * j:P * j + P], conv[:, XS + 4 * g + j, CHUNK * c:CHUNK * c + CHUNK], P)
                    ins.then_inc(filled, 1)
            for c in range(2):
                b = open_bank(f"bt{c}")
                for g in range(GROUPS):
                    ins = turn(b[:, P * g:P * g + P], conv[:, BT + g, CHUNK * c:CHUNK * c + CHUNK], P)
                ins.then_inc(filled, 1)
            for c in range(2):
                b = open_bank(f"cb{c}")
                for g in range(GROUPS):
                    w = slice(CHUNK * c, CHUNK * c + CHUNK)
                    ins = mm(b[:, P * g:P * g + P], conv[:, BT + g, w], conv[:, CT + g, w], True, True)
                ins.then_inc(filled, 1)
            pe.wait_ge(S["ex_set"], 1)
            b = open_bank("smp")
            for t in range(16):
                w = ex[:, 2 * t:2 * t + 2, :].rearrange("p h c -> p (h c)")
                mm(b[:, 16 * t:16 * t + 8], w, dtT[:, TP:NT], True, True)
                ins = mm(b[:, 16 * t + 8:16 * t + 16], w, acT[:, TP:NT], True, True)
            ins.then_inc(filled, 1)
            for w in range(2):
                b = open_bank(f"bc{w}")
                for g in range(GROUPS):
                    ins = turn(b[0:TS, P * g:P * g + P], conv[:, BT + 4 * w + g, TP:NT], P)
                ins.then_inc(filled, 1)
            pe.wait_ge(S["gates_loaded"], 64)
            pe.wait_ge(S["conv_done"], 2)
            for t in range(KT):
                for w, n in enumerate(("rg", "ig")):
                    b = open_bank(f"{n}{t}")
                    mm(b[:, 0:NT], gw[:, w, t, :], conv[:, LX + t, :], True, True).then_inc(filled, 1)
            in_groups(5, 1)
            pe.wait_ge(S["h_ready"], 1)
            for q in range(2):
                b = open_bank(f"hl{q}")
                for j in range(4):
                    ins = turn(b[0:9, P * j:P * j + P], conv[:, LX + 4 * q + j, TP - 1:NT], P)
                ins.then_inc(filled, 1)
            for g in range(GROUPS):
                pe.wait_ge(S["xw_ready"], g + 1)
                pe.wait_ge(emptied["s"], nth["bt1"] + 1)
                b = open_bank(f"s0{g}")
                mm(b[:, :], b_tok[:, 0, g, :], xw[g % 2][:, 0].rearrange("p h q -> p (h q)"), True, True).then_inc(filled, 1)
                b = open_bank(f"fs{g}")
                for j in range(4):
                    for c in range(2):
                        ins = mm(b[:, P * j:P * j + P], xw[g % 2][:, 1 + c, 2 * j:2 * j + 2, :].rearrange("p h q -> p (h q)"),
                                 b_tok[:, c, g, :], c == 0, c == 1)
                ins.then_inc(filled, 1)

            def ssd(c):
                for g in range(GROUPS):
                    i = GROUPS * c + g
                    for t in FILL[i]:
                        in_tile(6, t)
                    b = open_bank(f"y{c}{g}")
                    pe.wait_ge(S["m_ready"], i + 1)
                    if c == 1:
                        pe.wait_ge(S["cdec_ready"], g + 1)
                    for h in range(HPG):
                        out = b[64 * (h % 2):64 * (h % 2) + 64, P * (h // 2):P * (h // 2) + P]
                        ins = mm(out, xd[:, c, HPG * g + h, :], m_dec[i % 2][:, h, :], True, c == 0)
                        if c == 1:
                            ins = mm(out, s0T[:, HD * (HPG * g + h):HD * (HPG * g + h) + HD], c_dec[g % 2][:, h, :], False, True)
                    ins.then_inc(filled, 1)

            ssd(0)
            ssd(1)
            for t in range(sum(map(len, FILL)), 8):
                in_tile(6, t)
            in_groups(7, 1)
            in_groups(8, 1)
            def project(g0, k_tiles, x_of, tiles0, first=0, end=8, ready=None):
                per = 16 // k_tiles
                for t in range(first, end):
                    c, m = t // per, t % per
                    s, n = c % 4, tiles0 + t
                    if m == 0:
                        pe.wait_ge(landed[s], 16 * (g0 + c // 4) + 16)
                    if n < 10:
                        pe.wait_ge(S["acc_emptied"], 72 + n - 1)
                    else:
                        pe.wait_ge(S["acc2_emptied"], n - 9)
                    for k in range(k_tiles):
                        if t == 0 and ready:
                            pe.wait_ge(ready, k + 1)
                        width = SLOT // k_tiles
                        w = stream[s][:, width * k + P * m:width * k + P * m + P]
                        ins = mm(ps[n % 2][:, 0:NT], w, x_of(k), k == 0, k == k_tiles - 1)
                    ins.then_inc(S["acc_ready"], 1)

            pe.wait_ge(S["gated_ready"], 1)
            project(9, KT, lambda k: plain[:, GATE + k, :], 0, 0, 5)
            for g in range(GROUPS):
                pe.wait_ge(S["ysq_ready"], g + 1)
                sum_squares(f"gn{g}", lambda k: plain[:, Z + 4 * g + k, :], 4, None, False)
            project(9, KT, lambda k: plain[:, GATE + k, :], 0, 5, 8)
            project(10, 16, lambda k: yT[:, k, :], 8, ready=S["y_final"])
            project(12, KT, lambda k: plain[:, GA + k, :], 16, ready=S["merged_ready"])
            sum_squares("ss1", lambda k: conv[:, k, :], KT, S["x1_sq"], True)

            def turn_rows(w, src):
                for t, n in enumerate(ROWS):
                    for h in range(2):
                        b = open_bank(f"{w}{t}{h}")
                        for j in range(4):
                            ins = turn(b[0:n, P * j:P * j + P], src[:, 4 * h + j, P * t:P * t + n], P)
                        ins.then_inc(filled, 1)

            pe.wait_ge(S["router_loaded"], 32)
            b = open_bank("logits")
            for t, n in enumerate(ROWS):
                for k in range(KT):
                    if t == 0:
                        pe.wait_ge(S["u2_ready"], k + 1)
                    ins = mm(b[0:n, E * t:E * t + E], xnT[:, k, P * t:P * t + n], w_router[:, k, :], k == 0, k == KT - 1)
            ins.then_inc(filled, 1)
            turn_rows("u", xnT)
            pe.wait_ge(S["mark_ready"], 3)
            b = open_bank("rank")
            mm(b[:, 0:E], before[:, :], mark[:, 0, :], True, True)
            mm(b[:, E:2 * E], ones[:, :], mark[:, 0, :], True, False)
            mm(b[:, E:2 * E], before[:, :], mark[:, 1, :], False, True)
            mm(b[0:TS, 2 * E:3 * E], ones[:, 0:TS], mark[:, 0, :], True, False)
            mm(b[0:TS, 2 * E:3 * E], ones[:, 0:TS], mark[:, 1, :], False, False)
            mm(b[0:TS, 2 * E:3 * E], before[0:TS, 0:TS], mark[0:TS, 2, :], False, True)
            mm(b[:, 3 * E:4 * E], ones[:, :], mark[:, 0, :], True, False)
            mm(b[:, 3 * E:4 * E], ones[:, :], mark[:, 1, :], False, False)
            mm(b[:, 3 * E:4 * E], ones[0:TS, :], mark[0:TS, 2, :], False, True).then_inc(filled, 1)
            pe.wait_ge(S["passes_ready"], 1)
            n_passes = pe.value_load(passes[0:1, 0:1], min_val=1, max_val=MAXP)
            pe.wait_ge(emptied["s"], sum(w == "s" for _, w in uses))
            pe.wait_ge(emptied["v"], sum(w == "v" for _, w in uses))
            pe.wait_ge(S["bias_loaded"], 32)

            def gather(j):
                pe.wait_ge(S["pick_ready"], j + 1)
                for t, n in enumerate(ROWS):
                    for h in range(2):
                        ins = mm(p_xg[SLOTS * h:SLOTS * h + SLOTS, :], pick[0:n, t, :],
                                 u_tok[0:n, t, 512 * h:512 * h + 512], t == 0, t == 2)
                ins.then_inc(S["xg_filled"], 1)
                pe.wait_ge(S["xg_ready"], j + 1)
                for c in range(4):
                    ins = turn(p_xt[:, P * c:P * c + P], xg[:, P * c:P * c + P], P)
                ins.then_inc(S["xt_filled"], 1)

            def combine(i, c):
                pe.wait_ge(S["comb_emptied"], KT * i + c + 1)
                h = c // 4
                mm(p_comb[c % 2][:, 0:NT], y_out[SLOTS * h:SLOTS * h + SLOTS, P * (c % 4):P * (c % 4) + P],
                   pgt[SLOTS * h:SLOTS * h + SLOTS, :], True, True).then_inc(S["comb_filled"], 1)

            def item(p, q, r):
                e = ROUND * q + r
                i = E * p + e

                def chunk(c):
                    j = NSLOT * r + c
                    rounds = ROUND * NSLOT // MSLOT
                    return j % MSLOT, 16 * rounds * (E // ROUND * p + q) + 16 * (j // MSLOT + 1)

                pe.wait_ge(S["xt_ready"], (E + 1) * p + e + 1)
                pe.wait_ge(S["pick_e_ready"], (E + 1) * p + e + 1)
                pe.wait_ge(S["gu_emptied"], i)
                for n in range(4):
                    mm(p_gu[n // 2][SLOTS * (n % 2):SLOTS * (n % 2) + SLOTS, :], pick_e, e_bias[:, 512 * n:512 * n + 512], True, False)
                pe.wait_ge(S["y_copied"], i + 1)
                pe.wait_ge(S["pgt_ready"], i + 1)
                for k in range(KT):
                    combine(i, k)
                    slot, landed_by = chunk(k)
                    pe.wait_ge(w_landed[slot], landed_by)
                    for n in range(4):
                        ins = mm(p_gu[n // 2][SLOTS * (n % 2):SLOTS * (n % 2) + SLOTS, :],
                                 xt[:, k % 4, SLOTS * (k // 4):SLOTS * (k // 4) + SLOTS],
                                 stream[slot][:, 512 * n:512 * n + 512], False, k == KT - 1)
                    ins.then_inc(S["w_used"], 1)
                gather((E + 1) * p + e + 1)
                pe.wait_ge(S["pg_ready"], i + 1)
                for t, n in enumerate(ROWS):
                    ins = turn(p_xg[:, P * t:P * t + n], pg[0:n, t, :], n)
                ins.then_inc(S["pg_filled"], 1)
                for h in range(2):
                    mm(p_y[SLOTS * h:SLOTS * h + SLOTS, :], pick_e, e_bias[:, 2 * D + 512 * h:2 * D + 512 * h + 512], True, False)
                pe.wait_ge(S["ha_ready"], i + 1)
                for c in range(4):
                    ins = turn(p_ht[:, P * c:P * c + P], ha[:, P * c:P * c + P], P)
                ins.then_inc(S["ht_filled"], 1)
                pe.wait_ge(S["ht_ready"], i + 1)
                for k in range(KT):
                    if k % 2 == 0:
                        slot, landed_by = chunk(KT + k // 2)
                        pe.wait_ge(w_landed[slot], landed_by)
                    for h in range(2):
                        ins = mm(p_y[SLOTS * h:SLOTS * h + SLOTS, :],
                                 ht[:, k % 4, SLOTS * (k // 4):SLOTS * (k // 4) + SLOTS],
                                 stream[slot][:, D * (k % 2) + 512 * h:D * (k % 2) + 512 * h + 512], False, k == KT - 1)
                    if k % 2:
                        ins.then_inc(S["w_used"], 1)

            with pe.Fori(0, n_passes) as p:
                gather((E + 1) * p)
                with pe.Fori(0, E // ROUND) as q:
                    for r in range(ROUND):
                        item(p, q, r)
            items = E * n_passes
            pe.wait_ge(S["y_copied"], items + 1)
            pe.wait_ge(S["pgt_ready"], items + 1)
            combine(items, 0)
            combine(items, 1)
            for c in range(KT):
                pe.wait_ge(S["comb_emptied"], KT * items + c + 3)
                for t, n in enumerate(ROWS):
                    ins = turn(p_rows[t][c // 4][0:n, P * (c % 4):P * (c % 4) + P], xT[:, c, P * t:P * t + n], P)
                ins.then_inc(S["fin_filled"], 1)
                if c + 2 < KT:
                    combine(items, c + 2)

        @block.vector
        def _(dve):
            link = linker(dve, dve_step)
            V = nc.vector

            def done(name, ins):
                ins.then_inc(S[name], 1)

            V.memset(cin[:, :, 0:HIST], 0.0)
            for k in range(KT):
                dve.wait_ge(emptied["s"], k + 1)
                done("squares_ready", V.tensor_tensor(sq[:, k, :], xT[:, k, :], xT[:, k, :], ALU.mult))
            dve.wait_ge(S["dskip_loaded"], 16)
            done("dskip_spread", V.tensor_copy(rows_b[96:112, :].rearrange("t (h j) -> t h j", h=2),
                                               dsk[96:112, :].unsqueeze(2).to_broadcast([16, 2, HD])))
            b = take_bank(dve, "vec")
            V.tensor_copy(cvec[:, :, 0:24], b[:, 0:120].rearrange("p (j t) -> p j t", j=5))
            V.tensor_copy(cvec[:, :, 24:32], b[:, 128:168].rearrange("p (j t) -> p j t", j=5))
            V.tensor_copy(vec[:, 0:72], b[:, 168:240]).then_inc(emptied["v"], 1)
            dve.wait_ge(emptied["v"], 1)
            V.tensor_scalar(lt[4], lam, -1.0, 0.0, ALU.mult, ALU.max)
            link(V.tensor_scalar(lt[1], lam, -1.0, None, ALU.mult))
            done("lam_abs", V.tensor_tensor(lt[1], lt[1], lam, ALU.max))

            def log1p(e, s, s2, p):
                link(V.tensor_scalar(p, e, 2.0, None, ALU.add))
                link(V.reciprocal(p, p))
                link(V.tensor_tensor(s, e, p, ALU.mult))
                link(V.tensor_tensor(s2, s, s, ALU.mult))
                link(V.tensor_scalar(p, s2, 1.0 / 15, None, ALU.mult))
                for n in (13, 11, 9, 7, 5, 3):
                    link(V.scalar_tensor_tensor(out=p, in0=p, scalar=1.0 / n, in1=s2, op0=ALU.add, op1=ALU.mult))
                link(V.scalar_tensor_tensor(out=p, in0=p, scalar=1.0, in1=s, op0=ALU.add, op1=ALU.mult))

            dve.wait_ge(S["rms_ready"], 1)
            link(V.reciprocal(rstd[:, 0, :], rstd[:, 0, :]))
            for k in range(KT):
                ins = V.scalar_tensor_tensor(out=xnT[:, k, :], in0=xT[:, k, :], scalar=n_mix[:, k:k + 1],
                                             in1=rstd[:, 0, :], op0=ALU.mult, op1=ALU.mult)
                done("xn_ready", ins)
            dve.wait_ge(S["consts_set"], 1)
            done("ex_set", V.tensor_copy(ex, ident[0:E, 0:E].unsqueeze(2).to_broadcast([E, E, HD])))
            dve.wait_ge(S["lam_exp"], 2)
            log1p(lt[1], lt[2], lt[3], lt[0])
            link(V.scalar_tensor_tensor(out=lt[0], in0=lt[0], scalar=2.0, in1=lt[4], op0=ALU.mult, op1=ALU.add))
            V.tensor_scalar(sp4, lt[0], 4.0, None, ALU.mult)
            V.tensor_scalar(sp8n, lt[0], -8.0, None, ALU.mult)
            link(V.tensor_scalar(a_neg, a_neg, -1.0, None, ALU.mult))

            for q in range(2):
                b = take_bank(dve, f"hist{q}")
                V.tensor_copy(cin[:, 16 * q:16 * q + 16, S_IN:S_IN + HIST * TS].rearrange("p t (j b) -> p t j b", j=HIST),
                              b[:, 0:384].rearrange("p (t b j) -> p t j b", b=TS, j=HIST)).then_inc(emptied["v"], 1)
            b = take_bank(dve, "h0")
            V.tensor_copy(h0T, b[:, 0:64].rearrange("p (t b) -> p t b", b=TS)).then_inc(emptied["v"], 1)

            steps = [0]

            def convolve(t):
                dve.wait_ge(S["acc_emptied"], t + 1)
                o = conv[:, t, 0:TP]
                V.tensor_scalar(o, cin[:, t, 0:TP], cvec[:, 0, t:t + 1], cvec[:, 4, t:t + 1], ALU.mult, ALU.add).then_inc(S["conv_step"], 1)
                steps[0] += 1
                for j in range(1, CW):
                    dve.wait_ge(S["conv_step"], steps[0])
                    V.scalar_tensor_tensor(out=o, in0=cin[:, t, j:j + TP], scalar=cvec[:, j, t:t + 1], in1=o,
                                           op0=ALU.mult, op1=ALU.add).then_inc(S["conv_step"], 1)
                    steps[0] += 1

            def convolve_samples(t0, n):
                o = conv[:, t0:t0 + n, TP:NT]
                tmp = tmp_s[:, 0:n * TS].rearrange("p (t b) -> p t b", b=TS)

                def tap(j):
                    return cvec[:, j, t0:t0 + n].unsqueeze(2).to_broadcast([P, n, TS])
                link(V.tensor_tensor(o, cin[:, t0:t0 + n, S_IN:S_IN + TS], tap(0), ALU.mult))
                for j in range(1, CW):
                    link(V.tensor_tensor(tmp, cin[:, t0:t0 + n, S_IN + TS * j:S_IN + TS * j + TS], tap(j), ALU.mult))
                    link(V.tensor_tensor(o, o, tmp, ALU.add))
                return V.tensor_tensor(o, o, tap(CW), ALU.add)

            for t in range(LX):
                convolve(t)
            done("conv_done", convolve_samples(0, LX))
            z, e, s, s2, p, mz = dtw[0:6]
            b = take_bank(dve, "dt")
            V.tensor_scalar(z, b[0:HEADS, 0:NT], dt_b, None, ALU.add).then_inc(emptied["v"], 1)
            dve.wait_ge(emptied["v"], nth["dt"] + 1)
            link(V.tensor_scalar(mz, z, 0.0, None, ALU.max))
            link(V.tensor_scalar(e, z, -1.0, None, ALU.mult))
            done("dt_z", V.tensor_tensor(e, e, z, ALU.max))
            dve.wait_ge(S["dt_exp"], 1)
            log1p(e, s, s2, p)
            link(V.scalar_tensor_tensor(out=dtT, in0=p, scalar=2.0, in1=mz, op0=ALU.mult, op1=ALU.add))
            link(V.tensor_scalar(daT, dtT, a_neg, None, ALU.mult))
            for c in range(2):
                w = slice(CHUNK * c, CHUNK * c + CHUNK)
                link(V.tensor_tensor_scan(acT[:, w], ones[0:HEADS, 0:CHUNK], daT[:, w], 0.0, ALU.mult, ALU.add))
            link(V.tensor_copy(acT[:, TP:NT], daT[:, TP:NT]))
            for c in range(2):
                last_c = CHUNK * c + CHUNK - 1
                ins = V.tensor_scalar(diag[:, HEADS * c:HEADS * c + HEADS], ident[0:HEADS, 0:HEADS], acT[:, last_c:last_c + 1], None, ALU.mult)
            done("diag_ready", ins)
            b = take_bank(dve, "tok")
            V.tensor_copy(tok.rearrange("p w h -> p (w h)"), b[:, 0:128])
            V.tensor_copy(last.rearrange("p c h -> p (c h)"), b[:, 128:192]).then_inc(emptied["v"], 1)
            dve.wait_ge(emptied["v"], nth["tok"] + 1)
            V.tensor_tensor(wdec[:, 2, :], last[:, 1, :], tok[:, 3, :], ALU.subtract)
            link(V.tensor_tensor(wdec[:, 0, :], last[:, 0, :], tok[:, 2, :], ALU.subtract))
            done("wdec_in", V.tensor_tensor(wdec[:, 1, :], wdec[:, 0, :], last[:, 1, :], ALU.add))
            for t in range(LX, NCONV):
                convolve(t)
            done("conv_done", convolve_samples(LX, KT))
            dve.wait_ge(S["conv_done"], 2)
            dve.wait_ge(filled, index["ho7"] + 1)
            for c in range(2):
                for g in range(GROUPS):
                    b = take_bank(dve, f"xs{c}{g}")
                    hs = slice(HPG * g, HPG * g + HPG)
                    V.tensor_tensor(xd[:, c, hs, :], b[:, :].rearrange("p (h q) -> p h q", q=HD),
                                    tok[:, c, hs].unsqueeze(2).to_broadcast([P, HPG, HD]), ALU.mult).then_inc(emptied["v"], 1)
            b = take_bank(dve, "smp")
            V.tensor_copy(dx.rearrange("p t w -> p (t w)"), b[:, 0:256]).then_inc(emptied["v"], 1)
            dve.wait_ge(emptied["v"], nth["smp"] + 1)
            xs_s = conv[:, XS:XS + 16, TP:NT]
            done("smp_ready", V.tensor_tensor(xds, xs_s, dx[:, :, 0:TS], ALU.mult))
            dve.wait_ge(S["u_ready"], 1)
            lx = conv[:, LX:LX + KT, :]
            link(V.tensor_tensor(lx, lx, lru[1], ALU.mult))
            dve.wait_ge(S["sqrt_done"], 1)
            link(V.scalar_tensor_tensor(out=lru[0], in0=lru[2], scalar=1.0, in1=lru[0], op0=ALU.add, op1=ALU.mult))
            link(V.tensor_tensor(lru[0], lru[0], lx, ALU.mult))
            link(V.tensor_tensor(tmp_s[:, 0:64].rearrange("p (t b) -> p t b", b=TS), h0T, lru[2][:, :, TP:NT], ALU.mult))
            V.tensor_tensor(lx[:, :, TP:NT], tmp_s[:, 0:64].rearrange("p (t b) -> p t b", b=TS), lru[0][:, :, TP:NT], ALU.add)
            for t in range(KT):
                ins = V.tensor_tensor_scan(conv[:, LX + t, 0:TP], lru[2][:, t, 0:TP], lru[0][:, t, 0:TP], 0.0, ALU.mult, ALU.add)
            done("h_ready", ins)
            dve.wait_ge(S["h_ready"], 1)
            dve.wait_ge(S["sqrt_done"], 2)
            gate = plain[:, GATE:GATE + KT, :]
            done("gated_ready", V.tensor_tensor(gate, gate, lx, ALU.mult))
            dve.wait_ge(S["wdec_exp"], 1)
            dve.wait_ge(emptied["v"], nth["xs13"] + 1)
            for g in range(GROUPS):
                hs = slice(HPG * g, HPG * g + HPG)
                if g > 1:
                    dve.wait_ge(filled, index[f"fs{g - 2}"] + 1)
                for w, c in ((0, 0), (1, 0), (2, 1)):
                    ins = V.tensor_tensor(xw[g % 2][:, w], xd[:, c, hs, :], wdec[:, w, hs].unsqueeze(2).to_broadcast([P, HPG, HD]), ALU.mult)
                done("xw_ready", ins)

            def ssd(c):
                def differences(g):
                    i = GROUPS * c + g
                    dve.wait_ge(m_spread[i % 2], 16 * (i // 2) + 16)
                    for h in range(HPG):
                        m = m_dec[i % 2][:, h, :]
                        ins = V.scalar_tensor_tensor(out=m, in0=m, scalar=tok[:, 2 + c, HPG * g + h:HPG * g + h + 1],
                                                     in1=cmask[:, :], op0=ALU.subtract, op1=ALU.add)
                    done("dec_in", ins)

                differences(0)
                for g in range(GROUPS):
                    i = GROUPS * c + g
                    if c == 1:
                        dve.wait_ge(S["cdec_exp"], g + 1)
                        cw = conv[:, CT + g, CHUNK:TP].unsqueeze(1).to_broadcast([P, HPG, CHUNK])
                        done("cdec_ready", V.tensor_tensor(c_dec[g % 2], c_dec[g % 2], cw, ALU.mult))
                    dve.wait_ge(S["dec_exp"], i + 1)
                    if i == 0:
                        dve.wait_ge(emptied["s"], nth["cb1"] + 1)
                    done("m_ready", V.tensor_tensor(m_dec[i % 2], m_dec[i % 2], cb[:, c, g, :].unsqueeze(1).to_broadcast([P, HPG, CHUNK]), ALU.mult))
                    if g + 1 < GROUPS:
                        differences(g + 1)
                    b = take_bank(dve, f"y{c}{g}")
                    for j in range(4):
                        t = 4 * g + j
                        w = slice(CHUNK * c, CHUNK * c + CHUNK)
                        ins = V.scalar_tensor_tensor(out=yT[:, t, w], in0=conv[:, XS + t, w], scalar=dskip[:, t:t + 1],
                                                     in1=b[:, P * j:P * j + P], op0=ALU.mult, op1=ALU.add)
                    ins.then_inc(emptied["v"], 1)

            dve.wait_ge(filled, index["fs3"] + 1)
            ssd(0)
            ssd(1)
            dve.wait_ge(S["da_exp"], 1)
            for i in range(TS):
                dve.wait_ge(st_loaded[i % 4], 16 * (i // 4) + 16)
                dve.wait_ge(S["outer_ready"], i + 1)
                s_i, o_i = st[i % 4], outer[i % 2]
                for t in range(16):
                    ins = V.scalar_tensor_tensor(out=s_i[:, t, :], in0=s_i[:, t, :], scalar=dx[:, t, TS + i:TS + i + 1],
                                                 in1=o_i[:, t, :], op0=ALU.mult, op1=ALU.add)
                done("st_done", ins)
                dve.wait_ge(S["st_done"], i + 1)
                for t in range(16):
                    ins = V.tensor_tensor_reduce(o_i[:, t, :], s_i[:, t, :], bc_all[i % 3][:, 1, t // 4, :], 1.0, 0.0, ALU.mult, ALU.add,
                                                 ys[:, t, i:i + 1])
                done("bc_used", ins)
            dve.wait_ge(S["bc_used"], TS)
            link(V.tensor_tensor(xds, xs_s, dskip.unsqueeze(2).to_broadcast([P, 16, TS]), ALU.mult))
            link(V.tensor_tensor(yT[:, :, TP:NT], xds, ys, ALU.add))
            dve.wait_ge(S["z_silu"], 1)
            for g in range(GROUPS):
                w = slice(4 * g, 4 * g + 4)
                done("yz_ready", V.tensor_tensor(yT[:, w, :], yT[:, w, :], plain[:, Z + 4 * g:Z + 4 * g + 4, :], ALU.mult))
            dve.wait_ge(S["yz_ready"], GROUPS)
            dve.wait_ge(S["yrms_ready"], 1)
            for g in range(GROUPS):
                link(V.reciprocal(rstd[:, g, :], rstd[:, g, :]))
                for t in range(4 * g, 4 * g + 4):
                    done("y_final", V.scalar_tensor_tensor(out=yT[:, t, :], in0=yT[:, t, :], scalar=ssd_norm[:, t:t + 1],
                                                           in1=rstd[:, g, :], op0=ALU.mult, op1=ALU.mult))
            dve.wait_ge(S["ga_ready"], 1)
            dve.wait_ge(S["acc_emptied"], 80)
            link(V.tensor_tensor(plain[:, GA:GA + KT, :], plain[:, GA:GA + KT, :], xnT[:, :, :], ALU.mult))
            for t in range(KT):
                dve.wait_ge(S["acc_ready"], 80 + t + 1)
                V.tensor_tensor(plain[:, GB + t, :], plain[:, GB + t, :], ps[t % 2][:, 0:NT], ALU.mult).then_inc(S["acc2_emptied"], 1)
                dve.wait_ge(S["acc2_emptied"], t + 1)
                done("merged_ready", V.tensor_tensor(plain[:, GA + t, :], plain[:, GA + t, :], plain[:, GB + t, :], ALU.add))
            for t in range(KT):
                dve.wait_ge(S["acc_ready"], 88 + t + 1)
                V.tensor_tensor(xT[:, t, :], xT[:, t, :], ps[t % 2][:, 0:NT], ALU.add).then_inc(S["acc2_emptied"], 1)
                dve.wait_ge(S["acc2_emptied"], 8 + t + 1)
                done("x1_sq", V.tensor_tensor(conv[:, t, :], xT[:, t, :], xT[:, t, :], ALU.mult))
            dve.wait_ge(S["x1rms_ready"], 1)
            link(V.reciprocal(rstd[:, 0, :], rstd[:, 0, :]))
            for k in range(KT):
                ins = V.scalar_tensor_tensor(out=xnT[:, k, :], in0=xT[:, k, :], scalar=n_ffn[:, k:k + 1],
                                             in1=rstd[:, 0, :], op0=ALU.mult, op1=ALU.mult)
                done("u2_ready", ins)
            b = take_bank(dve, "logits")
            for n in range(4):
                dve.wait_ge(st_stored[n], 32)
            dve.wait_ge(S["router_loaded"], 32)
            for t, n in enumerate(ROWS):
                ins = V.tensor_tensor(logits[0:n, t, :], b[0:n, E * t:E * t + E], b_router[0:n, :], ALU.add)
            ins.then_inc(emptied["v"], 1)
            dve.wait_ge(emptied["v"], nth["logits"] + 1)
            for t, n in enumerate(ROWS):
                link(V.max(top[0:n, t, :], logits[0:n, t, :]))
                done("gates_in", V.tensor_scalar(gates[0:n, t, :], top[0:n, t, 0:TOPK], top[0:n, t, 0:1], None, ALU.subtract))
                link(V.max_index(top_i[0:n, t, :], top[0:n, t, :], logits[0:n, t, :]))
                link(V.tensor_copy(top_f[0:n, t, :], top_i[0:n, t, :]))
                for k in range(TOPK):
                    ins = V.tensor_scalar(hot[0:n, t, k, :], slot_no[0:n, 0:E], top_f[0:n, t, k:k + 1], None, ALU.is_equal)
                link(ins)
                V.tensor_tensor(mark[0:n, t, :], hot[0:n, t, 0, :], hot[0:n, t, 1, :], ALU.add)
                link(V.tensor_tensor(tmp_e[0:n, t, :], hot[0:n, t, 2, :], hot[0:n, t, 3, :], ALU.add))
                done("mark_ready", V.tensor_tensor(mark[0:n, t, :], mark[0:n, t, :], tmp_e[0:n, t, :], ALU.add))
            dve.wait_ge(S["mark_ready"], 3)
            b = take_bank(dve, "rank")
            for t, n in enumerate(ROWS):
                V.tensor_copy(rank[0:n, t, :], b[0:n, E * t:E * t + E])
            V.tensor_copy(total, b[:, 3 * E:4 * E]).then_inc(emptied["v"], 1)
            dve.wait_ge(emptied["v"], nth["rank"] + 1)
            link(V.tensor_reduce(most, total, AXX, ALU.max))
            link(V.tensor_scalar(passes_f, most, float(SLOTS), 1.0, ALU.is_gt, ALU.add))
            for j in range(2, MAXP):
                link(V.scalar_tensor_tensor(out=passes_f, in0=most, scalar=float(SLOTS * j), in1=passes_f, op0=ALU.is_gt, op1=ALU.add))
            done("passes_ready", V.tensor_copy(passes, passes_f))
            link(V.memset(slot_of[:, :, E:E + 1], -1.0))
            for t, n in enumerate(ROWS):
                r, m = rank[0:n, t, :], mark[0:n, t, :]
                link(V.scalar_tensor_tensor(out=slot_of[0:n, t, 0:E], in0=r, scalar=1.0, in1=m, op0=ALU.add, op1=ALU.mult))
                link(V.tensor_scalar(slot_of[0:n, t, 0:E], slot_of[0:n, t, 0:E], -1.0, None, ALU.add))
            dve.wait_ge(filled, len(uses))
            def pick_tokens(p, e):
                for t, n in enumerate(ROWS):
                    ins = V.tensor_scalar(pick[0:n, t, :], slot_no[0:n, bass.ds(SLOTS * p, SLOTS)],
                                          slot_of[0:n, t, bass.ds(e, 1)], None, ALU.is_equal)
                done("pick_ready", ins)

            def pick_expert(e):
                done("pick_e_ready", V.tensor_copy(pick_e, ident[0:E, bass.ds(e, 1)].to_broadcast([E, SLOTS])))

            pick_tokens(0, 0)
            pick_expert(0)
            done("comb_emptied", V.memset(y_out, 0.0))
            done("comb_emptied", V.memset(pgt, 0.0))
            dve.wait_ge(S["gates_exp"], 1)
            for t, n in enumerate(ROWS):
                link(V.tensor_reduce(ssq[0:n, t:t + 1], gates[0:n, t, :], AXX, ALU.add))
                link(V.reciprocal(ssq[0:n, t:t + 1], ssq[0:n, t:t + 1]))
                link(V.tensor_scalar(gates[0:n, t, :], gates[0:n, t, :], ssq[0:n, t:t + 1], None, ALU.mult))
                link(V.tensor_scalar(gates_e[0:n, t, :], hot[0:n, t, 0, :], gates[0:n, t, 0:1], None, ALU.mult))
                for k in range(1, TOPK):
                    link(V.scalar_tensor_tensor(out=gates_e[0:n, t, :], in0=hot[0:n, t, k, :], scalar=gates[0:n, t, k:k + 1],
                                                in1=gates_e[0:n, t, :], op0=ALU.mult, op1=ALU.add))

            def accumulate(i, c):
                dve.wait_ge(S["comb_filled"], KT * i + c + 1)
                done("comb_emptied", V.tensor_tensor(xT[:, c, :], xT[:, c, :], p_comb[c % 2][:, 0:NT], ALU.add))

            n_passes = dve.value_load(passes[0:1, 0:1], min_val=1, max_val=MAXP)
            with dve.Fori(0, n_passes) as p:
                with dve.Fori(0, E) as e:
                    i = E * p + e
                    dve.wait_ge(S["xg_filled"], (E + 1) * p + e + 1)
                    pick_tokens(p, e + 1)
                    dve.wait_ge(S["pg_filled"], i)
                    for t, n in enumerate(ROWS):
                        ins = V.tensor_scalar(pg[0:n, t, :].rearrange("p (w s) -> p w s", w=2),
                                              slot_no[0:n, bass.ds(SLOTS * p, SLOTS)].unsqueeze(1).to_broadcast([n, 2, SLOTS]),
                                              slot_of[0:n, t, bass.ds(e, 1)], gates_e[0:n, t, bass.ds(e, 1)], ALU.is_equal, ALU.mult)
                    done("pg_ready", ins)
                    for c in range(KT):
                        accumulate(i, c)
                    dve.wait_ge(S["w_used"], NSLOT * i + KT)
                    V.tensor_scalar(g1, p_gu[0][:, :], 7.0, None, ALU.min).then_inc(S["g1_ready"], 1)
                    V.tensor_scalar(u1, p_gu[1][:, :], 7.0, -7.0, ALU.min, ALU.max).then_inc(S["gu_emptied"], 1)
                    dve.wait_ge(S["gu_emptied"], i + 1)
                    V.scalar_tensor_tensor(out=u1, in0=u1, scalar=1.0, in1=g1, op0=ALU.add, op1=ALU.mult).then_inc(S["ug_ready"], 1)
                    dve.wait_ge(S["ug_ready"], i + 1)
                    dve.wait_ge(S["sg_ready"], i + 1)
                    V.tensor_tensor(ha, u1, sg, ALU.mult).then_inc(S["ha_ready"], 1)
                    dve.wait_ge(S["ht_filled"], i + 1)
                    pick_expert(e + 1)
                dve.wait_ge(S["xg_filled"], (E + 1) * (p + 1))
                pick_tokens(p + 1, 0)
                dve.wait_ge(S["w_used"], NSLOT * E * (p + 1))
                dve.wait_ge(S["pick_e_ready"], (E + 1) * (p + 1))
                pick_expert(0)
            for c in range(KT):
                accumulate(E * n_passes, c)
            for t, n in enumerate(ROWS):
                dve.wait_ge(S["sq_sum"], 2 * t + 2)
                link(V.tensor_tensor(ssq[0:n, t:t + 1], ssq_h[0:n, t, 0:1], ssq_h[0:n, t, 1:2], ALU.add))
                done("rms_in", V.tensor_scalar(ssq[0:n, t:t + 1], ssq[0:n, t:t + 1], 1.0 / D, EPS, ALU.mult, ALU.add))
            dve.wait_ge(S["final_loaded"], 16)
            for t, n in enumerate(ROWS):
                dve.wait_ge(S["fin_rms"], t + 1)
                link(V.reciprocal(ssq[0:n, t:t + 1], ssq[0:n, t:t + 1]))
                for h in range(2):
                    w = slice(512 * h, 512 * h + 512)
                    done("out_ready", V.scalar_tensor_tensor(out=rows_out[0:n, t, w], in0=p_rows[t][h][0:n, :], scalar=ssq[0:n, t:t + 1],
                                                             in1=n_final[0:n, w], op0=ALU.mult, op1=ALU.mult))


_INS = ['x_prompt', 'x_sample', 'state_lru_conv', 'state_lru_h', 'state_ssd_conv', 'state_ssd', 'norm_mix', 'w_in',
        'conv_lru_w', 'conv_lru_b', 'w_rg', 'b_rg', 'w_ig', 'b_ig', 'lam', 'w_proj_a', 'conv_ssd_w', 'conv_ssd_b',
        'dt_bias', 'a_log', 'd_skip', 'ssd_norm', 'w_proj_b', 'w_out', 'norm_ffn', 'w_router', 'b_router',
        'w_gate_up', 'b_gate_up', 'w_down', 'b_down', 'norm_final']
_CONV = 3072
_OUTS = [(1, TP, D), (TS, 1, D), (1, 1, HIST, D), (1, 1, D), (1, 1, HIST, _CONV), (1, 1, HEADS, HD, NS),
         (1, TS, HIST, D), (1, TS, D), (1, TS, HIST, _CONV), (1, TS, HEADS, HD, NS)]


def kernel(**inputs):
    import numpy as _np
    import concourse.bacc as _bacc
    from concourse import mybir as _mybir
    from concourse.bass_utils import run_bass_kernel_spmd as _run

    nc = _bacc.Bacc("TRN2", target_bir_lowering=False, num_devices=1)
    arrays, args = {}, {}
    for name in _INS:
        x = _np.ascontiguousarray(inputs[name])
        arrays[f"in_{name}"] = x
        args[name] = nc.dram_tensor(f"in_{name}", x.shape, _mybir.dt.from_np(x.dtype), kind="ExternalInput").ap()
    for i, shape in enumerate(_OUTS):
        args[f"out_{i}"] = nc.dram_tensor(f"out_{i}", shape, _mybir.dt.float32, kind="ExternalOutput").ap()
    build(nc, args)
    r = _run(nc, [arrays], core_ids=[0])
    return tuple(r.results[0][f"out_{i}"] for i in range(len(_OUTS)))
```
